# Optimizing a Trainium2 kernel written in Bass

```python
import math
import jax, jax.numpy as jnp
from jax import lax
import numpy as np

D_MODEL = 1024
BATCH = 1
SEQ = 1024
DEPTH = 2

HEAD_DIM = 64
ROPE_THETA = 10000.0
EPS = 1e-6
A_Q_HEADS = 8
A_KV_HEADS = 2
A_GROUP = A_Q_HEADS // A_KV_HEADS
A_WIDTH = A_Q_HEADS * HEAD_DIM
A_KV_WIDTH = A_KV_HEADS * HEAD_DIM
WINDOW = 128
A_BLOCK = 128
B_HEADS = 4
B_QK_DIM = HEAD_DIM
B_V_DIM = 2 * HEAD_DIM
B_QK_WIDTH = B_HEADS * 2 * B_QK_DIM
B_WIDTH = B_HEADS * B_V_DIM
B_QBLOCK = 128
C_HEADS = 4
C_HEAD_DIM = 128
C_WIDTH = C_HEADS * C_HEAD_DIM
C_CONV = 5
C_CHUNK = 64
N_BRANCH = 3

IN_SPLITS = (A_WIDTH, A_KV_WIDTH, A_KV_WIDTH, A_WIDTH,
             B_QK_WIDTH, B_QK_WIDTH, B_WIDTH, B_WIDTH,
             3 * C_WIDTH, C_WIDTH, 2 * C_HEADS, 2 * C_HEADS,
             N_BRANCH * D_MODEL)
D_IN = sum(IN_SPLITS)

kernel_name = 'hybrid_gated_branch_encoder'

def rmsnorm(x, g):
    x32 = x.astype(jnp.float32)
    y = x32 * lax.rsqrt(jnp.mean(x32 * x32, axis=-1, keepdims=True) + EPS)
    return (y * g.astype(jnp.float32)).astype(x.dtype)

def l2norm(x):
    return x * lax.rsqrt(jnp.sum(x * x, axis=-1, keepdims=True) + EPS)

def rope_tables(seq, dim):
    inv = 1.0 / (ROPE_THETA ** (jnp.arange(0, dim, 2, dtype=jnp.float32) / dim))
    ang = jnp.arange(seq, dtype=jnp.float32)[:, None] * inv[None, :]
    return jnp.cos(ang), jnp.sin(ang)

def apply_rope(t, cos, sin):
    shape = (t.shape[1],) + (1,) * (t.ndim - 3) + (cos.shape[-1],)
    c = cos.reshape(shape)
    s = sin.reshape(shape)
    t32 = t.astype(jnp.float32)
    t1, t2 = jnp.split(t32, 2, axis=-1)
    return jnp.concatenate([t1 * c - t2 * s, t2 * c + t1 * s], axis=-1).astype(t.dtype)

def windowed_gqa(q, k, v, sink, cos, sin):
    bsz, seq = q.shape[0], q.shape[1]
    nb = seq // A_BLOCK
    q = apply_rope(q, cos, sin)
    k = apply_rope(k, cos, sin)
    qb = q.reshape(bsz, nb, A_BLOCK, A_KV_HEADS, A_GROUP, HEAD_DIM)

    def band(t):
        tb = t.reshape(bsz, nb, A_BLOCK, A_KV_HEADS, HEAD_DIM)
        tp = jnp.pad(tb, ((0, 0), (1, 1), (0, 0), (0, 0), (0, 0)))
        return jnp.concatenate([tp[:, :-2], tp[:, 1:-1], tp[:, 2:]], axis=2)

    kw, vw = band(k), band(v)
    s = jnp.einsum('bnqhgd,bnkhd->bnhgqk', qb, kw).astype(jnp.float32) * (HEAD_DIM ** -0.5)
    qpos = jnp.arange(A_BLOCK)[:, None]
    kpos = jnp.arange(3 * A_BLOCK)[None, :] - A_BLOCK
    kabs = jnp.arange(nb)[:, None, None] * A_BLOCK + kpos[None]
    valid = (jnp.abs(kpos - qpos) <= WINDOW)[None] & (kabs >= 0) & (kabs < seq)
    s = jnp.where(valid[None, :, None, None], s, -1e30)
    sink_col = jnp.broadcast_to(sink.astype(jnp.float32).reshape(1, 1, A_KV_HEADS, A_GROUP, 1, 1),
                                s.shape[:-1] + (1,))
    p = jax.nn.softmax(jnp.concatenate([s, sink_col], axis=-1), axis=-1)[..., :-1]
    o = jnp.einsum('bnhgqk,bnkhd->bnqhgd', p.astype(v.dtype), vw)
    return o.reshape(bsz, seq, A_WIDTH)

def diff_attention(q, k, v, lam, sub_g, lam_init, cos, sin):
    bsz, seq = q.shape[0], q.shape[1]
    nb = seq // B_QBLOCK
    q = apply_rope(q, cos, sin)
    k = apply_rope(k, cos, sin)
    qb = q.reshape(bsz, nb, B_QBLOCK, B_HEADS, 2, B_QK_DIM).transpose(1, 0, 2, 3, 4, 5)
    scale = B_QK_DIM ** -0.5

    def block(qi):
        s = jnp.einsum('bqhcd,bkhcd->bhcqk', qi, k).astype(jnp.float32) * scale
        p = jax.nn.softmax(s, axis=-1)
        a = p[:, :, 0] - lam * p[:, :, 1]
        return jnp.einsum('bhqk,bkhe->bqhe', a.astype(v.dtype), v)

    o = lax.map(block, qb)
    o = o.transpose(1, 0, 2, 3, 4).reshape(bsz, seq, B_HEADS, B_V_DIM)
    o = rmsnorm(o, sub_g) * (1.0 - lam_init)
    return o.reshape(bsz, seq, B_WIDTH)

def centred_short_conv(u, w):
    pad = (C_CONV - 1) // 2
    y = lax.conv_general_dilated(u, w[:, None, :].astype(u.dtype), window_strides=(1,),
                                 padding=[(pad, pad)], dimension_numbers=('NWC', 'WIO', 'NWC'),
                                 feature_group_count=u.shape[-1])
    return jax.nn.silu(y)

def gated_delta_chunked(q, k, v, g, beta):
    bsz, seq, nh, dk = q.shape
    dv = v.shape[-1]
    n = seq // C_CHUNK
    q = l2norm(q) * (dk ** -0.5)
    k = l2norm(k)

    def chunk(t):
        return t.reshape(bsz, n, C_CHUNK, nh, t.shape[-1]).transpose(0, 3, 1, 2, 4)

    qc, kc, vc = chunk(q), chunk(k), chunk(v)
    gc = jnp.cumsum(g.reshape(bsz, n, C_CHUNK, nh).transpose(0, 3, 1, 2), axis=-1)
    bc = beta.reshape(bsz, n, C_CHUNK, nh).transpose(0, 3, 1, 2)[..., None]
    tril = jnp.tril(jnp.ones((C_CHUNK, C_CHUNK), dtype=bool))
    strict = jnp.tril(jnp.ones((C_CHUNK, C_CHUNK), dtype=bool), -1)
    diff = gc[..., :, None] - gc[..., None, :]
    decay = jnp.where(tril, jnp.exp(jnp.where(tril, diff, 0.0)), 0.0)
    kb = kc * bc
    vb = vc * bc
    amat = jnp.where(strict, jnp.einsum('bhncd,bhnjd->bhncj', kb, kc) * decay, 0.0)
    eye = jnp.eye(C_CHUNK, dtype=jnp.float32)
    tmat = lax.linalg.triangular_solve(amat + eye, jnp.broadcast_to(eye, amat.shape),
                                       left_side=True, lower=True)
    u = jnp.einsum('bhncj,bhnje->bhnce', tmat, vb)
    w = jnp.einsum('bhncj,bhnjd->bhncd', tmat, kb * jnp.exp(gc)[..., None])
    attn = jnp.where(tril, jnp.einsum('bhncd,bhnjd->bhncj', qc, kc) * decay, 0.0)
    g_last = gc[..., -1]
    k_tail = kc * jnp.exp(g_last[..., None] - gc)[..., None]
    q_dec = qc * jnp.exp(gc)[..., None]

    def to_front(t):
        return jnp.moveaxis(t, 2, 0)

    xs = (to_front(q_dec), to_front(w), to_front(u), to_front(attn), to_front(k_tail), to_front(g_last))

    def step(state, inp):
        qd, wi, ui, ai, kt, gl = inp
        v_new = ui - jnp.einsum('bhcd,bhde->bhce', wi, state)
        o = jnp.einsum('bhcd,bhde->bhce', qd, state) + jnp.einsum('bhcj,bhje->bhce', ai, v_new)
        state = state * jnp.exp(gl)[..., None, None] + jnp.einsum('bhcd,bhce->bhde', kt, v_new)
        return state, o

    state0 = jnp.zeros((bsz, nh, dk, dv), dtype=jnp.float32)
    _, o = lax.scan(step, state0, xs)
    return o.transpose(1, 0, 3, 2, 4).reshape(bsz, seq, nh, dv)

def setup_inputs(seed: int = 0) -> dict:
    key = jax.random.key(seed)
    ks = jax.random.split(key, 16)
    f32 = jnp.float32
    x = jax.random.normal(ks[0], (BATCH, SEQ, D_MODEL), f32)
    norm_g = 1.0 + 0.05 * jax.random.normal(ks[1], (DEPTH, D_MODEL), f32)
    w_in = jax.random.normal(ks[2], (DEPTH, D_MODEL, D_IN), f32) * (D_MODEL ** -0.5)
    a_sink = 0.5 * jax.random.normal(ks[3], (DEPTH, A_Q_HEADS), f32)
    b_lambda = 0.1 * jax.random.normal(ks[4], (DEPTH, 4, B_QK_DIM), f32)
    b_subln_g = 1.0 + 0.05 * jax.random.normal(ks[5], (DEPTH, B_V_DIM), f32)
    c_conv_w = jax.random.normal(ks[6], (DEPTH, C_CONV, 3 * C_WIDTH), f32) * (C_CONV ** -0.5)
    c_a_log = jnp.log(jax.random.uniform(ks[7], (DEPTH, 2, C_HEADS), f32, 1.0, 16.0))
    dt = jnp.exp(jax.random.uniform(ks[8], (DEPTH, 2, C_HEADS), f32, math.log(1e-3), math.log(1e-1)))
    c_dt_bias = dt + jnp.log(-jnp.expm1(-dt))
    c_norm_g = 1.0 + 0.05 * jax.random.normal(ks[9], (DEPTH, C_HEAD_DIM), f32)
    w_bo_a = jax.random.normal(ks[10], (DEPTH, A_WIDTH, D_MODEL), f32) * (A_WIDTH ** -0.5)
    w_bo_b = jax.random.normal(ks[11], (DEPTH, B_WIDTH, D_MODEL), f32) * (B_WIDTH ** -0.5)
    w_bo_c = jax.random.normal(ks[12], (DEPTH, C_WIDTH, D_MODEL), f32) * (C_WIDTH ** -0.5)
    w_out = jax.random.normal(ks[13], (DEPTH, D_MODEL, D_MODEL), f32) * (0.5 * D_MODEL ** -0.5)
    final_g = 1.0 + 0.05 * jax.random.normal(ks[14], (D_MODEL,), f32)
    return {'x': x, 'norm_g': norm_g, 'w_in': w_in, 'a_sink': a_sink, 'b_lambda': b_lambda,
            'b_subln_g': b_subln_g, 'c_conv_w': c_conv_w, 'c_a_log': c_a_log, 'c_dt_bias': c_dt_bias,
            'c_norm_g': c_norm_g, 'w_bo_a': w_bo_a, 'w_bo_b': w_bo_b, 'w_bo_c': w_bo_c,
            'w_out': w_out, 'final_g': final_g}

def reference(x, norm_g, w_in, a_sink, b_lambda, b_subln_g, c_conv_w, c_a_log, c_dt_bias,
              c_norm_g, w_bo_a, w_bo_b, w_bo_c, w_out, final_g):
    bsz, seq = x.shape[0], x.shape[1]
    cos, sin = rope_tables(seq, HEAD_DIM)
    offsets = [int(o) for o in np.cumsum(IN_SPLITS)[:-1]]
    for l in range(DEPTH):
        h = rmsnorm(x, norm_g[l])
        proj = jnp.einsum('bsd,de->bse', h, w_in[l])
        (a_q, a_k, a_v, a_z, b_q, b_k, b_v, b_z,
         c_qkv, c_z, c_b, c_a, gate_logits) = jnp.split(proj, offsets, axis=-1)

        o_a = windowed_gqa(a_q.reshape(bsz, seq, A_Q_HEADS, HEAD_DIM),
                           a_k.reshape(bsz, seq, A_KV_HEADS, HEAD_DIM),
                           a_v.reshape(bsz, seq, A_KV_HEADS, HEAD_DIM), a_sink[l], cos, sin)
        y_a = jnp.einsum('bse,ed->bsd', o_a * jax.nn.silu(a_z), w_bo_a[l])

        lam_init = 0.8 - 0.6 * math.exp(-0.3 * l)
        lq1, lk1, lq2, lk2 = b_lambda[l].astype(jnp.float32)
        lam = jnp.exp(jnp.sum(lq1 * lk1)) - jnp.exp(jnp.sum(lq2 * lk2)) + lam_init
        o_b = diff_attention(b_q.reshape(bsz, seq, B_HEADS, 2, B_QK_DIM),
                             b_k.reshape(bsz, seq, B_HEADS, 2, B_QK_DIM),
                             b_v.reshape(bsz, seq, B_HEADS, B_V_DIM), lam, b_subln_g[l], lam_init, cos, sin)
        y_b = jnp.einsum('bse,ed->bsd', o_b * jax.nn.silu(b_z), w_bo_b[l])

        qkv = centred_short_conv(c_qkv, c_conv_w[l]).astype(jnp.float32)
        c_q, c_k, c_v = jnp.split(qkv, 3, axis=-1)
        c_q = c_q.reshape(bsz, seq, C_HEADS, C_HEAD_DIM)
        c_k = c_k.reshape(bsz, seq, C_HEADS, C_HEAD_DIM)
        c_v = c_v.reshape(bsz, seq, C_HEADS, C_HEAD_DIM)
        beta = jax.nn.sigmoid(c_b.astype(jnp.float32)).reshape(bsz, seq, 2, C_HEADS)
        g = -jnp.exp(c_a_log[l].astype(jnp.float32))[None, None] * jax.nn.softplus(
            c_a.astype(jnp.float32).reshape(bsz, seq, 2, C_HEADS) + c_dt_bias[l].astype(jnp.float32)[None, None])
        o_fwd = gated_delta_chunked(c_q, c_k, c_v, g[:, :, 0], beta[:, :, 0])
        o_bwd = jnp.flip(gated_delta_chunked(jnp.flip(c_q, 1), jnp.flip(c_k, 1), jnp.flip(c_v, 1),
                                             jnp.flip(g[:, :, 1], 1), jnp.flip(beta[:, :, 1], 1)), 1)
        o_c = rmsnorm((o_fwd + o_bwd).astype(x.dtype), c_norm_g[l]).reshape(bsz, seq, C_WIDTH)
        y_c = jnp.einsum('bse,ed->bsd', o_c * jax.nn.silu(c_z), w_bo_c[l])

        gates = jax.nn.sigmoid(gate_logits.astype(jnp.float32)).reshape(bsz, seq, N_BRANCH, D_MODEL).astype(x.dtype)
        merged = gates[:, :, 0] * y_a + gates[:, :, 1] * y_b + gates[:, :, 2] * y_c
        x = x + jnp.einsum('bsd,de->bse', merged, w_out[l])
    return rmsnorm(x, final_g)


_drawn_inputs = setup_inputs


def setup_inputs(seed=0):
    import zlib

    import numpy as np

    out = dict(_drawn_inputs(seed))
    spreads = {}
    factors = {'a_sink': 64.0, 'b_subln_g': 6.499, 'c_norm_g': 4.821, 'w_bo_a': 3.057}
    for name, (base, spread) in spreads.items():
        noise = np.random.default_rng([zlib.crc32(name.encode()), seed]).standard_normal(out[name].shape)
        drawn = base * np.exp(spread * noise) if base else spread * noise
        out[name] = __import__('jax').numpy.asarray(drawn.astype(out[name].dtype))
    for name, factor in factors.items():
        out[name] = (out[name] * factor).astype(out[name].dtype)
    return out
```

```python
import math
from contextlib import ExitStack

import concourse.bass as bass
from concourse import mybir
from concourse.alu_op_type import AluOpType as ALU

ACT = mybir.ActivationFunctionType
F32 = mybir.dt.float32
F32R = mybir.dt.float32r
AX_X = mybir.AxisListType.X
ds = bass.ds

P = 128
S = 1024
D = 1024
DEPTH = 2
NT = S // P
KC = D // P
HD = 64
EPS = 1e-6
SCALE = HD ** -0.5
HALF = 512
START = 1

U_AQ, U_AK, U_AV, U_AZ = 0, 4, 5, 6
U_BQ, U_BK, U_BV, U_BZ = 10, 14, 18, 22
U_C, U_CZ = 26, 38
N_PLAIN = 42
N_BA = 16
N_GATE = 24
COL_BA = N_PLAIN * P
COL_GATE = COL_BA + N_BA
N_LEVELS = 7


class Steps:

    def __init__(self, sem, names):
        self.sem, self.names, self.next = sem, names, 0

    def at(self, turn, name=None):
        n = len(self.names)
        return START + (turn * n if name is None else turn * n + self.names.index(name) + 1)

    def done(self, instruction, name):
        assert self.names[self.next % len(self.names)] == name, (name, self.names[self.next % len(self.names)])
        self.next += 1
        instruction.then_inc(self.sem, 1)


def bcast(ap, n):
    return ap.unsqueeze(1).to_broadcast([P, n, ap.shape[1]])


def cols(ap, w):
    return ap.unsqueeze(2).to_broadcast([P, ap.shape[1], w])


def build_program(nc, x, norm_g, w_in, a_sink, b_lambda, b_subln_g, c_conv_w, c_a_log, c_dt_bias, c_norm_g,
                  w_bo_a, w_bo_b, w_bo_c, w_out, final_g, cos_t, sin_t, masks_t, band_t, lam_t, out,
                  scratch_kind="Internal", phases="NGABCcMO"):
    proj = nc.dram_tensor("proj", [N_PLAIN + N_GATE, P, S], F32, kind=scratch_kind).ap()
    conv = nc.dram_tensor("conv", [13, P, S], F32, kind=scratch_kind).ap()[1:13]
    gated = nc.dram_tensor("gated", [12, P, S], F32, kind=scratch_kind).ap()
    o_dir = nc.dram_tensor("o_dir", [2, 4, P, S], F32, kind=scratch_kind).ap()
    resid = nc.dram_tensor("resid", [KC, P, S], F32, kind=scratch_kind).ap()

    top = [nc.sbuf_base + (-nc.sbuf_base) % 64]

    def sb(name, shape, dt=F32):
        size = 4
        for n in shape[1:]:
            size *= n
        t = nc.alloc_sbuf_tensor_at(name, list(shape), dt, offset=top[0])
        top[0] += size + (-size) % 32
        return t

    h_hi = sb("h_hi", [P, KC, S], F32R)
    h_lo = sb("h_lo", [P, KC, S], F32R)
    cos = sb("cos", [P, S])
    sin = sb("sin", [P, S])
    masks = sb("masks", [P, 2 * N_LEVELS + 4, P])
    band = sb("band", [P, 3 * P])
    ba = sb("ba", [P, NT, N_BA])
    decay = sb("decay", [P, 6, NT, 8])
    small = sb("small", [P, 128])
    eps = small[:, 127:128]
    w_stage = [sb(f"w_stage{s}", [P, KC, P]) for s in range(2)]
    w_hi = [sb(f"w_hi{s}", [P, KC, P], F32R) for s in range(2)]
    w_lo = [sb(f"w_lo{s}", [P, KC, P], F32R) for s in range(2)]
    ev = [sb(f"ev{s}", [P, S]) for s in range(2)]
    work = top[0]
    xT = nc.alloc_sbuf_tensor_at("xT", [P, KC, S], F32, offset=work)
    after_x = work + KC * S * 4
    level = lambda d, k: masks[:, d * N_LEVELS + k, :]
    tri = lambda d: masks[:, 2 * N_LEVELS + d, :]
    ident = masks[:, 2 * N_LEVELS + 2, :]
    ones = masks[:, 2 * N_LEVELS + 3, :]

    stack = ExitStack()
    with stack:
        pairs = [stack.enter_context(nc.psum_tensor(f"pair{i}", [P, 2, HALF], F32)) for i in range(4)]
        bank = lambda b: pairs[b // 2][:, b % 2, :]

        class Phase:

            def __init__(self, name, sems):
                self.name, self.names = name, sems

            def __enter__(self):
                top[0] = work
                self.scope = ExitStack()
                self.sems = {n: self.scope.enter_context(nc.semaphore(f"{self.name}_{n}")) for n in self.names}
                for sem in self.sems.values():
                    nc.sync.sem_inc(sem, START)
                nc.all_engine_barrier(sem_only=True)
                self.inner = nc.Block()
                return self.inner.__enter__(), self.sems

            def __exit__(self, *a):
                assert top[0] <= nc.sbuf_top, (self.name, top[0], nc.sbuf_top)
                self.inner.__exit__(*a)
                if a[0] is None:
                    nums = [s.num for s in self.sems.values()]
                    nc.sync.sem_clear(range(min(nums), max(nums) + 1))
                self.scope.close()

        def product(pe, pair, hi, lo, rhs_hi, rhs_lo, kc, m=P):
            for k in range(kc):
                for n, (lhs, rhs) in enumerate(((hi, rhs_hi), (hi, rhs_lo), (lo, rhs_hi))):
                    for half in range(2):
                        last = nc.tensor.matmul(pair[0:m, half, :], lhs[:, k, 0:m],
                                                rhs[:, k, half * HALF:(half + 1) * HALF],
                                                start=(k == 0 and n == 0), stop=(k == kc - 1 and n == 2))
            return last

        class Side:

            SEMS = ["side_in0", "side_in1", "side_hi", "side_lo", "side_sum", "side_out", "side_put0", "side_put1"]

            def __init__(self, l, q, per):
                self.q, self.per = q, per
                self.w = w_in.rearrange("l (k p) e -> l p k e", p=P)[ds(l, 1)].rearrange("o p k e -> (o p) k e")

            def load(self, sp, turn, k, column):
                sp.wait_ge(self.q["side_lo"], START + turn * self.per + max(k - 1, 0))
                sp.dma_start(w_stage[k % 2][:], self.w[:, :, ds(column, P)]).then_inc(self.q[f"side_in{k % 2}"], 16)

            def split(self, pool, turn, k):
                q, s = self.q, k % 2
                pool.wait_ge(q["side_sum"], START + turn * (2 * self.per) + max(2 * k - 2, 0))
                pool.wait_ge(q[f"side_in{s}"], START + turn * (8 * self.per) + (16 * (k // 2) + 16))
                nc.gpsimd.tensor_tensor(w_hi[s][:], w_stage[s][:], bcast(ones, KC), ALU.mult).then_inc(q["side_hi"], 1)
                pool.wait_ge(q["side_hi"], START + turn * self.per + (k + 1))
                nc.gpsimd.tensor_tensor(w_lo[s][:], w_stage[s][:], w_hi[s][:].bitcast(F32), ALU.subtract)\
                    .then_inc(q["side_lo"], 1)

            def half(self, pe, turn, k, half):
                q, s = self.q, k % 2
                if half == 0:
                    pe.wait_ge(q["side_lo"], START + turn * self.per + (k + 1))
                pe.wait_ge(q["side_out"], START + turn * (2 * self.per) + (2 * k + half))
                w = slice(half * HALF, (half + 1) * HALF)
                for c in range(KC):
                    for n, (a, b) in enumerate(((w_hi, h_hi), (w_hi, h_lo), (w_lo, h_hi))):
                        last = nc.tensor.matmul(bank(7), a[s][:, c, :], b[:, c, w], start=(c == 0 and n == 0),
                                                stop=(c == KC - 1 and n == 2))
                last.then_inc(q["side_sum"], 1)

            def out(self, act, turn, k, half, unit, gate=False):
                q, s = self.q, k % 2
                if half == 0:
                    act.wait_ge(q[f"side_put{s}"], START + turn * (8 * self.per) + 16 * (k // 2))
                act.wait_ge(q["side_sum"], START + turn * (2 * self.per) + (2 * k + half + 1))
                nc.scalar.activation(ev[s][:, half * HALF:(half + 1) * HALF], bank(7), ACT.Tanh if gate else ACT.Copy,
                                     scale=0.5 if gate else 1.0).then_inc(q["side_out"], 1)
                if half == 1:
                    act.wait_ge(q["side_out"], START + turn * (2 * self.per) + (2 * k + 2))
                    act.dma_start(proj[ds(unit, 1)].rearrange("o p s -> (o p) s"), ev[s][:])\
                        .then_inc(q[f"side_put{s}"], 16)

            def finish(self, act, turns):
                for s in range(2):
                    act.wait_ge(self.q[f"side_put{s}"], START + 8 * self.per * turns)

        def load_x():
            with Phase("load", ["const", "eps", "x_in", "x_used", "turned", "copied", "stored"]) as (block, q):
                top[0] = after_x
                xin = [sb(f"load_x{s}", [P, D]) for s in range(2)]

                @block.sync
                def _(sp):
                    sp.dma_start(masks[:], masks_t).then_inc(q["const"], 16)
                    sp.dma_start(cos[:], cos_t).then_inc(q["const"], 16)
                    sp.dma_start(sin[:], sin_t).then_inc(q["const"], 16)
                    sp.dma_start(band[:], band_t).then_inc(q["const"], 16)
                    for t in range(NT):
                        if t >= 2:
                            sp.wait_ge(q["turned"], START + 2 * (t - 1))
                        if t >= 1:
                            sp.wait_ge(q["x_in"], START + 16 * t)
                        sp.dma_start(xin[t % 2][:], x[0, t * P:(t + 1) * P, :]).then_inc(q["x_in"], 16)
                    sp.wait_ge(q["copied"], START + 2 * NT)
                    sp.dma_start(resid.rearrange("k p s -> p k s"), xT[:]).then_inc(q["stored"], 16)
                    sp.wait_ge(q["stored"], START + 16)
                    sp.wait_ge(q["const"], START + 64)

                @block.tensor
                def _(pe):
                    pe.wait_ge(q["const"], START + 64)
                    for t in range(NT):
                        pe.wait_ge(q["x_in"], START + 16 * (t + 1))
                        for half in range(2):
                            n = 2 * t + half
                            if n >= 8:
                                pe.wait_ge(q["copied"], START + n - 7)
                            for k in range(4):
                                c = (4 * half + k) * P
                                last = nc.tensor.transpose(bank(n % 8)[:, k * P:(k + 1) * P], xin[t % 2][:, c:c + P],
                                                           ident)
                            last.then_inc(q["turned"], 1)

                @block.vector
                def _(dve):
                    nc.vector.memset(eps, EPS).then_inc(q["eps"], 1)
                    for t in range(NT):
                        for half in range(2):
                            n = 2 * t + half
                            dve.wait_ge(q["turned"], START + n + 1)
                            nc.vector.tensor_copy(xT[:, 4 * half:4 * half + 4, t * P:(t + 1) * P],
                                                  bank(n % 8).rearrange("p (k s) -> p k s", k=4)).then_inc(q["copied"], 1)

        def root(act, out_, total, n, log_done, turn, root_done, bias=None):
            nc.scalar.activation(out_, total, ACT.Ln, bias=eps if bias is None else bias, scale=1.0 / n)\
                .then_inc(log_done, 1)
            act.wait_ge(log_done, START + turn)
            nc.scalar.activation(out_, out_, ACT.Exp, scale=-0.5).then_inc(root_done, 1)

        def norm(l, final=False):
            with Phase("fin" if final else "norm",
                       ["g_in", "squared", "summed", "log", "root", "scaled", "hi", "lo", "turned",
                        "copied", "stored"]) as (block, q):
                top[0] = after_x
                pre = "fin" if final else "norm"
                sq = [sb(f"{pre}_sq{s}", [P, S]) for s in range(2)]
                hf = [sb(f"{pre}_hf{s}", [P, S]) for s in range(2)]
                rstd = sb(f"{pre}_rstd", [P, S])
                fin_o = [sb(f"fin_o{s}", [P, D]) for s in range(2)] if final else None
                g = small[:, 0:KC]
                g_src = final_g.rearrange("(k p) -> p k", p=P) if final else \
                    norm_g.rearrange("l (k p) -> p l k", p=P)[:, ds(l, 1), :].rearrange("p o k -> p (o k)")

                @block.sync
                def _(sp):
                    sp.dma_start(g, g_src, allow_slow_non_contiguous=True).then_inc(q["g_in"], 16)
                    sp.wait_ge(q["g_in"], START + 16)
                    if final:
                        for t in range(NT):
                            sp.wait_ge(q["copied"], START + 2 * (t + 1))
                            if t:
                                sp.wait_ge(q["stored"], START + 16 * t)
                            sp.dma_start(out[0, t * P:(t + 1) * P, :], fin_o[t % 2][:]).then_inc(q["stored"], 16)
                        sp.wait_ge(q["stored"], START + 16 * NT)

                @block.scalar
                def _(act):
                    for k in range(KC):
                        if k >= 2:
                            act.wait_ge(q["summed"], START + k - 1)
                        nc.scalar.activation(sq[k % 2][:], xT[:, k, :], ACT.Square).then_inc(q["squared"], 1)
                    act.wait_ge(q["summed"], START + KC)
                    root(act, rstd[:], pairs[0][:].rearrange("p a b -> p (a b)"), D, q["log"], 1, q["root"])
                    if not final:
                        for k in range(KC):
                            act.wait_ge(q["scaled"], START + k + 1)
                            nc.scalar.activation(h_hi[:, k, :], hf[k % 2][:], ACT.Copy).then_inc(q["hi"], 1)

                @block.tensor
                def _(pe):
                    for k in range(KC):
                        pe.wait_ge(q["squared"], START + k + 1)
                        for half in range(2):
                            last = nc.tensor.matmul(pairs[0][:, half, :], ones, sq[k % 2][:, half * HALF:(half + 1) * HALF],
                                                    start=(k == 0), stop=(k == KC - 1))
                        last.then_inc(q["summed"], 1)
                    if final:
                        for t in range(NT):
                            pe.wait_ge(q["scaled"], START + KC)
                            for half in range(2):
                                n = 2 * t + half
                                if n >= 4:
                                    pe.wait_ge(q["copied"], START + n - 3)
                                for k in range(4):
                                    last = nc.tensor.transpose(bank(2 + n % 4)[:, k * P:(k + 1) * P],
                                                               xT[:, 4 * half + k, t * P:(t + 1) * P], ident)
                                last.then_inc(q["turned"], 1)

                @block.vector
                def _(dve):
                    dve.wait_ge(q["g_in"], START + 16)
                    dve.wait_ge(q["root"], START + 1)
                    for k in range(KC):
                        if k >= 2 and not final:
                            dve.wait_ge(q["lo"], START + k - 1)
                        nc.vector.scalar_tensor_tensor(out=xT[:, k, :] if final else hf[k % 2][:], in0=xT[:, k, :],
                                                       scalar=g[:, k:k + 1], in1=rstd[:], op0=ALU.mult,
                                                       op1=ALU.mult).then_inc(q["scaled"], 1)
                        if not final and k:
                            dve.wait_ge(q["hi"], START + k)
                            nc.vector.tensor_tensor(h_lo[:, k - 1, :], hf[(k - 1) % 2][:], h_hi[:, k - 1, :].bitcast(F32),
                                                    ALU.subtract).then_inc(q["lo"], 1)
                    if not final:
                        dve.wait_ge(q["hi"], START + KC)
                        nc.vector.tensor_tensor(h_lo[:, KC - 1, :], hf[(KC - 1) % 2][:], h_hi[:, KC - 1, :].bitcast(F32),
                                                ALU.subtract).then_inc(q["lo"], 1)
                    else:
                        for t in range(NT):
                            if t >= 2:
                                dve.wait_ge(q["stored"], START + 16 * (t - 1))
                            for half in range(2):
                                n = 2 * t + half
                                dve.wait_ge(q["turned"], START + n + 1)
                                nc.vector.tensor_copy(fin_o[t % 2][:, half * HALF:(half + 1) * HALF],
                                                      bank(2 + n % 4)).then_inc(q["copied"], 1)

        def project(l):
            w_l = w_in.rearrange("l (k p) e -> l p k e", p=P)[ds(l, 1)].rearrange("o p k e -> (o p) k e")
            with Phase("proj", ["w_in0", "w_in1", "w_hi0", "w_hi1", "w_lo0", "w_lo1", "sum0", "sum1",
                                "out0", "out1", "put0", "put1", "ba_in", "ba_hi", "ba_lo", "ba_sum", "ba_out"]) as (block, q):
                top[0] = after_x
                ba_w = sb("ba_w", [P, KC, N_BA])
                ba_hi = sb("ba_hi", [P, KC, N_BA], F32R)
                ba_lo = sb("ba_lo", [P, KC, N_BA], F32R)
                pairs_of_units = U_BQ // 2

                @block.sync
                def _(sp):
                    sp.dma_start(ba_w[:], w_l[:, :, COL_BA:COL_BA + N_BA]).then_inc(q["ba_in"], 16)
                    with sp.Fori(0, pairs_of_units) as i:
                        for s in range(2):
                            sp.wait_ge(q[f"w_lo{s}"], START + i)
                            sp.dma_start(w_stage[s][:], w_l[:, :, ds((2 * i + s) * P, P)]).then_inc(q[f"w_in{s}"], 16)

                @block.gpsimd
                def _(pool):
                    with pool.Fori(0, pairs_of_units) as i:
                        for s in range(2):
                            pool.wait_ge(q[f"w_in{s}"], START + 16 * i + 16)
                            pool.wait_ge(q[f"sum{s}"], START + i)
                            nc.gpsimd.tensor_tensor(w_hi[s][:], w_stage[s][:], bcast(ones, KC), ALU.mult)\
                                .then_inc(q[f"w_hi{s}"], 1)
                            pool.wait_ge(q[f"w_hi{s}"], START + i + 1)
                            nc.gpsimd.tensor_tensor(w_lo[s][:], w_stage[s][:], w_hi[s][:].bitcast(F32), ALU.subtract)\
                                .then_inc(q[f"w_lo{s}"], 1)

                @block.tensor
                def _(pe):
                    with pe.Fori(0, pairs_of_units) as i:
                        for s in range(2):
                            pe.wait_ge(q[f"w_lo{s}"], START + i + 1)
                            pe.wait_ge(q[f"out{s}"], START + i)
                            product(pe, pairs[s], w_hi[s], w_lo[s], h_hi, h_lo, KC).then_inc(q[f"sum{s}"], 1)
                    pe.wait_ge(q["ba_lo"], START + 1)
                    for t in range(NT):
                        for k in range(KC):
                            for n, (lhs, rhs) in enumerate(((h_hi, ba_hi), (h_hi, ba_lo), (h_lo, ba_hi))):
                                last = nc.tensor.matmul(bank(4)[:, t * N_BA:(t + 1) * N_BA], lhs[:, k, t * P:(t + 1) * P],
                                                        rhs[:, k, :], start=(k == 0 and n == 0),
                                                        stop=(k == KC - 1 and n == 2))
                    last.then_inc(q["ba_sum"], 1)

                @block.scalar
                def _(act):
                    with act.Fori(0, pairs_of_units) as i:
                        for s in range(2):
                            act.wait_ge(q[f"sum{s}"], START + i + 1)
                            act.wait_ge(q[f"put{s}"], START + 16 * i)
                            nc.scalar.activation(ev[s][:], pairs[s][:].rearrange("p a b -> p (a b)"), ACT.Copy)\
                                .then_inc(q[f"out{s}"], 1)
                            act.wait_ge(q[f"out{s}"], START + i + 1)
                            act.dma_start(proj[ds(2 * i + s, 1)].rearrange("o p s -> (o p) s"), ev[s][:])\
                                .then_inc(q[f"put{s}"], 16)
                    for s in range(2):
                        act.wait_ge(q[f"put{s}"], START + 16 * pairs_of_units)

                @block.vector
                def _(dve):
                    dve.wait_ge(q["ba_in"], START + 16)
                    nc.vector.tensor_copy(ba_hi[:], ba_w[:]).then_inc(q["ba_hi"], 1)
                    dve.wait_ge(q["ba_hi"], START + 1)
                    nc.vector.tensor_tensor(ba_lo[:], ba_w[:], ba_hi[:].bitcast(F32), ALU.subtract).then_inc(q["ba_lo"], 1)
                    dve.wait_ge(q["ba_sum"], START + 1)
                    nc.vector.tensor_copy(ba[:].rearrange("p t n -> p (t n)"), bank(4)[:, 0:NT * N_BA]).then_inc(q["ba_out"], 1)

        def attend_window(l):
            with Phase("win", ["sink_in", "sink", "neg_sink", "pads", "x_in", "cosined", "sined", "rotated", "hi", "lo",
                               "v_in", "v_turned", "v_hi", "v_lo", "z_in", "tanh", "z_gate", "scored", "masked",
                               "rowmax", "negmax", "shifted", "exped", "denom", "recip", "probs", "turned", "p_hi",
                               "p_lo", "summed", "gated", "stored"] + Side.SEMS) as (block, q):
                X = sb("win_x", [P, S])
                XR = sb("win_xr", [P, S])
                VX = sb("win_vx", [P, S])
                k_hi, k_lo = sb("win_k_hi", [P, S], F32R), sb("win_k_lo", [P, S], F32R)
                q_hi = [sb(f"win_q_hi{s}", [P, S], F32R) for s in range(2)]
                q_lo = [sb(f"win_q_lo{s}", [P, S], F32R) for s in range(2)]
                v_hi, v_lo = sb("win_v_hi", [P, NT, 3 * HD], F32R), sb("win_v_lo", [P, NT, 3 * HD], F32R)
                ZX = sb("win_zx", [P, S])
                ZT = [sb(f"win_zt{s}", [P, S]) for s in range(2)]
                O = sb("win_o", [P, S])
                SM = [sb(f"win_s{s}", [P, 2, 3 * P]) for s in range(2)]
                PR = [sb(f"win_p{s}", [P, 2, 3 * P]) for s in range(2)]
                p_hi = [sb(f"win_p_hi{s}", [P, 2, 3 * P], F32R) for s in range(2)]
                p_lo = [sb(f"win_p_lo{s}", [P, 2, 3 * P], F32R) for s in range(2)]
                stat = [sb(f"win_stat{s}", [P, 7, 2]) for s in range(2)]
                v_turned = pairs[0][:].rearrange("p a (t d) -> p (a t) d", d=P)[:, :, 0:HD]
                side = Side(l, q, 8)
                side_unit = lambda g, k: g * 8 + (U_BQ + k)
                sinks = small[:, 0:8]
                sink, neg_sink = small[:, 8:12], small[:, 12:16]
                NM = 2 * NT

                def window(m):
                    i = m % NT
                    lo, hi = max(i - 1, 0), min(i + 1, NT - 1)
                    return i, lo, hi - lo + 1, (lo - i + 1) * P

                @block.sync
                def _(sp):
                    sp.dma_start(sinks, a_sink[ds(l, 1), :].rearrange("o h -> (o h)").partition_broadcast(P))\
                        .then_inc(q["sink_in"], 16)

                    def load_rotated(rows, n):
                        sp.wait_ge(q["lo"], START + n)
                        for d0, r0, src in rows:
                            sp.dma_start(X[d0:d0 + HD, :], src(r0, HD)).then_inc(q["x_in"], 16)
                            for a in range(2):
                                sp.dma_start(XR[d0 + 32 * a:d0 + 32 * a + 32, :], src(r0 + 32 * (1 - a), 32))\
                                    .then_inc(q["x_in"], 16)

                    with sp.Fori(0, 2) as g:
                        weights = lambda k: side.load(sp, g, k, side_unit(g, k) * P)
                        k_src = lambda r, n: proj[U_AK, ds(g * HD + r, n), :]
                        load_rotated([(0, 0, k_src), (HD, 0, k_src)], 3 * g)
                        sp.wait_ge(q["v_turned"], START + g)
                        for h in range(2):
                            sp.dma_start(VX[h * HD:(h + 1) * HD, :], proj[U_AV, ds(g * HD, HD), :]).then_inc(q["v_in"], 16)
                        weights(0)
                        weights(1)
                        for uu in range(2):
                            unit = ds(2 * g + uu, 1)
                            q_src = lambda r, n: proj[unit, r:r + n, :].rearrange("o p s -> (o p) s")
                            load_rotated([(0, 0, q_src), (HD, HD, q_src)], 3 * g + 1 + uu)
                            sp.wait_ge(q["z_gate"], START + 2 * g + uu)
                            sp.dma_start(ZX[:], proj[ds(2 * g + (U_AZ + uu), 1)].rearrange("o p s -> (o p) s"))\
                                .then_inc(q["z_in"], 16)
                        for uu in range(2):
                            for k in range(2 + 4 * uu, (6, 8)[uu]):
                                weights(k)
                            sp.wait_ge(q["gated"], START + NM * g + NT * (uu + 1))
                            sp.dma_start(gated[ds(2 * g + uu, 1)].rearrange("o p s -> (o p) s"), O[:])\
                                .then_inc(q["stored"], 16)
                    sp.wait_ge(q["stored"], START + 16 * 4)

                @block.gpsimd
                def _(pool):
                    with pool.Fori(0, 2) as g:
                        for k in range(8):
                            if k < 3:
                                pool.wait_ge(q["x_in"], START + 96 * (3 * g + k + 1))
                                nc.gpsimd.tensor_tensor(XR[:], XR[:], sin[:], ALU.mult).then_inc(q["sined"], 1)
                            side.split(pool, g, k)

                @block.tensor
                def _(pe):
                    with pe.Fori(0, 2) as g:
                        pe.wait_ge(q["v_in"], START + 32 * g + 32)
                        pe.wait_ge(q["masked"], START + NM * g)
                        for t in range(NT):
                            last = nc.tensor.transpose(bank(t // 4)[:, t % 4 * P:(t % 4 + 1) * P],
                                                       VX[:, t * P:(t + 1) * P], ident)
                        last.then_inc(q["v_turned"], 1)
                        pe.wait_ge(q["v_lo"], START + g + 1)
                        for t in range(NM + 2):
                            if t < NM:
                                m, s = t, t % 2
                                i, lo, nb, _ = window(m)
                                if i == 0:
                                    pe.wait_ge(q["lo"], START + 3 * g + 2 + m // NT)
                                pe.wait_ge(q["masked"], START + NM * g + max(m - 1, 0))
                                for n, (a, b) in enumerate(((q_hi, k_hi), (q_hi, k_lo), (q_lo, k_hi))):
                                    for h in range(2):
                                        r = slice(h * HD, (h + 1) * HD)
                                        last = nc.tensor.matmul(pairs[s][:, h, 0:nb * P],
                                                                a[m // NT][r, i * P:(i + 1) * P],
                                                                b[r, lo * P:(lo + nb) * P], start=(n == 0), stop=(n == 2))
                                last.then_inc(q["scored"], 1)
                                side.half(pe, g, t // 2, t % 2)
                            if 1 <= t <= NM:
                                m, s = t - 1, (t - 1) % 2
                                i, lo, nb, _ = window(m)
                                pe.wait_ge(q["probs"], START + NM * g + m + 1)
                                pe.wait_ge(q["p_lo"], START + NM * g + m)
                                for h in range(2):
                                    for b in range(nb):
                                        last = nc.tensor.transpose(pairs[2][:, h, b * P:(b + 1) * P],
                                                                   PR[s][:, h, b * P:(b + 1) * P], ident)
                                last.then_inc(q["turned"], 1)
                            if 2 <= t:
                                m, s = t - 2, t % 2
                                i, lo, nb, _ = window(m)
                                pe.wait_ge(q["p_lo"], START + NM * g + m + 1)
                                pe.wait_ge(q["gated"], START + NM * g + m)
                                for h in range(2):
                                    v0 = HD * (1 - h)
                                    for b in range(nb):
                                        for n, (a, c) in enumerate(((v_hi, p_hi), (v_hi, p_lo), (v_lo, p_hi))):
                                            last = nc.tensor.matmul(bank(6)[:, 0:P],
                                                                    a[:, lo + b, v0:v0 + P], c[s][:, h, b * P:(b + 1) * P],
                                                                    start=(h == 0 and b == 0 and n == 0),
                                                                    stop=(h == 1 and b == nb - 1 and n == 2))
                                last.then_inc(q["summed"], 1)

                @block.scalar
                def _(act):
                    with act.Fori(0, 2) as g:
                        def q_part(uu):
                            act.wait_ge(q["rotated"], START + 3 * g + 2 + uu)
                            act.wait_ge(q["scored"], START + NM * g)
                            nc.scalar.activation(q_hi[uu][:], X[:], ACT.Copy).then_inc(q["hi"], 1)

                        def z_part(uu):
                            act.wait_ge(q["z_in"], START + 16 * (2 * g + uu + 1))
                            act.wait_ge(q["gated"], START + NM * g)
                            nc.scalar.activation(ZT[uu][:], ZX[:], ACT.Tanh, scale=0.5).then_inc(q["tanh"], 1)

                        act.wait_ge(q["rotated"], START + 3 * g + 1)
                        act.wait_ge(q["scored"], START + NM * g)
                        nc.scalar.activation(k_hi[:], X[:], ACT.Copy).then_inc(q["hi"], 1)
                        act.wait_ge(q["v_turned"], START + g + 1)
                        act.wait_ge(q["summed"], START + NM * g)
                        act.wait_ge(q["pads"], START + 2)
                        nc.scalar.activation(v_hi[:, :, HD:2 * HD], v_turned, ACT.Copy)\
                            .then_inc(q["v_hi"], 1)
                        q_part(0)
                        q_part(1)
                        for t in range(NM + 1):
                            if t % NT == 0 and t < NM:
                                z_part(t // NT)
                            if t < NM:
                                m, s = t, t % 2
                                i, lo, nb, _ = window(m)
                                act.wait_ge(q["shifted"], START + NM * g + m + 1)
                                act.wait_ge(q["turned"], START + NM * g + max(m - 1, 0))
                                for h in range(2):
                                    nc.scalar.activation(PR[s][:, h, 0:nb * P], SM[s][:, h, 0:nb * P], ACT.Exp,
                                                         bias=stat[s][:, 1, h:h + 1], accum_out=stat[s][:, 3, h:h + 1])
                                nc.scalar.activation(stat[s][:, 4, :], stat[s][:, 2, :], ACT.Exp).then_inc(q["exped"], 1)
                                side.out(act, g, t // 2, t % 2, side_unit(g, t // 2))
                            if 1 <= t:
                                m, s = t - 1, (t - 1) % 2
                                i, lo, nb, _ = window(m)
                                act.wait_ge(q["turned"], START + NM * g + m + 1)
                                act.wait_ge(q["summed"], START + NM * g + max(m - 1, 0))
                                nc.scalar.activation(p_hi[s][:, :, 0:nb * P], pairs[2][:, :, 0:nb * P], ACT.Copy)\
                                    .then_inc(q["p_hi"], 1)
                    side.finish(act, 2)

                @block.vector
                def _(dve):
                    for v in (v_hi, v_lo):
                        nc.vector.memset(v[:].bitcast(F32), 0.0).then_inc(q["pads"], 1)
                    dve.wait_ge(q["sink_in"], START + 16)
                    dve.wait_ge(q["pads"], START + 2)
                    with dve.Fori(0, 2) as g:
                        dve.wait_ge(q["shifted"], START + NM * g)
                        nc.vector.tensor_scalar(sink, sinks[:, ds(4 * g, 4)], 1.0, None, ALU.mult).then_inc(q["sink"], 1)
                        nc.vector.tensor_scalar(neg_sink, sinks[:, ds(4 * g, 4)], -1.0, None, ALU.mult)\
                            .then_inc(q["neg_sink"], 1)

                        def rotate(r):
                            dve.wait_ge(q["x_in"], START + 96 * (3 * g + r + 1))
                            nc.vector.tensor_tensor(X[:], X[:], cos[:], ALU.mult).then_inc(q["cosined"], 1)
                            dve.wait_ge(q["cosined"], START + 3 * g + r + 1)
                            dve.wait_ge(q["sined"], START + 3 * g + r + 1)
                            nc.vector.tensor_tensor(X[:], X[:], XR[:], ALU.add).then_inc(q["rotated"], 1)

                        def low(r, hi, lo):
                            dve.wait_ge(q["hi"], START + 3 * g + r + 1)
                            nc.vector.tensor_tensor(lo[:], X[:], hi[:].bitcast(F32), ALU.subtract).then_inc(q["lo"], 1)

                        rotate(0)
                        low(0, k_hi, k_lo)
                        dve.wait_ge(q["v_hi"], START + g + 1)
                        nc.vector.tensor_tensor(v_lo[:, :, HD:2 * HD], v_turned,
                                                v_hi[:, :, HD:2 * HD].bitcast(F32), ALU.subtract).then_inc(q["v_lo"], 1)
                        rotate(1)
                        low(1, q_hi[0], q_lo[0])
                        rotate(2)
                        low(2, q_hi[1], q_lo[1])
                        for t in range(NM + 2):
                            if t < NM:
                                m, s = t, t % 2
                                i, lo, nb, b0 = window(m)
                                st = stat[s]
                                hh = slice(2 * (m // NT), 2 * (m // NT) + 2)
                                dve.wait_ge(q["scored"], START + NM * g + m + 1)
                                dve.wait_ge(q["exped"], START + NM * g + max(m - 1, 0))
                                nc.vector.scalar_tensor_tensor(out=SM[s][:, :, 0:nb * P], in0=pairs[s][:, :, 0:nb * P],
                                                               scalar=SCALE, in1=bcast(band[:, b0:b0 + nb * P], 2),
                                                               op0=ALU.mult, op1=ALU.add).then_inc(q["masked"], 1)
                                dve.wait_ge(q["masked"], START + NM * g + m + 1)
                                nc.vector.tensor_reduce(st[:, 0, :], SM[s][:, :, 0:nb * P], AX_X, ALU.max)\
                                    .then_inc(q["rowmax"], 1)
                                dve.wait_ge(q["rowmax"], START + NM * g + m + 1)
                                dve.wait_ge(q["neg_sink"], START + g + 1)
                                nc.vector.scalar_tensor_tensor(out=st[:, 1, :], in0=st[:, 0, :], scalar=-1.0,
                                                               in1=neg_sink[:, hh], op0=ALU.mult, op1=ALU.min)\
                                    .then_inc(q["negmax"], 1)
                                dve.wait_ge(q["negmax"], START + NM * g + m + 1)
                                dve.wait_ge(q["sink"], START + g + 1)
                                nc.vector.tensor_tensor(st[:, 2, :], sink[:, hh], st[:, 1, :], ALU.add)\
                                    .then_inc(q["shifted"], 1)
                            if t % NT == 1 and t < NM:
                                uu = t // NT
                                dve.wait_ge(q["tanh"], START + 2 * g + uu + 1)
                                nc.vector.scalar_tensor_tensor(out=ZT[uu][:], in0=ZT[uu][:], scalar=1.0, in1=ZX[:],
                                                               op0=ALU.add, op1=ALU.mult).then_inc(q["z_gate"], 1)
                            if t < NM:
                                m, s = t, t % 2
                                i, lo, nb, _ = window(m)
                                st = stat[s]
                                dve.wait_ge(q["exped"], START + NM * g + m + 1)
                                nc.vector.tensor_tensor(st[:, 5, :], st[:, 3, :], st[:, 4, :], ALU.add)\
                                    .then_inc(q["denom"], 1)
                                dve.wait_ge(q["denom"], START + NM * g + m + 1)
                                nc.vector.reciprocal(st[:, 6, :], st[:, 5, :]).then_inc(q["recip"], 1)
                                dve.wait_ge(q["recip"], START + NM * g + m + 1)
                                for h in range(2):
                                    last = nc.vector.tensor_scalar(PR[s][:, h, 0:nb * P], PR[s][:, h, 0:nb * P],
                                                                   st[:, 6, h:h + 1], None, ALU.mult)
                                last.then_inc(q["probs"], 1)
                            if 1 <= t <= NM:
                                m, s = t - 1, (t - 1) % 2
                                i, lo, nb, _ = window(m)
                                dve.wait_ge(q["p_hi"], START + NM * g + m + 1)
                                dve.wait_ge(q["summed"], START + NM * g + max(m - 1, 0))
                                nc.vector.tensor_tensor(p_lo[s][:, :, 0:nb * P], pairs[2][:, :, 0:nb * P],
                                                        p_hi[s][:, :, 0:nb * P].bitcast(F32), ALU.subtract)\
                                    .then_inc(q["p_lo"], 1)
                            if 2 <= t:
                                m = t - 2
                                i = m % NT
                                dve.wait_ge(q["summed"], START + NM * g + m + 1)
                                if i == 0:
                                    dve.wait_ge(q["stored"], START + 16 * (2 * g + m // NT))
                                    dve.wait_ge(q["z_gate"], START + 2 * g + m // NT + 1)
                                nc.vector.scalar_tensor_tensor(out=O[:, i * P:(i + 1) * P], in0=bank(6)[:, 0:P],
                                                               scalar=0.5, in1=ZT[m // NT][:, i * P:(i + 1) * P],
                                                               op0=ALU.mult, op1=ALU.mult).then_inc(q["gated"], 1)

        def attend_full(l):
            with Phase("diff", ["par_in", "lam", "lq", "lsum", "lexp", "g_scaled", "x_in", "cosined", "sined", "rotated",
                                "hi", "lo", "v_in", "v_turned", "v_hi", "v_lo", "z_in", "tanh", "z_gate", "scored",
                                "negmax", "bias", "exped", "recip", "nlam", "scaled", "mixed", "turned", "a_hi",
                                "a_lo", "summed", "copied", "squared", "total", "log", "root", "normed", "gated",
                                "stored"] + Side.SEMS) as (block, q):
                X, XR = sb("diff_x", [P, S]), sb("diff_xr", [P, S])
                VX = sb("diff_vx", [P, S])
                ZT = sb("diff_zt", [P, S])
                qk_hi = [sb(f"diff_{n}_hi", [P, S], F32R) for n in "qk"]
                qk_lo = [sb(f"diff_{n}_lo", [P, S], F32R) for n in "qk"]
                v_hi, v_lo = sb("diff_v_hi", [P, NT, P], F32R), sb("diff_v_lo", [P, NT, P], F32R)
                PR = [[sb(f"diff_p{s}{c}", [P, S]) for c in range(2)] for s in range(2)]
                a_hi, a_lo = sb("diff_a_hi", [P, NT, 2 * P], F32R), sb("diff_a_lo", [P, NT, 2 * P], F32R)
                O = sb("diff_o", [P, S])
                OUT = sb("diff_out", [P, S])
                stat = [sb(f"diff_stat{s}", [P, 5, 2]) for s in range(2)]
                side = Side(l, q, 8)
                side_unit = lambda h, k: h * 4 + (U_C + k if k < 4 else N_PLAIN + k - 4)
                side_column = lambda h, k: side_unit(h, k) * P + (N_BA if k >= 4 else 0)
                lq = sb("diff_lq", [P, 4, HD])
                par = sb("diff_par", [P, 12])
                g_raw, g_sub, lam_in, lsum, lexp, lam, nlam = (par[:, 0:1], par[:, 1:2], par[:, 2:4], par[:, 4:6],
                                                               par[:, 6:8], par[:, 8:9], par[:, 9:10])
                flat = lambda pair: pair[:].rearrange("p a b -> p (a b)")

                @block.sync
                def _(sp):
                    sp.dma_start(lq[:].rearrange("p a b -> p (a b)"),
                                 b_lambda[ds(l, 1)].rearrange("o a b -> (o a b)").partition_broadcast(P))\
                        .then_inc(q["par_in"], 16)
                    sp.dma_start(g_raw, b_subln_g[ds(l, 1), :].rearrange("o p -> p o"), allow_slow_non_contiguous=True)\
                        .then_inc(q["par_in"], 16)
                    sp.dma_start(lam_in, lam_t[:, ds(l, 1), :].rearrange("p o n -> p (o n)")).then_inc(q["par_in"], 16)
                    with sp.Fori(0, 4) as h:
                        for n, u in enumerate((U_BQ, U_BK)):
                            src = lambda r, c: proj[u:u + 4][ds(h, 1), r:r + c, :].rearrange("o p s -> (o p) s")
                            if n == 0:
                                sp.wait_ge(q["normed"], START + h)
                            sp.wait_ge(q["lo"], START + 2 * h + n)
                            sp.dma_start(X[:], src(0, P)).then_inc(q["x_in"], 16)
                            for a in range(4):
                                sp.dma_start(XR[32 * a:32 * a + 32, :], src(32 * (a ^ 1), 32)).then_inc(q["x_in"], 16)
                            if n == 0:
                                sp.wait_ge(q["z_gate"], START + h)
                                sp.dma_start(VX[:], proj[U_BV:U_BV + 4][ds(h, 1)].rearrange("o p s -> (o p) s"))\
                                    .then_inc(q["v_in"], 16)
                            if n == 0:
                                for k in range(2):
                                    side.load(sp, h, k, side_column(h, k))
                        sp.wait_ge(q["v_turned"], START + h + 1)
                        sp.dma_start(VX[:], proj[U_BZ:U_BZ + 4][ds(h, 1)].rearrange("o p s -> (o p) s")).then_inc(q["z_in"], 16)
                        for k in range(2, 8):
                            side.load(sp, h, k, side_column(h, k))
                        sp.wait_ge(q["gated"], START + h + 1)
                        sp.dma_start(gated[4:8][ds(h, 1)].rearrange("o p s -> (o p) s"), OUT[:]).then_inc(q["stored"], 16)
                    sp.wait_ge(q["stored"], START + 16 * 4)

                @block.gpsimd
                def _(pool):
                    with pool.Fori(0, 4) as h:
                        for n in range(2):
                            pool.wait_ge(q["x_in"], START + 80 * (2 * h + n + 1))
                            nc.gpsimd.tensor_tensor(XR[:], XR[:], sin[:], ALU.mult).then_inc(q["sined"], 1)
                        for k in range(8):
                            side.split(pool, h, k)
                        pool.wait_ge(q["normed"], START + h + 1)
                        pool.wait_ge(q["stored"], START + 16 * h)
                        nc.gpsimd.tensor_tensor(OUT[:], O[:], ZT[:], ALU.mult).then_inc(q["gated"], 1)

                @block.tensor
                def _(pe):
                    with pe.Fori(0, 4) as h:
                        pe.wait_ge(q["v_in"], START + 16 * h + 16)
                        pe.wait_ge(q["exped"], START + 16 * h)
                        for t in range(NT):
                            last = nc.tensor.transpose(bank(t // 4)[:, t % 4 * P:(t % 4 + 1) * P],
                                                       VX[:, t * P:(t + 1) * P], ident)
                        last.then_inc(q["v_turned"], 1)
                        pe.wait_ge(q["lo"], START + 2 * h + 2)
                        pe.wait_ge(q["v_lo"], START + h + 1)
                        for t in range(NT + 1):
                            if t < NT:
                                m = t
                                for c in range(2):
                                    pe.wait_ge(q["exped"], START + 16 * h + max(2 * m + c - 1, 0))
                                    r = slice(c * HD, (c + 1) * HD)
                                    for n, (a, b) in enumerate(((qk_hi[0], qk_hi[1]), (qk_hi[0], qk_lo[1]),
                                                                (qk_lo[0], qk_hi[1]))):
                                        for half in range(2):
                                            last = nc.tensor.matmul(pairs[c][:, half, :], a[r, m * P:(m + 1) * P],
                                                                    b[r, half * HALF:(half + 1) * HALF],
                                                                    start=(n == 0), stop=(n == 2))
                                    last.then_inc(q["scored"], 1)
                                side.half(pe, h, t, 0)
                            if 1 <= t:
                                m = t - 1
                                pe.wait_ge(q["mixed"], START + NT * h + m + 1)
                                pe.wait_ge(q["a_lo"], START + NT * h + m)
                                for b in range(NT):
                                    last = nc.tensor.transpose(pairs[2][:, b // 4, b % 4 * P:(b % 4 + 1) * P],
                                                               PR[m % 2][0][:, b * P:(b + 1) * P], ident)
                                last.then_inc(q["turned"], 1)
                            if t < NT:
                                side.half(pe, h, t, 1)
                            if t >= 2 and t % 2 == 0:
                                j = t // 2 - 1
                                pe.wait_ge(q["a_lo"], START + NT * h + 2 * j + 2)
                                pe.wait_ge(q["copied"], START + 4 * h + j)
                                for b in range(NT):
                                    for n, (a, c) in enumerate(((v_hi, a_hi), (v_hi, a_lo), (v_lo, a_hi))):
                                        last = nc.tensor.matmul(bank(6)[:, 0:2 * P], a[:, b, :], c[:, b, :],
                                                                start=(b == 0 and n == 0), stop=(b == NT - 1 and n == 2))
                                last.then_inc(q["summed"], 1)
                        pe.wait_ge(q["squared"], START + h + 1)
                        for half in range(2):
                            last = nc.tensor.matmul(pairs[2][:, half, :], ones, X[:, half * HALF:(half + 1) * HALF],
                                                    start=True, stop=True)
                        last.then_inc(q["total"], 1)

                @block.scalar
                def _(act):
                    act.wait_ge(q["lsum"], START + 2)
                    nc.scalar.activation(lexp, lsum, ACT.Exp).then_inc(q["lexp"], 1)
                    with act.Fori(0, 4) as h:
                        for n in range(2):
                            act.wait_ge(q["rotated"], START + 2 * h + n + 1)
                            act.wait_ge(q["scored"], START + 16 * h)
                            nc.scalar.activation(qk_hi[n][:], X[:], ACT.Copy).then_inc(q["hi"], 1)
                            if n == 0:
                                act.wait_ge(q["v_turned"], START + h + 1)
                                act.wait_ge(q["summed"], START + 4 * h)
                                nc.scalar.activation(v_hi[:].rearrange("p t d -> p (t d)"), flat(pairs[0]), ACT.Copy)\
                                    .then_inc(q["v_hi"], 1)
                        act.wait_ge(q["z_in"], START + 16 * h + 16)
                        act.wait_ge(q["gated"], START + h)
                        nc.scalar.activation(ZT[:], VX[:], ACT.Tanh, scale=0.5).then_inc(q["tanh"], 1)
                        for t in range(NT + 1):
                            if t < NT:
                                m, st = t, stat[t % 2]
                                for c in range(2):
                                    act.wait_ge(q["bias"], START + 16 * h + 2 * m + c + 1)
                                    act.wait_ge(q["turned"], START + NT * h + max(m - 1, 0))
                                    nc.scalar.activation(PR[m % 2][c][:], flat(pairs[c]), ACT.Exp, scale=SCALE,
                                                         bias=st[:, 1, c:c + 1], accum_out=st[:, 2, c:c + 1])\
                                        .then_inc(q["exped"], 1)
                                act.wait_ge(q["recip"], START + NT * h + m + 1)
                                nc.scalar.activation(PR[m % 2][0][:], PR[m % 2][0][:], ACT.Copy, scale=st[:, 3, 0:1])\
                                    .then_inc(q["scaled"], 1)
                                side.out(act, h, t, 0, side_unit(h, t), gate=t >= 4)
                            if 1 <= t:
                                m = t - 1
                                act.wait_ge(q["turned"], START + NT * h + m + 1)
                                if m % 2 == 0:
                                    act.wait_ge(q["summed"], START + 4 * h + m // 2)
                                nc.scalar.activation(a_hi[:, :, m % 2 * P:(m % 2 + 1) * P],
                                                     pairs[2][:].rearrange("p a (b s) -> p (a b) s", s=P), ACT.Copy)\
                                    .then_inc(q["a_hi"], 1)
                            if t < NT:
                                side.out(act, h, t, 1, side_unit(h, t), gate=t >= 4)
                            if t >= 2 and t % 2 == 0:
                                j = t // 2 - 1
                                act.wait_ge(q["summed"], START + 4 * h + j + 1)
                                if j == 0:
                                    act.wait_ge(q["gated"], START + h)
                                nc.scalar.activation(O[:, j * 2 * P:(j + 1) * 2 * P], bank(6)[:, 0:2 * P], ACT.Copy)\
                                    .then_inc(q["copied"], 1)
                        act.wait_ge(q["copied"], START + 4 * h + 4)
                        act.wait_ge(q["lo"], START + 2 * h + 2)
                        nc.scalar.activation(X[:], O[:], ACT.Square).then_inc(q["squared"], 1)
                        act.wait_ge(q["total"], START + h + 1)
                        root(act, XR[:], flat(pairs[2]), P, q["log"], h + 1, q["root"])
                    side.finish(act, 4)

                @block.vector
                def _(dve):
                    dve.wait_ge(q["par_in"], START + 48)
                    nc.vector.tensor_tensor(lq[:, 0:4:2, :], lq[:, 0:4:2, :], lq[:, 1:4:2, :], ALU.mult).then_inc(q["lq"], 1)
                    dve.wait_ge(q["lq"], START + 1)
                    for n in range(2):
                        nc.vector.tensor_reduce(lsum[:, n:n + 1], lq[:, 2 * n, :], AX_X, ALU.add).then_inc(q["lsum"], 1)
                    dve.wait_ge(q["lexp"], START + 1)
                    nc.vector.tensor_tensor(lam, lexp[:, 0:1], lexp[:, 1:2], ALU.subtract).then_inc(q["lam"], 1)
                    dve.wait_ge(q["lam"], START + 1)
                    nc.vector.tensor_tensor(lam, lam, lam_in[:, 0:1], ALU.add).then_inc(q["lam"], 1)
                    dve.wait_ge(q["lam"], START + 2)
                    nc.vector.tensor_scalar(nlam, lam, -1.0, None, ALU.mult).then_inc(q["lam"], 1)
                    nc.vector.tensor_tensor(g_sub, g_raw, lam_in[:, 1:2], ALU.mult).then_inc(q["g_scaled"], 1)
                    dve.wait_ge(q["lam"], START + 3)
                    dve.wait_ge(q["g_scaled"], START + 1)
                    with dve.Fori(0, 4) as h:
                        for n in range(2):
                            dve.wait_ge(q["x_in"], START + 80 * (2 * h + n + 1))
                            nc.vector.tensor_tensor(X[:], X[:], cos[:], ALU.mult).then_inc(q["cosined"], 1)
                            dve.wait_ge(q["cosined"], START + 2 * h + n + 1)
                            dve.wait_ge(q["sined"], START + 2 * h + n + 1)
                            nc.vector.tensor_tensor(X[:], X[:], XR[:], ALU.add).then_inc(q["rotated"], 1)
                            dve.wait_ge(q["hi"], START + 2 * h + n + 1)
                            nc.vector.tensor_tensor(qk_lo[n][:], X[:], qk_hi[n][:].bitcast(F32), ALU.subtract)\
                                .then_inc(q["lo"], 1)
                            if n == 0:
                                dve.wait_ge(q["v_hi"], START + h + 1)
                                nc.vector.tensor_tensor(v_lo[:].rearrange("p t d -> p (t d)"), flat(pairs[0]),
                                                        v_hi[:].rearrange("p t d -> p (t d)").bitcast(F32), ALU.subtract)\
                                    .then_inc(q["v_lo"], 1)
                        for t in range(NT + 1):
                            if t < NT:
                                m, st = t, stat[t % 2]
                                for c in range(2):
                                    dve.wait_ge(q["scored"], START + 16 * h + 2 * m + c + 1)
                                    nc.vector.tensor_reduce(st[:, 0, c:c + 1], flat(pairs[c]), AX_X, ALU.max, negate=True)\
                                        .then_inc(q["negmax"], 1)
                                    dve.wait_ge(q["negmax"], START + 16 * h + 2 * m + c + 1)
                                    nc.vector.tensor_scalar(st[:, 1, c:c + 1], st[:, 0, c:c + 1], SCALE, None, ALU.mult)\
                                        .then_inc(q["bias"], 1)
                            if t == 0:
                                dve.wait_ge(q["tanh"], START + h + 1)
                                nc.vector.scalar_tensor_tensor(out=ZT[:], in0=ZT[:], scalar=1.0, in1=VX[:],
                                                               op0=ALU.add, op1=ALU.mult).then_inc(q["z_gate"], 1)
                            if t < NT:
                                m, st = t, stat[t % 2]
                                dve.wait_ge(q["exped"], START + 16 * h + 2 * m + 2)
                                nc.vector.reciprocal(st[:, 3, :], st[:, 2, :]).then_inc(q["recip"], 1)
                                dve.wait_ge(q["recip"], START + NT * h + m + 1)
                                nc.vector.tensor_scalar(st[:, 4, 0:1], st[:, 3, 1:2], nlam, None, ALU.mult)\
                                    .then_inc(q["nlam"], 1)
                                dve.wait_ge(q["nlam"], START + NT * h + m + 1)
                                dve.wait_ge(q["scaled"], START + NT * h + m + 1)
                                nc.vector.scalar_tensor_tensor(out=PR[m % 2][0][:], in0=PR[m % 2][1][:],
                                                               scalar=st[:, 4, 0:1], in1=PR[m % 2][0][:],
                                                               op0=ALU.mult, op1=ALU.add).then_inc(q["mixed"], 1)
                            if t >= 1:
                                m = t - 1
                                dve.wait_ge(q["a_hi"], START + NT * h + m + 1)
                                w = slice(m % 2 * P, (m % 2 + 1) * P)
                                nc.vector.tensor_tensor(a_lo[:, :, w], pairs[2][:].rearrange("p a (b s) -> p (a b) s", s=P),
                                                        a_hi[:, :, w].bitcast(F32), ALU.subtract).then_inc(q["a_lo"], 1)
                        dve.wait_ge(q["root"], START + h + 1)
                        nc.vector.scalar_tensor_tensor(out=O[:], in0=O[:], scalar=g_sub, in1=XR[:], op0=ALU.mult,
                                                       op1=ALU.mult).then_inc(q["normed"], 1)

        def convolve(l):
            with Phase("conv", ["in0", "in1", "in2", "pad", "tap", "tanh", "silu", "squared", "total", "log", "root",
                                "normed", "put0", "put1", "put2", "par_in", "pre", "pre_act", "sums"]
                       + Side.SEMS) as (block, q):
                X = [sb(f"conv_x{n}", [P, S + 4]) for n in range(3)]
                Y = [sb(f"conv_y{n}", [P, S]) for n in range(3)]
                T = [sb(f"conv_t{n}", [P, S]) for n in range(3)]
                W = [sb(f"conv_w{n}", [P, 5]) for n in range(3)]
                R = [sb(f"conv_r{n}", [P, S]) for n in range(2)]
                side = Side(l, q, 2)
                side_unit = lambda h, k: h * 2 + (N_PLAIN + 16 + k)
                par = sb("conv_par", [P, 2, 8])
                tmp = sb("conv_tmp", [P, 4, NT, 8])
                eps4 = sb("conv_eps4", [P, 1])
                flat = lambda pair: pair[:].rearrange("p a b -> p (a b)")
                a_log, dt = par[:, 0, :], par[:, 1, :]
                t0, t1, t2, t3 = (tmp[:, n] for n in range(4))

                @block.sync
                def _(sp):
                    for n, src in enumerate((c_a_log, c_dt_bias)):
                        sp.dma_start(par[:, n, :], src[ds(l, 1)].rearrange("o d h -> (o d h)").partition_broadcast(P))\
                            .then_inc(q["par_in"], 16)
                    sp.wait_ge(q["pad"], START + 3)
                    with sp.Fori(0, 4) as h:
                        for n in range(3):
                            sp.wait_ge(q["silu"], START + 3 * h)
                            sp.dma_start(X[n][:, 2:S + 2], proj[U_C + 4 * n:U_C + 4 * n + 4][ds(h, 1)]
                                         .rearrange("o p s -> (o p) s")).then_inc(q[f"in{n}"], 16)
                            sp.dma_start(W[n][:], c_conv_w[ds(l, 1), :, 4 * n * P:4 * (n + 1) * P]
                                         .rearrange("o t (h p) -> h p (o t)", p=P)[ds(h, 1)].rearrange("o p t -> (o p) t"),
                                         allow_slow_non_contiguous=True).then_inc(q[f"in{n}"], 16)
                        for k in range(2):
                            side.load(sp, h, k, side_unit(h, k) * P + N_BA)
                        for n in range(3):
                            if n < 2:
                                sp.wait_ge(q["normed"], START + 2 * h + n + 1)
                            else:
                                sp.wait_ge(q["silu"], START + 3 * h + 3)
                            sp.dma_start(conv[4 * n:4 * n + 4][ds(h, 1)].rearrange("o p s -> (o p) s"), Y[n][:])\
                                .then_inc(q[f"put{n}"], 16)
                    for n in range(3):
                        sp.wait_ge(q[f"put{n}"], START + 64)

                @block.scalar
                def _(act):
                    act.wait_ge(q["pre"], START + 3)
                    nc.scalar.activation(t1, t1, ACT.Exp).then_inc(q["pre_act"], 1)
                    nc.scalar.activation(a_log, a_log, ACT.Exp).then_inc(q["pre_act"], 1)
                    nc.scalar.activation(t2, ba[:, :, 0:8], ACT.Exp, scale=-1.0).then_inc(q["pre_act"], 1)
                    act.wait_ge(q["pre_act"], START + 3)
                    nc.scalar.activation(t1, t1, ACT.Ln, bias=ones[:, 0:1]).then_inc(q["pre_act"], 1)
                    act.wait_ge(q["pre"], START + 10)
                    nc.scalar.activation(decay[:, 3], decay[:, 2], ACT.Exp).then_inc(q["pre_act"], 1)
                    nc.scalar.activation(decay[:, 4], t3, ACT.Exp).then_inc(q["pre_act"], 1)
                    nc.scalar.activation(decay[:, 5], t0, ACT.Exp).then_inc(q["pre_act"], 1)
                    with act.Fori(0, 4) as h:
                        def tanh(n):
                            act.wait_ge(q["tap"], START + 15 * h + 5 * n + 5)
                            nc.scalar.activation(T[n][:], Y[n][:], ACT.Tanh, scale=0.5).then_inc(q["tanh"], 1)

                        def unit_length(n):
                            act.wait_ge(q["silu"], START + 3 * h + n + 1)
                            nc.scalar.activation(T[n][:], Y[n][:], ACT.Square).then_inc(q["squared"], 1)
                            act.wait_ge(q["total"], START + 2 * h + n + 1)
                            root(act, R[n][:], flat(pairs[n]), 1, q["log"], 2 * h + n + 1, q["root"], bias=eps4[:])

                        for n in range(3):
                            tanh(n)
                            side.out(act, h, n // 2, n % 2, side_unit(h, n // 2), gate=True)
                        unit_length(0)
                        side.out(act, h, 1, 1, side_unit(h, 1), gate=True)
                        unit_length(1)
                    side.finish(act, 4)

                @block.gpsimd
                def _(pool):
                    with pool.Fori(0, 4) as h:
                        for k in range(2):
                            side.split(pool, h, k)

                @block.tensor
                def _(pe):
                    pe.wait_ge(q["pre"], START + 7)
                    for d in range(2):
                        last = nc.tensor.matmul(bank(4 + d)[:, 0:4 * NT], tri(d), decay[:, 0, :, 4 * d:4 * d + 4],
                                                start=True, stop=True)
                    nc.tensor.matmul(bank(6)[:, 0:8 * NT], ones, decay[:, 0].rearrange("p t n -> p (t n)"),
                                     start=True, stop=True).then_inc(q["sums"], 1)
                    with pe.Fori(0, 4) as h:
                        for k in range(3):
                            side.half(pe, h, k // 2, k % 2)
                        for n in range(2):
                            if n == 1:
                                side.half(pe, h, 1, 1)
                            pe.wait_ge(q["squared"], START + 2 * h + n + 1)
                            for half in range(2):
                                last = nc.tensor.matmul(pairs[n][:, half, :], ones, T[n][:, half * HALF:(half + 1) * HALF],
                                                        start=True, stop=True)
                            last.then_inc(q["total"], 1)

                @block.vector
                def _(dve):
                    nc.vector.memset(eps4[:], 4 * EPS)
                    for n in range(3):
                        nc.vector.memset(X[n][:], 0.0).then_inc(q["pad"], 1)
                    done = [0]

                    def pre(ins):
                        done[0] += 1
                        ins.then_inc(q["pre"], 1)
                        dve.wait_ge(q["pre"], START + done[0])

                    by_head = lambda a: a.unsqueeze(1).to_broadcast([P, NT, 8])
                    dve.wait_ge(q["par_in"], START + 32)
                    pre(nc.vector.tensor_tensor(t0, ba[:, :, 8:16], by_head(dt), ALU.add))
                    pre(nc.vector.scalar_tensor_tensor(out=t1, in0=t0, scalar=-1.0, in1=t0, op0=ALU.mult, op1=ALU.min))
                    pre(nc.vector.tensor_scalar(t0, t0, 0.0, None, ALU.max))
                    dve.wait_ge(q["pre_act"], START + 4)
                    pre(nc.vector.tensor_tensor(t0, t0, t1, ALU.add))
                    pre(nc.vector.scalar_tensor_tensor(out=decay[:, 0], in0=t0, scalar=-1.0, in1=by_head(a_log),
                                                       op0=ALU.mult, op1=ALU.mult))
                    pre(nc.vector.tensor_scalar(t2, t2, 1.0, None, ALU.add))
                    pre(nc.vector.reciprocal(decay[:, 1], t2))
                    dve.wait_ge(q["sums"], START + 1)
                    for d in range(2):
                        last = nc.vector.tensor_copy(decay[:, 2, :, 4 * d:4 * d + 4],
                                                     bank(4 + d)[:, 0:4 * NT].rearrange("p (t n) -> p t n", n=4))
                    pre(last)
                    pre(nc.vector.tensor_copy(t3, bank(6)[:, 0:8 * NT].rearrange("p (t n) -> p t n", n=8)))
                    pre(nc.vector.tensor_tensor(t0, t3, decay[:, 2], ALU.subtract))
                    dve.wait_ge(q["pre_act"], START + 7)
                    pre(nc.vector.tensor_scalar(decay[:, 3], decay[:, 3], -1.0, None, ALU.mult))

                    with dve.Fori(0, 4) as h:
                        def taps(n):
                            dve.wait_ge(q[f"in{n}"], START + 32 * h + 32)
                            dve.wait_ge(q[f"put{n}"], START + 16 * h)
                            for t in range(5):
                                x_t = X[n][:, t:t + S]
                                if t == 0:
                                    last = nc.vector.tensor_scalar(Y[n][:], x_t, W[n][:, 0:1], None, ALU.mult)
                                else:
                                    dve.wait_ge(q["tap"], START + 15 * h + 5 * n + t)
                                    last = nc.vector.scalar_tensor_tensor(out=Y[n][:], in0=x_t, scalar=W[n][:, t:t + 1],
                                                                          in1=Y[n][:], op0=ALU.mult, op1=ALU.add)
                                last.then_inc(q["tap"], 1)

                        def silu(n):
                            dve.wait_ge(q["tanh"], START + 3 * h + n + 1)
                            nc.vector.scalar_tensor_tensor(out=Y[n][:], in0=T[n][:], scalar=1.0, in1=Y[n][:],
                                                           op0=ALU.add, op1=ALU.mult).then_inc(q["silu"], 1)

                        def unit_length(n):
                            dve.wait_ge(q["root"], START + 2 * h + n + 1)
                            nc.vector.scalar_tensor_tensor(out=Y[n][:], in0=Y[n][:], scalar=(P ** -0.5, 1.0)[n],
                                                           in1=R[n][:], op0=ALU.mult, op1=ALU.mult).then_inc(q["normed"], 1)

                        taps(0)
                        taps(1)
                        silu(0)
                        taps(2)
                        silu(1)
                        silu(2)
                        unit_length(0)
                        unit_length(1)

        def delta_rule(l):
            pe_names = ["k_turned", "v_turned", "rows", "gram", "qk", "a_turned"]
            dve_names = ["col", "diff", "neg", "attn", "qm", "t_off", "t0"]
            for k in range(1, N_LEVELS):
                pe_names += [f"x{k}", f"tx{k}", f"ux{k}"] if k < N_LEVELS - 1 else [f"x{k}", f"ux{k}"]
                dve_names += [f"xm{k}", f"t{k}", f"u{k}"] if k < N_LEVELS - 1 else [f"xm{k}", f"u{k}"]
            pe_names += ["z", "v_new", "o", "s_add"]
            dve_names += ["r", "vw", "s"]
            act_names = ["k_tok", "v_tok", "rows_exp", "decay", "o_out"]
            pool_names = ["dtm", "bm", "u1", "u", "qd", "vt"]
            with Phase("delta", ["in0", "in1", "put0", "put1", "state", "pe0", "pe1", "dve0", "dve1", "act0", "act1",
                                 "pool0", "pool1"]) as (block, q):
                pe_s, dve_s, act_s, pool_s = ([Steps(q[f"{e}{d}"], names) for d in range(2)] for e, names in
                                              (("pe", pe_names), ("dve", dve_names), ("act", act_names),
                                               ("pool", pool_names)))
                two = lambda name, shape: [sb(f"delta_{name}{d}", shape) for d in range(2)]
                IN = two("in", [P, 12, P])
                KT, VT, DT, EG, AT, BM, QM, T, U, XM, R, VW, VD, QD, ST, OC = (
                    two(n, [P, 4, P]) for n in ("kt", "vt", "dt", "eg", "at", "bm", "qm", "t", "u", "xm", "r", "vw", "vd",
                                                "qd", "st", "oc"))
                COL = two("col", [P, 6, 4])
                G, BETA, GC, NEG, EL, ET = range(6)
                B = [[bank(3 * d + n).rearrange("p (h s) -> p h s", h=4) for n in range(3)] for d in range(2)]
                tile_of = lambda c, d: c if d == 0 else c * -1 + (NT - 1)
                col = lambda d, what: cols(COL[d][:, what, :], P)
                heads = lambda ap: bcast(ap, 4)

                @block.sync
                def _(sp):
                    def load(c, d):
                        t = tile_of(c, d)
                        src = conv[:, :, ds(t * P, P)] if not isinstance(t, int) else conv[:, :, t * P:(t + 1) * P]
                        sp.dma_start(IN[d][:], src.rearrange("u p s -> p u s")).then_inc(q[f"in{d}"], 16)

                    for d in range(2):
                        load(0, d)
                    with sp.Fori(0, NT - 1) as c:
                        for d in range(2):
                            sp.wait_ge(pe_s[d].sem, pe_s[d].at(c, "z"))
                            sp.wait_ge(pool_s[d].sem, pool_s[d].at(c, "qd"))
                            load(c + 1, d)

                @block.tensor
                def _(pe):
                    with pe.Fori(0, NT) as c:
                        def four(d, out, lhs, rhs, name):
                            for h in range(4):
                                last = nc.tensor.matmul(out[:, h, :], lhs(h), rhs(h), start=True, stop=True)
                            pe_s[d].done(last, name)

                        kT = lambda d: lambda h: IN[d][:, 4 + h, :]
                        qT = lambda d: lambda h: IN[d][:, h, :]
                        of = lambda t: lambda h: t[:, h, :]
                        for d in range(2):
                            a, b, e = B[d]
                            pe.wait_ge(q[f"in{d}"], START + 16 * c + 16)
                            pe.wait_ge(dve_s[d].sem, dve_s[d].at(c))
                            pe.wait_ge(act_s[d].sem, act_s[d].at(c))
                            for name, out_, first in (("k_turned", a, 4), ("v_turned", b, 8)):
                                for h in range(4):
                                    last = nc.tensor.transpose(out_[:, h, :], IN[d][:, first + h, :], ident)
                                pe_s[d].done(last, name)
                            pe.wait_ge(dve_s[d].sem, dve_s[d].at(c, "col"))
                            four(d, e, lambda h: COL[d][:, G, h:h + 1].to_broadcast([P, P]), lambda h: tri(d), "rows")
                        for d in range(2):
                            a, b, e = B[d]
                            pe.wait_ge(act_s[d].sem, act_s[d].at(c, "k_tok"))
                            four(d, a, kT(d), kT(d), "gram")
                            pe.wait_ge(act_s[d].sem, act_s[d].at(c, "v_tok"))
                            four(d, b, kT(d), qT(d), "qk")
                        for d in range(2):
                            a, b, e = B[d]
                            pe.wait_ge(dve_s[d].sem, dve_s[d].at(c, "qm"))
                            pe.wait_ge(act_s[d].sem, act_s[d].at(c, "rows_exp"))
                            for h in range(4):
                                last = nc.tensor.transpose(e[:, h, :], QM[d][:, h, :], ident)
                            pe_s[d].done(last, "a_turned")
                        for k in range(1, N_LEVELS):
                            for d in range(2):
                                a, b, e = B[d]
                                t_name = f"t{k - 1}"
                                pe.wait_ge(dve_s[d].sem, dve_s[d].at(c, t_name))
                                four(d, a, of(QM[d]), of(T[d]), f"x{k}")
                            for d in range(2):
                                a, b, e = B[d]
                                if k == 1:
                                    pe.wait_ge(pool_s[d].sem, pool_s[d].at(c, "u"))
                                pe.wait_ge(dve_s[d].sem, dve_s[d].at(c, f"xm{k}"))
                                if k < N_LEVELS - 1:
                                    four(d, b, of(U[d]), of(XM[d]), f"tx{k}")
                                four(d, e, of(XM[d]), of(U[d]), f"ux{k}")
                        for d in range(2):
                            a, b, e = B[d]
                            if d == 0:
                                pe.wait_ge(q["state"], START + 2)
                            four(d, a, kT(d), of(ST[d]), "z")
                        for d in range(2):
                            a, b, e = B[d]
                            pe.wait_ge(dve_s[d].sem, dve_s[d].at(c, "r"))
                            four(d, b, of(U[d]), of(R[d]), "v_new")
                        for d in range(2):
                            a, b, e = B[d]
                            pe.wait_ge(dve_s[d].sem, dve_s[d].at(c, "vw"))
                            pe.wait_ge(pool_s[d].sem, pool_s[d].at(c, "qd"))
                            for h in range(4):
                                nc.tensor.matmul(e[:, h, :], ST[d][:, h, :], QD[d][:, h, :], start=True, stop=False)
                                last = nc.tensor.matmul(e[:, h, :], VW[d][:, h, :], AT[d][:, h, :], start=False, stop=True)
                            pe_s[d].done(last, "o")
                            pe.wait_ge(pool_s[d].sem, pool_s[d].at(c, "vt"))
                            four(d, a, of(KT[d]), of(VD[d]), "s_add")

                @block.scalar
                def _(act):
                    with act.Fori(0, NT) as c:
                        for d in range(2):
                            a, b, e = B[d]
                            act.wait_ge(pe_s[d].sem, pe_s[d].at(c, "k_turned"))
                            act_s[d].done(nc.scalar.activation(KT[d][:], a, ACT.Copy), "k_tok")
                            act.wait_ge(pe_s[d].sem, pe_s[d].at(c, "v_turned"))
                            act_s[d].done(nc.scalar.activation(VT[d][:], b, ACT.Copy, scale=0.5), "v_tok")
                        for d in range(2):
                            a, b, e = B[d]
                            act.wait_ge(dve_s[d].sem, dve_s[d].at(c, "diff"))
                            act_s[d].done(nc.scalar.activation(EG[d][:], e, ACT.Exp), "rows_exp")
                            act.wait_ge(dve_s[d].sem, dve_s[d].at(c, "neg"))
                            act_s[d].done(nc.scalar.activation(DT[d][:], DT[d][:], ACT.Exp), "decay")
                        for d in range(2):
                            a, b, e = B[d]
                            act.wait_ge(pe_s[d].sem, pe_s[d].at(c, "o"))
                            act.wait_ge(q[f"put{d}"], START + 16 * c)
                            act_s[d].done(nc.scalar.activation(OC[d][:], e, ACT.Copy), "o_out")
                            act.wait_ge(act_s[d].sem, act_s[d].at(c, "o_out"))
                            act.dma_start(o_dir[d].rearrange("h p s -> p h s")[:, :, ds(tile_of(c, d) * P, P)], OC[d][:])\
                                .then_inc(q[f"put{d}"], 16)
                    for d in range(2):
                        act.wait_ge(q[f"put{d}"], START + 16 * NT)

                @block.gpsimd
                def _(pool):
                    with pool.Fori(0, NT) as c:
                        for d in range(2):
                            tt = nc.gpsimd.tensor_tensor
                            s = pool_s[d]
                            pool.wait_ge(act_s[d].sem, act_s[d].at(c, "decay"))
                            s.done(tt(DT[d][:], DT[d][:], heads(tri(d)), ALU.mult), "dtm")
                            pool.wait_ge(s.sem, s.at(c, "dtm"))
                            s.done(tt(BM[d][:], DT[d][:], col(d, BETA), ALU.mult), "bm")
                        for d in range(2):
                            s = pool_s[d]
                            pool.wait_ge(dve_s[d].sem, dve_s[d].at(c, "qm"))
                            s.done(tt(U[d][:], QM[d][:], heads(level(1 - d, 0)), ALU.mult), "u1")
                            pool.wait_ge(s.sem, s.at(c, "u1"))
                            s.done(tt(U[d][:], heads(ident), U[d][:], ALU.subtract), "u")
                        for d in range(2):
                            s = pool_s[d]
                            pool.wait_ge(q[f"in{d}"], START + 16 * c + 16)
                            pool.wait_ge(act_s[d].sem, act_s[d].at(c, "rows_exp"))
                            s.done(tt(QD[d][:], IN[d][:, 0:4, :], EG[d][:], ALU.mult), "qd")
                        for d in range(2):
                            s = pool_s[d]
                            pool.wait_ge(dve_s[d].sem, dve_s[d].at(c, "vw"))
                            s.done(tt(VD[d][:], VW[d][:], col(d, ET), ALU.mult), "vt")

                @block.vector
                def _(dve):
                    for d in range(2):
                        nc.vector.memset(ST[d][:], 0.0).then_inc(q["state"], 1)
                    tt = nc.vector.tensor_tensor
                    with dve.Fori(0, NT) as c:
                        for d in range(2):
                            a, b, e = B[d]
                            s = dve_s[d]
                            dve.wait_ge(s.sem, s.at(c))
                            s.done(nc.vector.tensor_scalar(
                                COL[d][:], decay[:, :, ds(tile_of(c, d), 1), 4 * d:4 * d + 4].rearrange("p w o n -> p w (o n)"),
                                1.0, None, ALU.mult), "col")
                            dve.wait_ge(s.sem, s.at(c, "col"))
                            dve.wait_ge(pe_s[d].sem, pe_s[d].at(c, "rows"))
                            s.done(tt(DT[d][:], e, col(d, GC), ALU.subtract), "diff")
                            dve.wait_ge(s.sem, s.at(c, "diff"))
                            s.done(nc.vector.tensor_scalar(DT[d][:], DT[d][:], 0.0, None, ALU.min), "neg")
                        for d in range(2):
                            a, b, e = B[d]
                            s = dve_s[d]
                            dve.wait_ge(pool_s[d].sem, pool_s[d].at(c, "dtm"))
                            dve.wait_ge(pe_s[d].sem, pe_s[d].at(c, "qk"))
                            s.done(tt(AT[d][:], b, DT[d][:], ALU.mult), "attn")
                            dve.wait_ge(pool_s[d].sem, pool_s[d].at(c, "bm"))
                            s.done(tt(QM[d][:], a, BM[d][:], ALU.mult), "qm")
                        for d in range(2):
                            a, b, e = B[d]
                            s = dve_s[d]
                            dve.wait_ge(pe_s[d].sem, pe_s[d].at(c, "a_turned"))
                            s.done(tt(T[d][:], e, heads(level(d, 0)), ALU.mult), "t_off")
                            dve.wait_ge(s.sem, s.at(c, "t_off"))
                            s.done(tt(T[d][:], heads(ident), T[d][:], ALU.subtract), "t0")
                        for k in range(1, N_LEVELS):
                            for d in range(2):
                                a, b, e = B[d]
                                dve.wait_ge(pe_s[d].sem, pe_s[d].at(c, f"x{k}"))
                                dve_s[d].done(tt(XM[d][:], a, heads(level(d, k)), ALU.mult), f"xm{k}")
                            for d in range(2):
                                a, b, e = B[d]
                                if k < N_LEVELS - 1:
                                    dve.wait_ge(pe_s[d].sem, pe_s[d].at(c, f"tx{k}"))
                                    dve_s[d].done(tt(T[d][:], T[d][:], b, ALU.subtract), f"t{k}")
                                dve.wait_ge(pe_s[d].sem, pe_s[d].at(c, f"ux{k}"))
                                dve_s[d].done(tt(U[d][:], U[d][:], e, ALU.subtract), f"u{k}")
                        for d in range(2):
                            a, b, e = B[d]
                            dve.wait_ge(pe_s[d].sem, pe_s[d].at(c, "z"))
                            dve.wait_ge(act_s[d].sem, act_s[d].at(c, "v_tok"))
                            for h in range(4):
                                last = nc.vector.scalar_tensor_tensor(out=R[d][:, h, :], in0=a[:, h, :],
                                                                      scalar=COL[d][:, NEG, h:h + 1], in1=VT[d][:, h, :],
                                                                      op0=ALU.mult, op1=ALU.add)
                            dve_s[d].done(last, "r")
                        for d in range(2):
                            a, b, e = B[d]
                            dve.wait_ge(pe_s[d].sem, pe_s[d].at(c, "v_new"))
                            dve_s[d].done(tt(VW[d][:], b, col(d, BETA), ALU.mult), "vw")
                        for d in range(2):
                            a, b, e = B[d]
                            dve.wait_ge(pe_s[d].sem, pe_s[d].at(c, "s_add"))
                            for h in range(4):
                                last = nc.vector.scalar_tensor_tensor(out=ST[d][:, h, :], in0=ST[d][:, h, :],
                                                                      scalar=COL[d][:, EL, h:h + 1], in1=a[:, h, :],
                                                                      op0=ALU.mult, op1=ALU.add)
                            dve_s[d].done(last, "s")

        def gate_delta(l):
            with Phase("dgate", ["g_in", "in0", "in1", "summed", "squared", "total", "log", "root", "tanh", "normed",
                                 "z_gate", "g_half", "gated", "stored"]) as (block, q):
                A, Bk, Z, ZT, SQ, R, OUT = ([sb(f"dgate_{n}{s}", [P, S]) for s in range(2)]
                                            for n in ("a", "b", "z", "zt", "sq", "r", "out"))
                g_raw, g_half = small[:, 0:1], small[:, 1:2]
                flat = lambda pair: pair[:].rearrange("p a b -> p (a b)")

                @block.sync
                def _(sp):
                    sp.dma_start(g_raw, c_norm_g[ds(l, 1), :].rearrange("o p -> p o"), allow_slow_non_contiguous=True)\
                        .then_inc(q["g_in"], 16)
                    for h in range(4):
                        s = h % 2
                        if h >= 2:
                            sp.wait_ge(q["gated"], START + h - 1)
                        for dst, src in ((A[s], o_dir[0, h]), (Bk[s], o_dir[1, h]), (Z[s], proj[U_CZ + h])):
                            sp.dma_start(dst[:], src).then_inc(q[f"in{s}"], 16)
                        if h >= 1:
                            sp.wait_ge(q["gated"], START + h)
                            sp.dma_start(gated[8 + h - 1], OUT[(h - 1) % 2][:]).then_inc(q["stored"], 16)
                    sp.wait_ge(q["gated"], START + 4)
                    sp.dma_start(gated[11], OUT[1][:]).then_inc(q["stored"], 16)
                    sp.wait_ge(q["stored"], START + 64)

                @block.vector
                def _(dve):
                    dve.wait_ge(q["g_in"], START + 16)
                    nc.vector.tensor_scalar(g_half, g_raw, 0.5, None, ALU.mult).then_inc(q["g_half"], 1)
                    for h in range(4):
                        s = h % 2
                        dve.wait_ge(q[f"in{s}"], START + 48 * (h // 2 + 1))
                        nc.vector.tensor_tensor(A[s][:], A[s][:], Bk[s][:], ALU.add).then_inc(q["summed"], 1)
                        dve.wait_ge(q["tanh"], START + h + 1)
                        nc.vector.scalar_tensor_tensor(out=ZT[s][:], in0=ZT[s][:], scalar=1.0, in1=Z[s][:], op0=ALU.add,
                                                       op1=ALU.mult).then_inc(q["z_gate"], 1)
                        dve.wait_ge(q["root"], START + h + 1)
                        dve.wait_ge(q["g_half"], START + 1)
                        nc.vector.scalar_tensor_tensor(out=A[s][:], in0=A[s][:], scalar=g_half, in1=R[s][:],
                                                       op0=ALU.mult, op1=ALU.mult).then_inc(q["normed"], 1)
                        dve.wait_ge(q["normed"], START + h + 1)
                        dve.wait_ge(q["z_gate"], START + h + 1)
                        if h >= 2:
                            dve.wait_ge(q["stored"], START + 16 * (h - 1))
                        nc.vector.tensor_tensor(OUT[s][:], A[s][:], ZT[s][:], ALU.mult).then_inc(q["gated"], 1)

                @block.scalar
                def _(act):
                    for h in range(4):
                        s = h % 2
                        act.wait_ge(q[f"in{s}"], START + 48 * (h // 2 + 1))
                        if h >= 2:
                            act.wait_ge(q["gated"], START + h - 1)
                        nc.scalar.activation(ZT[s][:], Z[s][:], ACT.Tanh, scale=0.5).then_inc(q["tanh"], 1)
                        act.wait_ge(q["summed"], START + h + 1)
                        nc.scalar.activation(SQ[s][:], A[s][:], ACT.Square).then_inc(q["squared"], 1)
                        act.wait_ge(q["total"], START + h + 1)
                        root(act, R[s][:], flat(pairs[s]), P, q["log"], h + 1, q["root"])

                @block.tensor
                def _(pe):
                    for h in range(4):
                        s = h % 2
                        pe.wait_ge(q["squared"], START + h + 1)
                        for half in range(2):
                            last = nc.tensor.matmul(pairs[s][:, half, :], ones, SQ[s][:, half * HALF:(half + 1) * HALF],
                                                    start=True, stop=True)
                        last.then_inc(q["total"], 1)

        def merge(l):
            with Phase("merge", ["in", "o_hi", "o_lo", "w_in0", "w_in1", "w_hi0", "w_hi1", "w_lo0", "w_lo1", "t_in0",
                                 "t_in1", "sum0", "sum1", "out0", "out1", "added0", "added1", "m_hi", "m_lo"]) as (block, q):
                merged = sb("merged", [P, KC, S])
                branch = sb("branch", [P, 4, S])
                o_hi, o_lo = sb("branch_hi", [P, 4, S], F32R), sb("branch_lo", [P, 4, S], F32R)
                gate = [sb(f"gate{s}", [P, S]) for s in range(2)]
                w_bo = (w_bo_a, w_bo_b, w_bo_c)
                flat = lambda pair: pair[:].rearrange("p a b -> p (a b)")
                one = lambda ap: ap.rearrange("p o s -> p (o s)")

                @block.sync
                def _(sp):
                    for br in range(3):
                        sp.wait_ge(q["o_lo"], START + 4 * br)
                        sp.dma_start(branch[:], gated[4 * br:4 * br + 4].rearrange("u p s -> p u s")).then_inc(q["in"], 16)
                        w_l = w_bo[br].rearrange("l (k p) e -> l p k e", p=P)[ds(l, 1)].rearrange("o p k e -> (o p) k e")
                        with sp.Fori(4 * br, 4 * br + 4) as i:
                            for s in range(2):
                                j = 2 * i + (s - 8 * br)
                                sp.wait_ge(q[f"w_lo{s}"], START + i)
                                sp.dma_start(w_stage[s][:, 0:4, :], w_l[:, :, ds(j * P, P)]).then_inc(q[f"w_in{s}"], 16)
                                sp.wait_ge(q[f"out{s}"], START + i)
                                sp.dma_start(gate[s][:], proj[ds(2 * i + (N_PLAIN + s), 1)].rearrange("o p s -> (o p) s"))\
                                    .then_inc(q[f"t_in{s}"], 16)

                @block.gpsimd
                def _(pool):
                    with pool.Fori(0, 12) as i:
                        for s in range(2):
                            stage, hi, lo = (w[s][:, 0:4, :] for w in (w_stage, w_hi, w_lo))
                            pool.wait_ge(q[f"w_in{s}"], START + 16 * i + 16)
                            pool.wait_ge(q[f"sum{s}"], START + i)
                            nc.gpsimd.tensor_tensor(hi, stage, bcast(ones, 4), ALU.mult).then_inc(q[f"w_hi{s}"], 1)
                            pool.wait_ge(q[f"w_hi{s}"], START + i + 1)
                            nc.gpsimd.tensor_tensor(lo, stage, hi.bitcast(F32), ALU.subtract).then_inc(q[f"w_lo{s}"], 1)

                @block.tensor
                def _(pe):
                    for br in range(3):
                        pe.wait_ge(q["o_lo"], START + 4 * br + 4)
                        with pe.Fori(4 * br, 4 * br + 4) as i:
                            for s in range(2):
                                pe.wait_ge(q[f"w_lo{s}"], START + i + 1)
                                pe.wait_ge(q[f"out{s}"], START + i)
                                product(pe, pairs[s], w_hi[s], w_lo[s], o_hi, o_lo, 4).then_inc(q[f"sum{s}"], 1)

                @block.scalar
                def _(act):
                    for br in range(3):
                        act.wait_ge(q["in"], START + 16 * br + 16)
                        for s in range(2):
                            act.wait_ge(q[f"sum{s}"], START + 4 * br)
                        for k in range(4):
                            nc.scalar.activation(o_hi[:, k, :], branch[:, k, :], ACT.Copy).then_inc(q["o_hi"], 1)
                    for s in range(2):
                        act.wait_ge(q[f"added{s}"], START + 12)
                    for k in range(KC):
                        nc.scalar.activation(h_hi[:, k, :], merged[:, k, :], ACT.Copy, scale=0.5).then_inc(q["m_hi"], 1)

                @block.vector
                def _(dve):
                    for br in range(3):
                        for k in range(4):
                            dve.wait_ge(q["o_hi"], START + 4 * br + k + 1)
                            nc.vector.tensor_tensor(o_lo[:, k, :], branch[:, k, :], o_hi[:, k, :].bitcast(F32), ALU.subtract)\
                                .then_inc(q["o_lo"], 1)
                        with dve.Fori(4 * br, 4 * br + 4) as i:
                            for s in range(2):
                                j = 2 * i + (s - 8 * br)
                                dve.wait_ge(q[f"sum{s}"], START + i + 1)
                                dve.wait_ge(q[f"t_in{s}"], START + 16 * i + 16)
                                into = one(merged[:, ds(j, 1), :])
                                if br == 0:
                                    nc.vector.scalar_tensor_tensor(out=into, in0=gate[s][:], scalar=1.0, in1=flat(pairs[s]),
                                                                   op0=ALU.add, op1=ALU.mult).then_inc(q[f"out{s}"], 1)
                                    dve.wait_ge(q[f"out{s}"], START + i + 1)
                                    dve.sem_inc(q[f"added{s}"], 1)
                                else:
                                    nc.vector.scalar_tensor_tensor(out=ev[s][:], in0=gate[s][:], scalar=1.0,
                                                                   in1=flat(pairs[s]), op0=ALU.add, op1=ALU.mult)\
                                        .then_inc(q[f"out{s}"], 1)
                                    dve.wait_ge(q[f"out{s}"], START + i + 1)
                                    dve.wait_ge(q[f"added{s}"], START + i)
                                    nc.vector.tensor_tensor(into, into, ev[s][:], ALU.add).then_inc(q[f"added{s}"], 1)
                    for k in range(KC):
                        dve.wait_ge(q["m_hi"], START + k + 1)
                        nc.vector.scalar_tensor_tensor(out=h_lo[:, k, :], in0=merged[:, k, :], scalar=0.5,
                                                       in1=h_hi[:, k, :].bitcast(F32), op0=ALU.mult, op1=ALU.subtract)\
                            .then_inc(q["m_lo"], 1)

        def add_output(l):
            with Phase("wout", ["w_in0", "w_in1", "w_hi0", "w_hi1", "w_lo0", "w_lo1", "x_in0", "x_in1", "sum0", "sum1",
                                "out0", "out1", "put0", "put1"]) as (block, q):
                top[0] = after_x
                flat = lambda pair: pair[:].rearrange("p a b -> p (a b)")
                w_l = w_out.rearrange("l (k p) e -> l p k e", p=P)[ds(l, 1)].rearrange("o p k e -> (o p) k e")

                @block.sync
                def _(sp):
                    with sp.Fori(0, KC // 2) as i:
                        for s in range(2):
                            sp.wait_ge(q[f"w_lo{s}"], START + i)
                            sp.dma_start(w_stage[s][:], w_l[:, :, ds((2 * i + s) * P, P)]).then_inc(q[f"w_in{s}"], 16)
                            sp.wait_ge(q[f"out{s}"], START + i)
                            sp.dma_start(ev[s][:], resid[ds(2 * i + s, 1)].rearrange("o p s -> (o p) s"))\
                                .then_inc(q[f"x_in{s}"], 16)

                @block.gpsimd
                def _(pool):
                    with pool.Fori(0, KC // 2) as i:
                        for s in range(2):
                            pool.wait_ge(q[f"w_in{s}"], START + 16 * i + 16)
                            pool.wait_ge(q[f"sum{s}"], START + i)
                            nc.gpsimd.tensor_tensor(w_hi[s][:], w_stage[s][:], bcast(ones, KC), ALU.mult)\
                                .then_inc(q[f"w_hi{s}"], 1)
                            pool.wait_ge(q[f"w_hi{s}"], START + i + 1)
                            nc.gpsimd.tensor_tensor(w_lo[s][:], w_stage[s][:], w_hi[s][:].bitcast(F32), ALU.subtract)\
                                .then_inc(q[f"w_lo{s}"], 1)

                @block.tensor
                def _(pe):
                    with pe.Fori(0, KC // 2) as i:
                        for s in range(2):
                            pe.wait_ge(q[f"w_lo{s}"], START + i + 1)
                            pe.wait_ge(q[f"out{s}"], START + i)
                            product(pe, pairs[s], w_hi[s], w_lo[s], h_hi, h_lo, KC).then_inc(q[f"sum{s}"], 1)

                @block.vector
                def _(dve):
                    with dve.Fori(0, KC // 2) as i:
                        for s in range(2):
                            dve.wait_ge(q[f"sum{s}"], START + i + 1)
                            dve.wait_ge(q[f"x_in{s}"], START + 16 * i + 16)
                            nc.vector.tensor_tensor(xT[:, ds(2 * i + s, 1), :].rearrange("p o s -> p (o s)"),
                                                    ev[s][:], flat(pairs[s]), ALU.add).then_inc(q[f"out{s}"], 1)

                @block.scalar
                def _(act):
                    with act.Fori(0, KC // 2) as i:
                        for s in range(2):
                            act.wait_ge(q[f"out{s}"], START + i + 1)
                            act.dma_start(resid[ds(2 * i + s, 1)].rearrange("o p s -> (o p) s"),
                                          xT[:, ds(2 * i + s, 1), :].rearrange("p o s -> p (o s)"))\
                                .then_inc(q[f"put{s}"], 16)
                    for s in range(2):
                        act.wait_ge(q[f"put{s}"], START + 16 * (KC // 2))

        load_x()
        layers = nc.Fori(0, DEPTH)
        with layers as l:
            norm(l)
            if "G" in phases:
                project(l)
            if "A" in phases:
                attend_window(l)
            if "B" in phases:
                attend_full(l)
            if "C" in phases:
                convolve(l)
            if "c" in phases:
                delta_rule(l)
                gate_delta(l)
            if "M" in phases:
                merge(l)
            if "O" in phases:
                add_output(l)
        if "O" in phases:
            norm(0, final=True)


_INS = ["x", "norm_g", "w_in", "a_sink", "b_lambda", "b_subln_g", "c_conv_w", "c_a_log", "c_dt_bias", "c_norm_g",
        "w_bo_a", "w_bo_b", "w_bo_c", "w_out", "final_g"]


def constants():
    import numpy as np
    inv = (1.0 / (np.float32(10000.0) ** (np.arange(0, HD, 2, dtype=np.float32) / np.float32(HD)))).astype(np.float32)
    ang = (np.arange(S, dtype=np.float32)[None, :] * inv[:, None]).astype(np.float32)
    cos, sin = np.cos(ang), np.sin(ang)
    cos_t = np.tile(cos, (4, 1)).astype(np.float32)
    sin_t = np.concatenate([-sin, sin, -sin, sin], 0).astype(np.float32)
    r = np.arange(P)
    m = np.zeros((P, 2 * N_LEVELS + 4, P), np.float32)
    for k in range(N_LEVELS):
        b = 1 << k
        low = (r[:, None] // (2 * b) == r[None, :] // (2 * b)) & (r[:, None] // b % 2 == 1) & (r[None, :] // b % 2 == 0)
        m[:, k] = low
        m[:, N_LEVELS + k] = low.T
    m[:, 2 * N_LEVELS] = r[:, None] <= r[None, :]
    m[:, 2 * N_LEVELS + 1] = r[:, None] >= r[None, :]
    m[:, 2 * N_LEVELS + 2] = np.eye(P)
    m[:, 2 * N_LEVELS + 3] = 1.0
    kpos = np.arange(3 * P)[None, :] - P
    band = np.where(np.abs(kpos - r[:, None]) <= P, 0.0, -1e30).astype(np.float32)
    lam = np.zeros((P, DEPTH, 2), np.float32)
    for l in range(DEPTH):
        lam[:, l, 0] = 0.8 - 0.6 * math.exp(-0.3 * l)
        lam[:, l, 1] = 0.5 * (1.0 - lam[0, l, 0])
    return {"cos_t": cos_t, "sin_t": sin_t, "masks_t": m, "band_t": band, "lam_t": lam}


def kernel(**inputs):
    import numpy as _np
    import concourse.bacc as _bacc
    from concourse.bass_utils import run_bass_kernel_spmd as _run

    nc = _bacc.Bacc("TRN2", target_bir_lowering=False, num_devices=1)
    arrays, args = {}, []
    for name, a in {**{n: inputs[n] for n in _INS}, **constants()}.items():
        a = _np.ascontiguousarray(a)
        arrays[f"in_{name}"] = a
        args.append(nc.dram_tensor(f"in_{name}", a.shape, mybir.dt.from_np(a.dtype), kind="ExternalInput").ap())
    args.append(nc.dram_tensor("out_x", (1, S, D), F32, kind="ExternalOutput").ap())
    build_program(nc, *args)
    r = _run(nc, [arrays], core_ids=[0])
    return r.results[0]["out_x"]
```

```python
import math
from contextlib import ExitStack

import concourse.bass as bass
from concourse import mybir
from concourse.alu_op_type import AluOpType as ALU

ACT = mybir.ActivationFunctionType
F32 = mybir.dt.float32
F32R = mybir.dt.float32r
AX_X = mybir.AxisListType.X
ds = bass.ds

P = 128
S = 1024
D = 1024
DEPTH = 2
NT = S // P
KC = D // P
HD = 64
EPS = 1e-6
SCALE = HD ** -0.5
HALF = 512
START = 1

U_AQ, U_AK, U_AV, U_AZ = 0, 4, 5, 6
U_BQ, U_BK, U_BV, U_BZ = 10, 14, 18, 22
U_C, U_CZ = 26, 38
N_PLAIN = 42
N_BA = 16
N_GATE = 24
COL_BA = N_PLAIN * P
COL_GATE = COL_BA + N_BA
N_LEVELS = 7


class Steps:

    def __init__(self, sem, names):
        self.sem, self.names, self.next = sem, names, 0

    def at(self, turn, name=None):
        n = len(self.names)
        return START + (turn * n if name is None else turn * n + self.names.index(name) + 1)

    def done(self, instruction, name):
        assert self.names[self.next % len(self.names)] == name, (name, self.names[self.next % len(self.names)])
        self.next += 1
        instruction.then_inc(self.sem, 1)


def bcast(ap, n):
    return ap.unsqueeze(1).to_broadcast([P, n, ap.shape[1]])


def cols(ap, w):
    return ap.unsqueeze(2).to_broadcast([P, ap.shape[1], w])


def build_program(nc, x, norm_g, w_in, a_sink, b_lambda, b_subln_g, c_conv_w, c_a_log, c_dt_bias, c_norm_g,
                  w_bo_a, w_bo_b, w_bo_c, w_out, final_g, cos_t, sin_t, masks_t, band_t, lam_t, out,
                  scratch_kind="Internal", phases="NGABCcMO"):
    proj = nc.dram_tensor("proj", [N_PLAIN + N_GATE, P, S], F32, kind=scratch_kind).ap()
    conv = nc.dram_tensor("conv", [13, P, S], F32, kind=scratch_kind).ap()[1:13]
    gated = nc.dram_tensor("gated", [12, P, S], F32, kind=scratch_kind).ap()
    o_dir = nc.dram_tensor("o_dir", [2, 4, P, S], F32, kind=scratch_kind).ap()
    resid = nc.dram_tensor("resid", [KC, P, S], F32, kind=scratch_kind).ap()

    top = [nc.sbuf_base + (-nc.sbuf_base) % 64]

    def sb(name, shape, dt=F32):
        size = 4
        for n in shape[1:]:
            size *= n
        t = nc.alloc_sbuf_tensor_at(name, list(shape), dt, offset=top[0])
        top[0] += size + (-size) % 32
        return t

    h_start = top[0]
    h_hi = sb("h_hi", [P, KC, S], F32R)
    h_lo = sb("h_lo", [P, KC, S], F32R)
    cos = sb("cos", [P, S])
    sin = sb("sin", [P, S])
    masks = sb("masks", [P, 2 * N_LEVELS + 4, P])
    band = sb("band", [P, 3 * P])
    ba = sb("ba", [P, NT, N_BA])
    decay = sb("decay", [P, 6, NT, 8])
    small = sb("small", [P, 128])
    eps = small[:, 127:128]
    w_stage = [sb(f"w_stage{s}", [P, KC, P]) for s in range(2)]
    w_hi = [sb(f"w_hi{s}", [P, KC, P], F32R) for s in range(2)]
    w_lo = [sb(f"w_lo{s}", [P, KC, P], F32R) for s in range(2)]
    ev = [sb(f"ev{s}", [P, S]) for s in range(2)]
    work = top[0]
    xT = nc.alloc_sbuf_tensor_at("xT", [P, KC, S], F32, offset=work)
    x_sq = nc.alloc_sbuf_tensor_at("x_sq", [P, S], F32, offset=work + KC * S * 4)
    after_x = work + (KC + 1) * S * 4
    level = lambda d, k: masks[:, d * N_LEVELS + k, :]
    tri = lambda d: masks[:, 2 * N_LEVELS + d, :]
    ident = masks[:, 2 * N_LEVELS + 2, :]
    ones = masks[:, 2 * N_LEVELS + 3, :]

    stack = ExitStack()
    with stack:
        pairs = [stack.enter_context(nc.psum_tensor(f"pair{i}", [P, 2, HALF], F32)) for i in range(4)]
        bank = lambda b: pairs[b // 2][:, b % 2, :]

        class Phase:

            def __init__(self, name, sems, ahead={}):
                self.name, self.names, self.ahead = name, sems, ahead

            def __enter__(self):
                top[0] = work
                self.scope = ExitStack()
                self.sems = {n: self.scope.enter_context(nc.semaphore(f"{self.name}_{n}")) for n in self.names}
                for n, sem in self.sems.items():
                    nc.sync.sem_inc(sem, START + self.ahead.get(n, 0))
                nc.all_engine_barrier(sem_only=True)
                self.inner = nc.Block()
                return self.inner.__enter__(), self.sems

            def __exit__(self, *a):
                assert top[0] <= nc.sbuf_top, (self.name, top[0], nc.sbuf_top)
                self.inner.__exit__(*a)
                if a[0] is None:
                    nums = [s.num for s in self.sems.values()]
                    nc.sync.sem_clear(range(min(nums), max(nums) + 1))
                self.scope.close()

        def product(pe, pair, hi, lo, rhs_hi, rhs_lo, kc, m=P, ready=None):
            for k in range(kc):
                if ready:
                    ready(k)
                for n, (lhs, rhs) in enumerate(((hi, rhs_hi), (hi, rhs_lo), (lo, rhs_hi))):
                    for half in range(2):
                        last = nc.tensor.matmul(pair[0:m, half, :], lhs[:, k, 0:m],
                                                rhs[:, k, half * HALF:(half + 1) * HALF],
                                                start=(k == 0 and n == 0), stop=(k == kc - 1 and n == 2))
            return last

        class Side:

            AHEAD = {"side_in0": 16, "side_in1": 16, "side_hi": 2, "side_lo": 2}

            SEMS = ["side_in0", "side_in1", "side_hi", "side_lo", "side_sum", "side_out", "side_put0", "side_put1"]

            def __init__(self, l, q, per):
                self.q, self.per = q, per
                self.in_slot = [(per + 1 - s) // 2 for s in range(2)]
                self.w = w_in.rearrange("l (k p) e -> l p k e", p=P)[ds(l, 1)].rearrange("o p k e -> (o p) k e")

            def load(self, sp, turn, k, column, ahead=False):
                sp.wait_ge(self.q["side_lo"], START + turn * self.per + (k - 1 if ahead else max(k - 1, 0)))
                sp.dma_start(w_stage[k % 2][:], self.w[:, :, ds(column, P)]).then_inc(self.q[f"side_in{k % 2}"], 16)

            def split(self, pool, turn, k, ahead=False):
                q, s = self.q, k % 2
                pool.wait_ge(q["side_sum"], START + turn * (2 * self.per) + (2 * k - 2 if ahead else max(2 * k - 2, 0)))
                pool.wait_ge(q[f"side_in{s}"], START + turn * (16 * self.in_slot[s]) + (16 * (k // 2) + 16))
                nc.gpsimd.tensor_tensor(w_hi[s][:], w_stage[s][:], bcast(ones, KC), ALU.mult).then_inc(q["side_hi"], 1)
                pool.wait_ge(q["side_hi"], START + turn * self.per + (k + 1))
                nc.gpsimd.tensor_tensor(w_lo[s][:], w_stage[s][:], w_hi[s][:].bitcast(F32), ALU.subtract)\
                    .then_inc(q["side_lo"], 1)

            def part(self, pe, turn, k, half, c):
                q, s = self.q, k % 2
                if half == 0 and c == 0:
                    pe.wait_ge(q["side_lo"], START + turn * self.per + (k + 1))
                if c == 0:
                    pe.wait_ge(q["side_out"], START + turn * (2 * self.per) + (2 * k + half))
                w = slice(half * HALF, (half + 1) * HALF)
                for n, (a, b) in enumerate(((w_hi, h_hi), (w_hi, h_lo), (w_lo, h_hi))):
                    last = nc.tensor.matmul(bank(7), a[s][:, c, :], b[:, c, w], start=(c == 0 and n == 0),
                                            stop=(c == KC - 1 and n == 2))
                if c == KC - 1:
                    last.then_inc(q["side_sum"], 1)

            def half(self, pe, turn, k, half):
                for c in range(KC):
                    self.part(pe, turn, k, half, c)

            def out(self, act, turn, k, half, unit, gate=False):
                q, s = self.q, k % 2
                if half == 0:
                    act.wait_ge(q[f"side_put{s}"], START + turn * (16 * self.in_slot[s]) + 16 * (k // 2))
                act.wait_ge(q["side_sum"], START + turn * (2 * self.per) + (2 * k + half + 1))
                nc.scalar.activation(ev[s][:, half * HALF:(half + 1) * HALF], bank(7), ACT.Tanh if gate else ACT.Copy,
                                     scale=0.5 if gate else 1.0).then_inc(q["side_out"], 1)
                if half == 1:
                    act.wait_ge(q["side_out"], START + turn * (2 * self.per) + (2 * k + 2))
                    act.dma_start(proj[ds(unit, 1)].rearrange("o p s -> (o p) s"), ev[s][:])\
                        .then_inc(q[f"side_put{s}"], 16)

            def finish(self, act, turns):
                for s in range(2):
                    if self.in_slot[s]:
                        act.wait_ge(self.q[f"side_put{s}"], START + 16 * self.in_slot[s] * turns)

        def load_x():
            with Phase("load", ["const", "eps", "x_in", "turned", "copied", "squared", "summed", "x_sq",
                                "stored"]) as (block, q):
                top[0] = after_x
                xin = [sb(f"load_x{s}", [P, D]) for s in range(2)]
                sq = [sb(f"load_sq{s}", [P, 4, P]) for s in range(2)]
                part = [sb(f"load_part{s}", [P, P]) for s in range(2)]

                @block.sync
                def _(sp):
                    def store(t):
                        w = slice(t * P, (t + 1) * P)
                        sp.wait_ge(q["copied"], START + 2 * t + 2)
                        sp.dma_start(resid.rearrange("k p s -> p k s")[:, :, w], xT[:, :, w]).then_inc(q["stored"], 16)

                    sp.dma_start(masks[:], masks_t).then_inc(q["const"], 16)
                    sp.dma_start(cos[:], cos_t).then_inc(q["const"], 16)
                    sp.dma_start(sin[:], sin_t).then_inc(q["const"], 16)
                    sp.dma_start(band[:], band_t).then_inc(q["const"], 16)
                    for t in range(NT):
                        if t >= 2:
                            sp.wait_ge(q["turned"], START + 2 * (t - 1))
                        if t >= 1:
                            sp.wait_ge(q["x_in"], START + 16 * t)
                        sp.dma_start(xin[t % 2][:], x[0, t * P:(t + 1) * P, :]).then_inc(q["x_in"], 16)
                        if t >= 2:
                            store(t - 2)
                    store(NT - 2)
                    store(NT - 1)
                    sp.wait_ge(q["stored"], START + 16 * NT)
                    sp.wait_ge(q["const"], START + 64)

                @block.tensor
                def _(pe):
                    pe.wait_ge(q["const"], START + 64)
                    for t in range(NT):
                        pe.wait_ge(q["x_in"], START + 16 * (t + 1))
                        for half in range(2):
                            n = 2 * t + half
                            if n >= 8:
                                pe.wait_ge(q["copied"], START + n - 7)
                            for k in range(4):
                                c = (4 * half + k) * P
                                last = nc.tensor.transpose(bank(n % 8)[:, k * P:(k + 1) * P], xin[t % 2][:, c:c + P],
                                                           ident)
                            last.then_inc(q["turned"], 1)

                @block.scalar
                def _(act):
                    for n in range(2 * NT):
                        act.wait_ge(q["copied"], START + n + 1)
                        if n >= 2:
                            act.wait_ge(q["summed"], START + n - 1)
                        t, half = n // 2, n % 2
                        nc.scalar.activation(sq[half][:], xT[:, 4 * half:4 * half + 4, t * P:(t + 1) * P], ACT.Square)\
                            .then_inc(q["squared"], 1)

                @block.vector
                def _(dve):
                    nc.vector.memset(eps, EPS).then_inc(q["eps"], 1)
                    for t in range(NT):
                        for half in range(2):
                            n = 2 * t + half
                            dve.wait_ge(q["turned"], START + n + 1)
                            nc.vector.tensor_copy(xT[:, 4 * half:4 * half + 4, t * P:(t + 1) * P],
                                                  bank(n % 8).rearrange("p (k s) -> p k s", k=4)).then_inc(q["copied"], 1)
                            dve.wait_ge(q["squared"], START + n + 1)
                            if t:
                                dve.wait_ge(q["x_sq"], START + t)
                            nc.vector.tensor_reduce(part[half][:], sq[half][:].rearrange("p k s -> p s k"), AX_X, ALU.add)\
                                .then_inc(q["summed"], 1)
                        dve.wait_ge(q["summed"], START + 2 * t + 2)
                        nc.vector.tensor_tensor(x_sq[:, t * P:(t + 1) * P], part[0][:], part[1][:], ALU.add)\
                            .then_inc(q["x_sq"], 1)

        sums = pairs[3][:].rearrange("p a b -> p (a b)")

        def total_squares(pe):
            for half in range(2):
                last = nc.tensor.matmul(pairs[3][:, half, :], ones, x_sq[:, half * HALF:(half + 1) * HALF],
                                        start=True, stop=True)
            return last

        def root(act, out_, total, n, log_done, turn, root_done, bias=None):
            nc.scalar.activation(out_, total, ACT.Ln, bias=eps if bias is None else bias, scale=1.0 / n)\
                .then_inc(log_done, 1)
            act.wait_ge(log_done, START + turn)
            nc.scalar.activation(out_, out_, ACT.Exp, scale=-0.5).then_inc(root_done, 1)

        def final_norm():
            with Phase("fin", ["g_in", "total", "log", "root", "scaled", "turned", "copied0", "copied1",
                               "stored"]) as (block, q):
                top[0] = after_x
                rstd = sb("fin_rstd", [P, S])
                fin_o = [sb(f"fin_o{s}", [P, D]) for s in range(2)]
                g = small[:, 0:KC]

                @block.sync
                def _(sp):
                    sp.dma_start(g, final_g.rearrange("(k p) -> p k", p=P), allow_slow_non_contiguous=True)\
                        .then_inc(q["g_in"], 16)
                    for t in range(NT):
                        for half in range(2):
                            sp.wait_ge(q[f"copied{half}"], START + t + 1)
                        if t:
                            sp.wait_ge(q["stored"], START + 16 * t)
                        sp.dma_start(out[0, t * P:(t + 1) * P, :], fin_o[t % 2][:]).then_inc(q["stored"], 16)
                    sp.wait_ge(q["stored"], START + 16 * NT)

                @block.tensor
                def _(pe):
                    total_squares(pe).then_inc(q["total"], 1)
                    for t in range(NT):
                        pe.wait_ge(q["scaled"], START + KC)
                        for half in range(2):
                            n = 2 * t + half
                            if n >= 4:
                                pe.wait_ge(q[f"copied{half}"], START + t - 1)
                            for k in range(4):
                                last = nc.tensor.transpose(bank(2 + n % 4)[:, k * P:(k + 1) * P],
                                                           xT[:, 4 * half + k, t * P:(t + 1) * P], ident)
                            last.then_inc(q["turned"], 1)

                @block.scalar
                def _(act):
                    act.wait_ge(q["total"], START + 1)
                    root(act, rstd[:], sums, D, q["log"], 1, q["root"])
                    for t in range(NT):
                        if t >= 2:
                            act.wait_ge(q["stored"], START + 16 * (t - 1))
                        n = 2 * t + 1
                        act.wait_ge(q["turned"], START + n + 1)
                        nc.scalar.activation(fin_o[t % 2][:, HALF:D], bank(2 + n % 4), ACT.Copy).then_inc(q["copied1"], 1)

                @block.vector
                def _(dve):
                    dve.wait_ge(q["g_in"], START + 16)
                    dve.wait_ge(q["root"], START + 1)
                    for k in range(KC):
                        nc.vector.scalar_tensor_tensor(out=xT[:, k, :], in0=xT[:, k, :], scalar=g[:, k:k + 1], in1=rstd[:],
                                                       op0=ALU.mult, op1=ALU.mult).then_inc(q["scaled"], 1)
                    for t in range(NT):
                        if t >= 2:
                            dve.wait_ge(q["stored"], START + 16 * (t - 1))
                        n = 2 * t
                        dve.wait_ge(q["turned"], START + n + 1)
                        nc.vector.tensor_copy(fin_o[t % 2][:, 0:HALF], bank(2 + n % 4)).then_inc(q["copied0"], 1)

        def project(l):
            w_l = w_in.rearrange("l (k p) e -> l p k e", p=P)[ds(l, 1)].rearrange("o p k e -> (o p) k e")
            with Phase("proj", ["w_in0", "w_in1", "w_hi0", "w_hi1", "w_lo0", "w_lo1", "sum0", "sum1",
                                "out0", "out1", "put0", "put1", "ba_in", "ba_hi", "ba_lo", "ba_sum", "ba_out",
                                "g_in", "total", "log", "root", "scaled", "hi", "lo0", "lo1",
                                "par_in", "pre", "pre_act", "sums"]) as (block, q):
                top[0] = after_x
                hf = [sb(f"norm_h{n}", [P, S]) for n in range(4)]
                rstd = sb("norm_rstd", [P, S])
                g = small[:, 0:KC]
                ba_w = sb("ba_w", [P, KC, N_BA])
                ba_hi = sb("ba_hi", [P, KC, N_BA], F32R)
                ba_lo = sb("ba_lo", [P, KC, N_BA], F32R)
                par = sb("decay_par", [P, 2, 8])
                tmp = sb("decay_tmp", [P, 4, NT, 8])
                a_log, dt = par[:, 0, :], par[:, 1, :]
                t0, t1, t2, t3 = (tmp[:, n] for n in range(4))
                pairs_of_units = U_BQ // 2

                @block.sync
                def _(sp):
                    sp.dma_start(g, norm_g.rearrange("l (k p) -> p l k", p=P)[:, ds(l, 1), :].rearrange("p o k -> p (o k)"),
                                 allow_slow_non_contiguous=True).then_inc(q["g_in"], 16)
                    for s in range(2):
                        sp.dma_start(w_stage[s][:], w_l[:, :, s * P:(s + 1) * P]).then_inc(q[f"w_in{s}"], 16)
                    sp.dma_start(ba_w[:], w_l[:, :, COL_BA:COL_BA + N_BA]).then_inc(q["ba_in"], 16)
                    for n, src in enumerate((c_a_log, c_dt_bias)):
                        sp.dma_start(par[:, n, :], src[ds(l, 1)].rearrange("o d h -> (o d h)").partition_broadcast(P))\
                            .then_inc(q["par_in"], 16)
                    with sp.Fori(1, pairs_of_units + 1) as i:
                        for s in range(2):
                            sp.wait_ge(q[f"w_lo{s}"], START + i)
                            sp.dma_start(w_stage[s][:], w_l[:, :, ds((2 * i + s) * P, P)]).then_inc(q[f"w_in{s}"], 16)

                @block.gpsimd
                def _(pool):
                    def split(i, s):
                        pool.wait_ge(q[f"w_in{s}"], START + 16 * i + 16)
                        pool.wait_ge(q[f"sum{s}"], START + i)
                        nc.gpsimd.tensor_tensor(w_hi[s][:], w_stage[s][:], bcast(ones, KC), ALU.mult)\
                            .then_inc(q[f"w_hi{s}"], 1)
                        pool.wait_ge(q[f"w_hi{s}"], START + i + 1)
                        nc.gpsimd.tensor_tensor(w_lo[s][:], w_stage[s][:], w_hi[s][:].bitcast(F32), ALU.subtract)\
                            .then_inc(q[f"w_lo{s}"], 1)

                    for s in range(2):
                        split(0, s)
                    for k in range(1, KC, 2):
                        pool.wait_ge(q["hi"], START + k + 1)
                        nc.gpsimd.tensor_tensor(h_lo[:, k, :], hf[k % 4][:], h_hi[:, k, :].bitcast(F32), ALU.subtract)\
                            .then_inc(q["lo1"], 1)
                    with pool.Fori(1, pairs_of_units + 1) as i:
                        for s in range(2):
                            split(i, s)

                @block.tensor
                def _(pe):
                    total_squares(pe).then_inc(q["total"], 1)

                    def units(i):
                        for s in range(2):
                            pe.wait_ge(q[f"w_lo{s}"], START + i + 1)
                            pe.wait_ge(q[f"out{s}"], START + i)
                            product(pe, pairs[s], w_hi[s], w_lo[s], h_hi, h_lo, KC,
                                    ready=lambda k: pe.wait_ge(q[f"lo{k % 2}"], START + k // 2 + 1))\
                                .then_inc(q[f"sum{s}"], 1)

                    units(0)
                    pe.wait_ge(q["ba_lo"], START + 1)
                    for t in range(NT):
                        for k in range(KC):
                            for n, (lhs, rhs) in enumerate(((h_hi, ba_hi), (h_hi, ba_lo), (h_lo, ba_hi))):
                                last = nc.tensor.matmul(bank(4)[:, t * N_BA:(t + 1) * N_BA], lhs[:, k, t * P:(t + 1) * P],
                                                        rhs[:, k, :], start=(k == 0 and n == 0),
                                                        stop=(k == KC - 1 and n == 2))
                    last.then_inc(q["ba_sum"], 1)
                    with pe.Fori(1, pairs_of_units) as i:
                        units(i)
                    pe.wait_ge(q["pre"], START + 7)
                    for d in range(2):
                        last = nc.tensor.matmul(bank(4 + d)[:, 0:4 * NT], tri(d), decay[:, 0, :, 4 * d:4 * d + 4],
                                                start=True, stop=True)
                    nc.tensor.matmul(bank(6)[:, 0:8 * NT], ones, decay[:, 0].rearrange("p t n -> p (t n)"),
                                     start=True, stop=True).then_inc(q["sums"], 1)

                @block.scalar
                def _(act):
                    act.wait_ge(q["total"], START + 1)
                    root(act, rstd[:], sums, D, q["log"], 1, q["root"])
                    for k in range(KC):
                        act.wait_ge(q["scaled"], START + k + 1)
                        nc.scalar.activation(h_hi[:, k, :], hf[k % 4][:], ACT.Copy).then_inc(q["hi"], 1)
                    def outs(i):
                        for s in range(2):
                            act.wait_ge(q[f"sum{s}"], START + i + 1)
                            act.wait_ge(q[f"put{s}"], START + 16 * i)
                            nc.scalar.activation(ev[s][:], pairs[s][:].rearrange("p a b -> p (a b)"), ACT.Copy)\
                                .then_inc(q[f"out{s}"], 1)
                            act.wait_ge(q[f"out{s}"], START + i + 1)
                            act.dma_start(proj[ds(2 * i + s, 1)].rearrange("o p s -> (o p) s"), ev[s][:])\
                                .then_inc(q[f"put{s}"], 16)

                    outs(0)
                    act.wait_ge(q["ba_out"], START + 1)
                    act.wait_ge(q["pre"], START + 3)
                    nc.scalar.activation(t1, t1, ACT.Exp).then_inc(q["pre_act"], 1)
                    nc.scalar.activation(a_log, a_log, ACT.Exp).then_inc(q["pre_act"], 1)
                    nc.scalar.activation(t2, ba[:, :, 0:8], ACT.Exp, scale=-1.0).then_inc(q["pre_act"], 1)
                    act.wait_ge(q["pre_act"], START + 3)
                    nc.scalar.activation(t1, t1, ACT.Ln, bias=ones[:, 0:1]).then_inc(q["pre_act"], 1)
                    with act.Fori(1, pairs_of_units) as i:
                        outs(i)
                    act.wait_ge(q["pre"], START + 10)
                    nc.scalar.activation(decay[:, 3], decay[:, 2], ACT.Exp).then_inc(q["pre_act"], 1)
                    nc.scalar.activation(decay[:, 4], t3, ACT.Exp).then_inc(q["pre_act"], 1)
                    nc.scalar.activation(decay[:, 5], t0, ACT.Exp).then_inc(q["pre_act"], 1)
                    for s in range(2):
                        act.wait_ge(q[f"put{s}"], START + 16 * pairs_of_units)

                @block.vector
                def _(dve):
                    def low(k):
                        dve.wait_ge(q["hi"], START + k + 1)
                        nc.vector.tensor_tensor(h_lo[:, k, :], hf[k % 4][:], h_hi[:, k, :].bitcast(F32), ALU.subtract)\
                            .then_inc(q["lo0"], 1)

                    dve.wait_ge(q["g_in"], START + 16)
                    dve.wait_ge(q["root"], START + 1)
                    for k in range(KC):
                        if k >= 4:
                            dve.wait_ge(q[f"lo{k % 2}"], START + k // 2 - 1)
                        nc.vector.scalar_tensor_tensor(out=hf[k % 4][:], in0=xT[:, k, :], scalar=g[:, k:k + 1],
                                                       in1=rstd[:], op0=ALU.mult, op1=ALU.mult).then_inc(q["scaled"], 1)
                        if k % 2:
                            low(k - 1)
                    dve.wait_ge(q["ba_in"], START + 16)
                    nc.vector.tensor_copy(ba_hi[:], ba_w[:]).then_inc(q["ba_hi"], 1)
                    dve.wait_ge(q["ba_hi"], START + 1)
                    nc.vector.tensor_tensor(ba_lo[:], ba_w[:], ba_hi[:].bitcast(F32), ALU.subtract).then_inc(q["ba_lo"], 1)
                    dve.wait_ge(q["ba_sum"], START + 1)
                    nc.vector.tensor_copy(ba[:].rearrange("p t n -> p (t n)"), bank(4)[:, 0:NT * N_BA]).then_inc(q["ba_out"], 1)
                    dve.wait_ge(q["ba_out"], START + 1)
                    done = [0]

                    def pre(ins):
                        done[0] += 1
                        ins.then_inc(q["pre"], 1)
                        dve.wait_ge(q["pre"], START + done[0])

                    by_head = lambda a: a.unsqueeze(1).to_broadcast([P, NT, 8])
                    dve.wait_ge(q["par_in"], START + 32)
                    pre(nc.vector.tensor_tensor(t0, ba[:, :, 8:16], by_head(dt), ALU.add))
                    pre(nc.vector.scalar_tensor_tensor(out=t1, in0=t0, scalar=-1.0, in1=t0, op0=ALU.mult, op1=ALU.min))
                    pre(nc.vector.tensor_scalar(t0, t0, 0.0, None, ALU.max))
                    dve.wait_ge(q["pre_act"], START + 4)
                    pre(nc.vector.tensor_tensor(t0, t0, t1, ALU.add))
                    pre(nc.vector.scalar_tensor_tensor(out=decay[:, 0], in0=t0, scalar=-1.0, in1=by_head(a_log),
                                                       op0=ALU.mult, op1=ALU.mult))
                    pre(nc.vector.tensor_scalar(t2, t2, 1.0, None, ALU.add))
                    pre(nc.vector.reciprocal(decay[:, 1], t2))
                    dve.wait_ge(q["sums"], START + 1)
                    for d in range(2):
                        last = nc.vector.tensor_copy(decay[:, 2, :, 4 * d:4 * d + 4],
                                                     bank(4 + d)[:, 0:4 * NT].rearrange("p (t n) -> p t n", n=4))
                    pre(last)
                    pre(nc.vector.tensor_copy(t3, bank(6)[:, 0:8 * NT].rearrange("p (t n) -> p t n", n=8)))
                    pre(nc.vector.tensor_tensor(t0, t3, decay[:, 2], ALU.subtract))
                    dve.wait_ge(q["pre_act"], START + 7)
                    pre(nc.vector.tensor_scalar(decay[:, 3], decay[:, 3], -1.0, None, ALU.mult))


        def attend_window(l):
            with Phase("win", ["sink_in", "sink", "neg_sink", "pads", "x_in", "cosined", "sined", "rotated", "hi", "lo",
                               "v_in", "v_turned", "v_hi", "v_lo", "z_in", "tanh", "z_gate", "scored", "masked",
                               "rowmax", "negmax", "shifted", "exped", "denom", "recip", "probs", "turned", "p_hi",
                               "p_lo", "summed", "gated", "stored"] + Side.SEMS, Side.AHEAD) as (block, q):
                X = sb("win_x", [P, S])
                XR = sb("win_xr", [P, S])
                VX = sb("win_vx", [P, S])
                k_hi, k_lo = sb("win_k_hi", [P, S], F32R), sb("win_k_lo", [P, S], F32R)
                q_hi = [sb(f"win_q_hi{s}", [P, S], F32R) for s in range(2)]
                q_lo = [sb(f"win_q_lo{s}", [P, S], F32R) for s in range(2)]
                v_hi, v_lo = sb("win_v_hi", [P, NT, 3 * HD], F32R), sb("win_v_lo", [P, NT, 3 * HD], F32R)
                ZX = sb("win_zx", [P, S])
                ZT = [sb(f"win_zt{s}", [P, S]) for s in range(2)]
                O = ZT
                SM = [sb(f"win_s{s}", [P, 2, 3 * P]) for s in range(2)]
                PR = [sb(f"win_p{s}", [P, 2, 3 * P]) for s in range(2)]
                p_hi = [sb(f"win_p_hi{s}", [P, 2, 3 * P], F32R) for s in range(2)]
                p_lo = [sb(f"win_p_lo{s}", [P, 2, 3 * P], F32R) for s in range(2)]
                stat = [sb(f"win_stat{s}", [P, 7, 2]) for s in range(2)]
                v_turned = pairs[0][:].rearrange("p a (t d) -> p (a t) d", d=P)[:, :, 0:HD]
                side = Side(l, q, 8)
                side_unit = lambda g, k: g * 8 + (U_BQ + k)
                side_column = lambda g, k: (side_unit(g, k) if g < 2 else diff_unit(0, k)) * P + \
                    (N_BA if g == 2 and k == 0 else 0)
                NM = 2 * NT
                EARLY = 4
                side_steps = [t for t in range(NM) if t % 4 < 3]
                sinks = small[:, 0:8]
                sink, neg_sink = small[:, 8:12], small[:, 12:16]

                def window(m):
                    i = m % NT
                    lo, hi = max(i - 1, 0), min(i + 1, NT - 1)
                    return i, lo, hi - lo + 1, (lo - i + 1) * P

                @block.sync
                def _(sp):
                    sp.dma_start(sinks, a_sink[ds(l, 1), :].rearrange("o h -> (o h)").partition_broadcast(P))\
                        .then_inc(q["sink_in"], 16)

                    def load_rotated(rows, n):
                        sp.wait_ge(q["lo"], START + n)
                        for d0, r0, src in rows:
                            sp.dma_start(X[d0:d0 + HD, :], src(r0, HD)).then_inc(q["x_in"], 16)
                            for a in range(2):
                                sp.dma_start(XR[d0 + 32 * a:d0 + 32 * a + 32, :], src(r0 + 32 * (1 - a), 32))\
                                    .then_inc(q["x_in"], 16)

                    for g in range(2):
                        weights = lambda k: side.load(sp, g, k, side_column(g, k))
                        k_src = lambda r, n: proj[U_AK, ds(g * HD + r, n), :]
                        load_rotated([(0, 0, k_src), (HD, 0, k_src)], 3 * g)
                        sp.wait_ge(q["v_turned"], START + g)
                        for h in range(2):
                            sp.dma_start(VX[h * HD:(h + 1) * HD, :], proj[U_AV, ds(g * HD, HD), :]).then_inc(q["v_in"], 16)
                        for uu in range(2):
                            unit = ds(2 * g + uu, 1)
                            q_src = lambda r, n: proj[unit, r:r + n, :].rearrange("o p s -> (o p) s")
                            load_rotated([(0, 0, q_src), (HD, HD, q_src)], 3 * g + 1 + uu)
                            weights(2 + uu)
                            sp.wait_ge(q["z_gate"], START + 2 * g + uu)
                            sp.dma_start(ZX[:], proj[ds(2 * g + (U_AZ + uu), 1)].rearrange("o p s -> (o p) s"))\
                                .then_inc(q["z_in"], 16)
                        for uu in range(2):
                            if uu == 0:
                                for k in range(4, 8):
                                    weights(k)
                            else:
                                for k in range(2):
                                    side.load(sp, g + 1, k, side_column(g + 1, k), ahead=True)
                            sp.wait_ge(q["gated"], START + NM * g + NT * (uu + 1))
                            sp.dma_start(gated[ds(2 * g + uu, 1)].rearrange("o p s -> (o p) s"), O[uu][:])\
                                .then_inc(q["stored"], 16)
                    sp.wait_ge(q["stored"], START + 16 * 4)

                @block.gpsimd
                def _(pool):
                    with pool.Fori(0, 2) as g:
                        for k in range(10):
                            if k < 3:
                                pool.wait_ge(q["x_in"], START + 96 * (3 * g + k + 1))
                                nc.gpsimd.tensor_tensor(XR[:], XR[:], sin[:], ALU.mult).then_inc(q["sined"], 1)
                            if 2 <= k < 8:
                                side.split(pool, g, k)
                            if k >= 8:
                                side.split(pool, g + 1, k - 8, ahead=True)

                @block.tensor
                def _(pe):
                    with pe.Fori(0, 2) as g:
                        side.half(pe, g, 0, 0)
                        side.half(pe, g, 0, 1)
                        pe.wait_ge(q["v_in"], START + 32 * g + 32)
                        pe.wait_ge(q["masked"], START + NM * g)
                        for t in range(NT):
                            last = nc.tensor.transpose(bank(t // 4)[:, t % 4 * P:(t % 4 + 1) * P],
                                                       VX[:, t * P:(t + 1) * P], ident)
                        last.then_inc(q["v_turned"], 1)
                        side.half(pe, g, 1, 0)
                        side.half(pe, g, 1, 1)
                        pe.wait_ge(q["v_lo"], START + g + 1)
                        for t in range(NM + 2):
                            if t < NM:
                                m, s = t, t % 2
                                i, lo, nb, _ = window(m)
                                if i == 0:
                                    pe.wait_ge(q["lo"], START + 3 * g + 2 + m // NT)
                                pe.wait_ge(q["masked"], START + NM * g + max(m - 1, 0))
                                for n, (a, b) in enumerate(((q_hi, k_hi), (q_hi, k_lo), (q_lo, k_hi))):
                                    for h in range(2):
                                        r = slice(h * HD, (h + 1) * HD)
                                        last = nc.tensor.matmul(pairs[s][:, h, 0:nb * P],
                                                                a[m // NT][r, i * P:(i + 1) * P],
                                                                b[r, lo * P:(lo + nb) * P], start=(n == 0), stop=(n == 2))
                                last.then_inc(q["scored"], 1)
                                if t in side_steps:
                                    n = EARLY + side_steps.index(t)
                                    side.half(pe, g, n // 2, n % 2)
                            if 1 <= t <= NM:
                                m, s = t - 1, (t - 1) % 2
                                i, lo, nb, _ = window(m)
                                pe.wait_ge(q["probs"], START + NM * g + m + 1)
                                pe.wait_ge(q["p_lo"], START + NM * g + m)
                                for h in range(2):
                                    for b in range(nb):
                                        last = nc.tensor.transpose(pairs[2][:, h, b * P:(b + 1) * P],
                                                                   PR[s][:, h, b * P:(b + 1) * P], ident)
                                last.then_inc(q["turned"], 1)
                            if 2 <= t:
                                m, s = t - 2, t % 2
                                i, lo, nb, _ = window(m)
                                pe.wait_ge(q["p_lo"], START + NM * g + m + 1)
                                pe.wait_ge(q["gated"], START + NM * g + m)
                                for h in range(2):
                                    v0 = HD * (1 - h)
                                    for b in range(nb):
                                        for n, (a, c) in enumerate(((v_hi, p_hi), (v_hi, p_lo), (v_lo, p_hi))):
                                            last = nc.tensor.matmul(bank(6)[:, 0:P],
                                                                    a[:, lo + b, v0:v0 + P], c[s][:, h, b * P:(b + 1) * P],
                                                                    start=(h == 0 and b == 0 and n == 0),
                                                                    stop=(h == 1 and b == nb - 1 and n == 2))
                                last.then_inc(q["summed"], 1)

                @block.scalar
                def _(act):
                    with act.Fori(0, 2) as g:
                        def q_part(uu):
                            act.wait_ge(q["rotated"], START + 3 * g + 2 + uu)
                            act.wait_ge(q["scored"], START + NM * g)
                            nc.scalar.activation(q_hi[uu][:], X[:], ACT.Copy).then_inc(q["hi"], 1)

                        def z_part(uu):
                            act.wait_ge(q["z_in"], START + 16 * (2 * g + uu + 1))
                            act.wait_ge(q["gated"], START + NM * g)
                            act.wait_ge(q["stored"], START + 32 * g)
                            nc.scalar.activation(ZT[uu][:], ZX[:], ACT.Tanh, scale=0.5).then_inc(q["tanh"], 1)

                        def side_out(n):
                            side.out(act, g, n // 2, n % 2, side_unit(g, n // 2))

                        act.wait_ge(q["rotated"], START + 3 * g + 1)
                        act.wait_ge(q["scored"], START + NM * g)
                        nc.scalar.activation(k_hi[:], X[:], ACT.Copy).then_inc(q["hi"], 1)
                        side_out(0)
                        side_out(1)
                        act.wait_ge(q["v_turned"], START + g + 1)
                        act.wait_ge(q["summed"], START + NM * g)
                        act.wait_ge(q["pads"], START + 2)
                        nc.scalar.activation(v_hi[:, :, HD:2 * HD], v_turned, ACT.Copy)\
                            .then_inc(q["v_hi"], 1)
                        q_part(0)
                        side_out(2)
                        q_part(1)
                        side_out(3)
                        for t in range(NM + 1):
                            if t % NT == 0 and t < NM:
                                z_part(t // NT)
                            if t < NM:
                                m, s = t, t % 2
                                i, lo, nb, _ = window(m)
                                act.wait_ge(q["shifted"], START + NM * g + m + 1)
                                act.wait_ge(q["turned"], START + NM * g + max(m - 1, 0))
                                for h in range(2):
                                    nc.scalar.activation(PR[s][:, h, 0:nb * P], SM[s][:, h, 0:nb * P], ACT.Exp,
                                                         bias=stat[s][:, 1, h:h + 1], accum_out=stat[s][:, 3, h:h + 1])
                                nc.scalar.activation(stat[s][:, 4, :], stat[s][:, 2, :], ACT.Exp).then_inc(q["exped"], 1)
                                if t in side_steps:
                                    side_out(EARLY + side_steps.index(t))
                            if 1 <= t:
                                m, s = t - 1, (t - 1) % 2
                                i, lo, nb, _ = window(m)
                                act.wait_ge(q["turned"], START + NM * g + m + 1)
                                act.wait_ge(q["summed"], START + NM * g + max(m - 1, 0))
                                nc.scalar.activation(p_hi[s][:, :, 0:nb * P], pairs[2][:, :, 0:nb * P], ACT.Copy)\
                                    .then_inc(q["p_hi"], 1)
                    side.finish(act, 2)

                @block.vector
                def _(dve):
                    for v in (v_hi, v_lo):
                        nc.vector.memset(v[:].bitcast(F32), 0.0).then_inc(q["pads"], 1)
                    dve.wait_ge(q["sink_in"], START + 16)
                    dve.wait_ge(q["pads"], START + 2)
                    with dve.Fori(0, 2) as g:
                        dve.wait_ge(q["shifted"], START + NM * g)
                        nc.vector.tensor_scalar(sink, sinks[:, ds(4 * g, 4)], 1.0, None, ALU.mult).then_inc(q["sink"], 1)
                        nc.vector.tensor_scalar(neg_sink, sinks[:, ds(4 * g, 4)], -1.0, None, ALU.mult)\
                            .then_inc(q["neg_sink"], 1)

                        def rotate(r):
                            dve.wait_ge(q["x_in"], START + 96 * (3 * g + r + 1))
                            nc.vector.tensor_tensor(X[:], X[:], cos[:], ALU.mult).then_inc(q["cosined"], 1)
                            dve.wait_ge(q["cosined"], START + 3 * g + r + 1)
                            dve.wait_ge(q["sined"], START + 3 * g + r + 1)
                            nc.vector.tensor_tensor(X[:], X[:], XR[:], ALU.add).then_inc(q["rotated"], 1)

                        def low(r, hi, lo):
                            dve.wait_ge(q["hi"], START + 3 * g + r + 1)
                            nc.vector.tensor_tensor(lo[:], X[:], hi[:].bitcast(F32), ALU.subtract).then_inc(q["lo"], 1)

                        rotate(0)
                        low(0, k_hi, k_lo)
                        dve.wait_ge(q["v_hi"], START + g + 1)
                        nc.vector.tensor_tensor(v_lo[:, :, HD:2 * HD], v_turned,
                                                v_hi[:, :, HD:2 * HD].bitcast(F32), ALU.subtract).then_inc(q["v_lo"], 1)
                        rotate(1)
                        low(1, q_hi[0], q_lo[0])
                        rotate(2)
                        low(2, q_hi[1], q_lo[1])
                        for t in range(NM + 2):
                            if t < NM:
                                m, s = t, t % 2
                                i, lo, nb, b0 = window(m)
                                st = stat[s]
                                hh = slice(2 * (m // NT), 2 * (m // NT) + 2)
                                dve.wait_ge(q["scored"], START + NM * g + m + 1)
                                dve.wait_ge(q["exped"], START + NM * g + max(m - 1, 0))
                                nc.vector.scalar_tensor_tensor(out=SM[s][:, :, 0:nb * P], in0=pairs[s][:, :, 0:nb * P],
                                                               scalar=SCALE, in1=bcast(band[:, b0:b0 + nb * P], 2),
                                                               op0=ALU.mult, op1=ALU.add).then_inc(q["masked"], 1)
                                dve.wait_ge(q["masked"], START + NM * g + m + 1)
                                nc.vector.tensor_reduce(st[:, 0, :], SM[s][:, :, 0:nb * P], AX_X, ALU.max)\
                                    .then_inc(q["rowmax"], 1)
                                dve.wait_ge(q["rowmax"], START + NM * g + m + 1)
                                dve.wait_ge(q["neg_sink"], START + g + 1)
                                nc.vector.scalar_tensor_tensor(out=st[:, 1, :], in0=st[:, 0, :], scalar=-1.0,
                                                               in1=neg_sink[:, hh], op0=ALU.mult, op1=ALU.min)\
                                    .then_inc(q["negmax"], 1)
                                dve.wait_ge(q["negmax"], START + NM * g + m + 1)
                                dve.wait_ge(q["sink"], START + g + 1)
                                nc.vector.tensor_tensor(st[:, 2, :], sink[:, hh], st[:, 1, :], ALU.add)\
                                    .then_inc(q["shifted"], 1)
                            if t % NT == 1 and t < NM:
                                uu = t // NT
                                dve.wait_ge(q["tanh"], START + 2 * g + uu + 1)
                                nc.vector.scalar_tensor_tensor(out=ZT[uu][:], in0=ZT[uu][:], scalar=1.0, in1=ZX[:],
                                                               op0=ALU.add, op1=ALU.mult).then_inc(q["z_gate"], 1)
                            if t < NM:
                                m, s = t, t % 2
                                i, lo, nb, _ = window(m)
                                st = stat[s]
                                dve.wait_ge(q["exped"], START + NM * g + m + 1)
                                nc.vector.tensor_tensor(st[:, 5, :], st[:, 3, :], st[:, 4, :], ALU.add)\
                                    .then_inc(q["denom"], 1)
                                dve.wait_ge(q["denom"], START + NM * g + m + 1)
                                nc.vector.reciprocal(st[:, 6, :], st[:, 5, :]).then_inc(q["recip"], 1)
                                dve.wait_ge(q["recip"], START + NM * g + m + 1)
                                for h in range(2):
                                    last = nc.vector.tensor_scalar(PR[s][:, h, 0:nb * P], PR[s][:, h, 0:nb * P],
                                                                   st[:, 6, h:h + 1], None, ALU.mult)
                                last.then_inc(q["probs"], 1)
                            if 1 <= t <= NM:
                                m, s = t - 1, (t - 1) % 2
                                i, lo, nb, _ = window(m)
                                dve.wait_ge(q["p_hi"], START + NM * g + m + 1)
                                dve.wait_ge(q["summed"], START + NM * g + max(m - 1, 0))
                                nc.vector.tensor_tensor(p_lo[s][:, :, 0:nb * P], pairs[2][:, :, 0:nb * P],
                                                        p_hi[s][:, :, 0:nb * P].bitcast(F32), ALU.subtract)\
                                    .then_inc(q["p_lo"], 1)
                            if 2 <= t:
                                m = t - 2
                                i = m % NT
                                dve.wait_ge(q["summed"], START + NM * g + m + 1)
                                if i == 0:
                                    dve.wait_ge(q["z_gate"], START + 2 * g + m // NT + 1)
                                nc.vector.scalar_tensor_tensor(out=O[m // NT][:, i * P:(i + 1) * P], in0=bank(6)[:, 0:P],
                                                               scalar=0.5, in1=ZT[m // NT][:, i * P:(i + 1) * P],
                                                               op0=ALU.mult, op1=ALU.mult).then_inc(q["gated"], 1)

        def diff_unit(h, k):
            return h + N_PLAIN if k == 0 else h * 3 + (U_C + k - 1)

        def attend_full(l):
            with Phase("diff", ["par_in", "lam", "lq", "lsum", "lexp", "g_scaled", "x_in0", "x_in1", "cosined", "sined", "rotated",
                                "hi", "lo", "v_in", "v_turned", "v_hi", "v_lo", "z_in", "tanh", "z_gate", "scored",
                                "negmax", "bias", "exped", "recip", "nlam", "scaled", "mixed", "turned", "a_hi",
                                "a_lo", "summed", "copied", "squared", "total", "log", "root", "normed", "gated",
                                "stored"] + Side.SEMS, Side.AHEAD) as (block, q):
                X, XR = [sb(f"diff_x{n}", [P, S]) for n in "qk"], sb("diff_xr", [P, S])
                VX = sb("diff_vx", [P, S])
                ZT = sb("diff_zt", [P, S])
                qk_hi = [sb(f"diff_{n}_hi", [P, S], F32R) for n in "qk"]
                qk_lo = [sb(f"diff_{n}_lo", [P, S], F32R) for n in "qk"]
                v_hi, v_lo = sb("diff_v_hi", [P, NT, P], F32R), sb("diff_v_lo", [P, NT, P], F32R)
                PR = [[sb(f"diff_p{s}{c}", [P, S]) for c in range(2)] for s in range(2)]
                a_hi, a_lo = sb("diff_a_hi", [P, NT, 2 * P], F32R), sb("diff_a_lo", [P, NT, 2 * P], F32R)
                XR0 = (XR, ZT)
                SQ, R = PR[0]
                O = sb("diff_o", [P, S])
                OUT = sb("diff_out", [P, S])
                stat = [sb(f"diff_stat{s}", [P, 5, 2]) for s in range(2)]
                side = Side(l, q, 4)
                side_unit = diff_unit
                side_steps = (0, 1, 2, 4, 5, 6)
                side_column = lambda h, k: side_unit(h, k) * P + (N_BA if k == 0 else 0)
                lq = sb("diff_lq", [P, 4, HD])
                par = sb("diff_par", [P, 12])
                g_raw, g_sub, lam_in, lsum, lexp, lam, nlam = (par[:, 0:1], par[:, 1:2], par[:, 2:4], par[:, 4:6],
                                                               par[:, 6:8], par[:, 8:9], par[:, 9:10])
                flat = lambda pair: pair[:].rearrange("p a b -> p (a b)")

                @block.sync
                def _(sp):
                    sp.dma_start(lq[:].rearrange("p a b -> p (a b)"),
                                 b_lambda[ds(l, 1)].rearrange("o a b -> (o a b)").partition_broadcast(P))\
                        .then_inc(q["par_in"], 16)
                    sp.dma_start(g_raw, b_subln_g[ds(l, 1), :].rearrange("o p -> p o"), allow_slow_non_contiguous=True)\
                        .then_inc(q["par_in"], 16)
                    sp.dma_start(lam_in, lam_t[:, ds(l, 1), :].rearrange("p o n -> p (o n)")).then_inc(q["par_in"], 16)

                    def load_rotated(h, n, XR=XR):
                        u = (U_BQ, U_BK)[n]
                        src = lambda r, c: proj[u:u + 5][ds(h, 1), r:r + c, :].rearrange("o p s -> (o p) s")
                        sp.dma_start(X[n][:], src(0, P)).then_inc(q[f"x_in{n}"], 16)
                        for a in range(4):
                            sp.dma_start(XR[32 * a:32 * a + 32, :], src(32 * (a ^ 1), 32)).then_inc(q[f"x_in{n}"], 16)

                    def load_v(h):
                        sp.dma_start(VX[:], proj[U_BV:U_BV + 5][ds(h, 1)].rearrange("o p s -> (o p) s"))\
                            .then_inc(q["v_in"], 16)

                    load_v(0)
                    load_rotated(0, 0)
                    load_rotated(0, 1, XR0[1])
                    with sp.Fori(0, 4) as h:
                        sp.wait_ge(q["v_turned"], START + h + 1)
                        sp.dma_start(VX[:], proj[U_BZ:U_BZ + 4][ds(h, 1)].rearrange("o p s -> (o p) s")).then_inc(q["z_in"], 16)
                        side.load(sp, h, 2, side_column(h, 2))
                        sp.wait_ge(q["lo"], START + 2 * h + 2)
                        load_rotated(h + 1, 0)
                        side.load(sp, h, 3, side_column(h, 3))
                        sp.wait_ge(q["rotated"], START + 2 * h + 3)
                        load_rotated(h + 1, 1)
                        sp.wait_ge(q["z_gate"], START + h + 1)
                        load_v(h + 1)
                        for k in range(2):
                            side.load(sp, h + 1, k, side_column(h + 1, k), ahead=True)
                        sp.wait_ge(q["gated"], START + h + 1)
                        sp.dma_start(gated[4:8][ds(h, 1)].rearrange("o p s -> (o p) s"), OUT[:]).then_inc(q["stored"], 16)
                    sp.wait_ge(q["v_in"], START + 16 * 5)
                    sp.wait_ge(q["stored"], START + 16 * 4)

                @block.gpsimd
                def _(pool):
                    def sine(h, n, XR=XR):
                        pool.wait_ge(q[f"x_in{n}"], START + 80 * (h + 1))
                        nc.gpsimd.tensor_tensor(XR[:], XR[:], sin[:], ALU.mult).then_inc(q["sined"], 1)

                    for n in range(2):
                        sine(0, n, XR0[n])
                    with pool.Fori(0, 4) as h:
                        for n in range(2):
                            side.split(pool, h, 2 + n)
                            sine(h + 1, n)
                        side.split(pool, h + 1, 0, ahead=True)
                        pool.wait_ge(q["normed"], START + h + 1)
                        pool.wait_ge(q["stored"], START + 16 * h)
                        nc.gpsimd.tensor_tensor(OUT[:], O[:], ZT[:], ALU.mult).then_inc(q["gated"], 1)
                        side.split(pool, h + 1, 1, ahead=True)

                @block.tensor
                def _(pe):
                    with pe.Fori(0, 4) as h:
                        def sum_values(j):
                            pe.wait_ge(q["a_lo"], START + NT * h + 2 * j + 2)
                            pe.wait_ge(q["copied"], START + 4 * h + j)
                            for b in range(NT):
                                for n, (a, c) in enumerate(((v_hi, a_hi), (v_hi, a_lo), (v_lo, a_hi))):
                                    last = nc.tensor.matmul(bank(6)[:, 0:2 * P], a[:, b, :], c[:, b, :],
                                                            start=(b == 0 and n == 0), stop=(b == NT - 1 and n == 2))
                            last.then_inc(q["summed"], 1)

                        side.half(pe, h, 0, 0)
                        pe.wait_ge(q["v_in"], START + 16 * h + 16)
                        pe.wait_ge(q["exped"], START + 16 * h)
                        for t in range(NT):
                            last = nc.tensor.transpose(bank(t // 4)[:, t % 4 * P:(t % 4 + 1) * P],
                                                       VX[:, t * P:(t + 1) * P], ident)
                        last.then_inc(q["v_turned"], 1)
                        pe.wait_ge(q["lo"], START + 2 * h + 2)
                        pe.wait_ge(q["v_lo"], START + h + 1)
                        for t in range(NT + 1):
                            if t < NT:
                                m = t
                                if t == 0:
                                    pe.wait_ge(q["root"], START + h)
                                for c in range(2):
                                    pe.wait_ge(q["exped"], START + 16 * h + max(2 * m + c - 1, 0))
                                    r = slice(c * HD, (c + 1) * HD)
                                    for n, (a, b) in enumerate(((qk_hi[0], qk_hi[1]), (qk_hi[0], qk_lo[1]),
                                                                (qk_lo[0], qk_hi[1]))):
                                        for half in range(2):
                                            last = nc.tensor.matmul(pairs[c][:, half, :], a[r, m * P:(m + 1) * P],
                                                                    b[r, half * HALF:(half + 1) * HALF],
                                                                    start=(n == 0), stop=(n == 2))
                                    last.then_inc(q["scored"], 1)
                                if t in side_steps:
                                    n = 1 + side_steps.index(t)
                                    side.half(pe, h, n // 2, n % 2)
                            if 3 <= t and t % 2:
                                sum_values(t // 2 - 1)
                            if 1 <= t:
                                m = t - 1
                                pe.wait_ge(q["mixed"], START + NT * h + m + 1)
                                pe.wait_ge(q["a_lo"], START + NT * h + m)
                                for b in range(NT):
                                    last = nc.tensor.transpose(pairs[2][:, b // 4, b % 4 * P:(b % 4 + 1) * P],
                                                               PR[m % 2][0][:, b * P:(b + 1) * P], ident)
                                last.then_inc(q["turned"], 1)
                        side.half(pe, h, 3, 1)
                        sum_values(3)
                        pe.wait_ge(q["squared"], START + h + 1)
                        for half in range(2):
                            last = nc.tensor.matmul(pairs[2][:, half, :], ones, SQ[:, half * HALF:(half + 1) * HALF],
                                                    start=True, stop=True)
                        last.then_inc(q["total"], 1)

                @block.scalar
                def _(act):
                    act.wait_ge(q["lsum"], START + 2)
                    nc.scalar.activation(lexp, lsum, ACT.Exp).then_inc(q["lexp"], 1)
                    with act.Fori(0, 4) as h:
                        def copy_values(j):
                            act.wait_ge(q["summed"], START + 4 * h + j + 1)
                            if j == 0:
                                act.wait_ge(q["gated"], START + h)
                            nc.scalar.activation(O[:, j * 2 * P:(j + 1) * 2 * P], bank(6)[:, 0:2 * P], ACT.Copy)\
                                .then_inc(q["copied"], 1)

                        for n in range(2):
                            act.wait_ge(q["rotated"], START + 2 * h + n + 1)
                            act.wait_ge(q["scored"], START + 16 * h)
                            nc.scalar.activation(qk_hi[n][:], X[n][:], ACT.Copy).then_inc(q["hi"], 1)
                            if n == 1:
                                act.wait_ge(q["v_turned"], START + h + 1)
                                act.wait_ge(q["summed"], START + 4 * h)
                                nc.scalar.activation(v_hi[:].rearrange("p t d -> p (t d)"), flat(pairs[0]), ACT.Copy)\
                                    .then_inc(q["v_hi"], 1)
                        side.out(act, h, 0, 0, side_unit(h, 0), gate=True)
                        act.wait_ge(q["z_in"], START + 16 * h + 16)
                        act.wait_ge(q["gated"], START + h)
                        nc.scalar.activation(ZT[:], VX[:], ACT.Tanh, scale=0.5).then_inc(q["tanh"], 1)
                        for t in range(NT + 1):
                            if t < NT:
                                m, st = t, stat[t % 2]
                                if t == 0:
                                    act.wait_ge(q["normed"], START + h)
                                for c in range(2):
                                    act.wait_ge(q["bias"], START + 16 * h + 2 * m + c + 1)
                                    act.wait_ge(q["turned"], START + NT * h + max(m - 1, 0))
                                    nc.scalar.activation(PR[m % 2][c][:], flat(pairs[c]), ACT.Exp, scale=SCALE,
                                                         bias=st[:, 1, c:c + 1], accum_out=st[:, 2, c:c + 1])\
                                        .then_inc(q["exped"], 1)
                                act.wait_ge(q["recip"], START + NT * h + m + 1)
                                nc.scalar.activation(PR[m % 2][0][:], PR[m % 2][0][:], ACT.Copy, scale=st[:, 3, 0:1])\
                                    .then_inc(q["scaled"], 1)
                                if t in side_steps:
                                    n = 1 + side_steps.index(t)
                                    side.out(act, h, n // 2, n % 2, side_unit(h, n // 2), gate=n < 2)
                            if 3 <= t and t % 2:
                                copy_values(t // 2 - 1)
                            if 1 <= t:
                                m = t - 1
                                act.wait_ge(q["turned"], START + NT * h + m + 1)
                                if m % 2 == 0:
                                    act.wait_ge(q["summed"], START + 4 * h + m // 2)
                                nc.scalar.activation(a_hi[:, :, m % 2 * P:(m % 2 + 1) * P],
                                                     pairs[2][:].rearrange("p a (b s) -> p (a b) s", s=P), ACT.Copy)\
                                    .then_inc(q["a_hi"], 1)
                        side.out(act, h, 3, 1, side_unit(h, 3))
                        copy_values(3)
                        act.wait_ge(q["copied"], START + 4 * h + 4)
                        nc.scalar.activation(SQ[:], O[:], ACT.Square).then_inc(q["squared"], 1)
                        act.wait_ge(q["total"], START + h + 1)
                        root(act, R[:], flat(pairs[2]), P, q["log"], h + 1, q["root"])
                    side.finish(act, 4)

                @block.vector
                def _(dve):
                    dve.wait_ge(q["par_in"], START + 48)
                    nc.vector.tensor_tensor(lq[:, 0:4:2, :], lq[:, 0:4:2, :], lq[:, 1:4:2, :], ALU.mult).then_inc(q["lq"], 1)
                    dve.wait_ge(q["lq"], START + 1)
                    for n in range(2):
                        nc.vector.tensor_reduce(lsum[:, n:n + 1], lq[:, 2 * n, :], AX_X, ALU.add).then_inc(q["lsum"], 1)
                    dve.wait_ge(q["lexp"], START + 1)
                    nc.vector.tensor_tensor(lam, lexp[:, 0:1], lexp[:, 1:2], ALU.subtract).then_inc(q["lam"], 1)
                    dve.wait_ge(q["lam"], START + 1)
                    nc.vector.tensor_tensor(lam, lam, lam_in[:, 0:1], ALU.add).then_inc(q["lam"], 1)
                    dve.wait_ge(q["lam"], START + 2)
                    nc.vector.tensor_scalar(nlam, lam, -1.0, None, ALU.mult).then_inc(q["lam"], 1)
                    nc.vector.tensor_tensor(g_sub, g_raw, lam_in[:, 1:2], ALU.mult).then_inc(q["g_scaled"], 1)
                    dve.wait_ge(q["lam"], START + 3)
                    dve.wait_ge(q["g_scaled"], START + 1)

                    def rotate(h, n, XR=XR):
                        dve.wait_ge(q[f"x_in{n}"], START + 80 * (h + 1))
                        nc.vector.tensor_tensor(X[n][:], X[n][:], cos[:], ALU.mult).then_inc(q["cosined"], 1)
                        dve.wait_ge(q["cosined"], START + 2 * h + n + 1)
                        dve.wait_ge(q["sined"], START + 2 * h + n + 1)
                        nc.vector.tensor_tensor(X[n][:], X[n][:], XR[:], ALU.add).then_inc(q["rotated"], 1)

                    for n in range(2):
                        rotate(0, n, XR0[n])
                    with dve.Fori(0, 4) as h:
                        for n in range(2):
                            dve.wait_ge(q["hi"], START + 2 * h + n + 1)
                            nc.vector.tensor_tensor(qk_lo[n][:], X[n][:], qk_hi[n][:].bitcast(F32), ALU.subtract)\
                                .then_inc(q["lo"], 1)
                        dve.wait_ge(q["v_hi"], START + h + 1)
                        nc.vector.tensor_tensor(v_lo[:].rearrange("p t d -> p (t d)"), flat(pairs[0]),
                                                v_hi[:].rearrange("p t d -> p (t d)").bitcast(F32), ALU.subtract)\
                            .then_inc(q["v_lo"], 1)
                        for t in range(NT + 1):
                            if t < NT:
                                m, st = t, stat[t % 2]
                                for c in range(2):
                                    dve.wait_ge(q["scored"], START + 16 * h + 2 * m + c + 1)
                                    nc.vector.tensor_reduce(st[:, 0, c:c + 1], flat(pairs[c]), AX_X, ALU.max, negate=True)\
                                        .then_inc(q["negmax"], 1)
                                    dve.wait_ge(q["negmax"], START + 16 * h + 2 * m + c + 1)
                                    nc.vector.tensor_scalar(st[:, 1, c:c + 1], st[:, 0, c:c + 1], SCALE, None, ALU.mult)\
                                        .then_inc(q["bias"], 1)
                            if t == 0:
                                dve.wait_ge(q["tanh"], START + h + 1)
                                nc.vector.scalar_tensor_tensor(out=ZT[:], in0=ZT[:], scalar=1.0, in1=VX[:],
                                                               op0=ALU.add, op1=ALU.mult).then_inc(q["z_gate"], 1)
                            if t < NT:
                                m, st = t, stat[t % 2]
                                dve.wait_ge(q["exped"], START + 16 * h + 2 * m + 2)
                                nc.vector.reciprocal(st[:, 3, :], st[:, 2, :]).then_inc(q["recip"], 1)
                                dve.wait_ge(q["recip"], START + NT * h + m + 1)
                                nc.vector.tensor_scalar(st[:, 4, 0:1], st[:, 3, 1:2], nlam, None, ALU.mult)\
                                    .then_inc(q["nlam"], 1)
                                dve.wait_ge(q["nlam"], START + NT * h + m + 1)
                                dve.wait_ge(q["scaled"], START + NT * h + m + 1)
                                nc.vector.scalar_tensor_tensor(out=PR[m % 2][0][:], in0=PR[m % 2][1][:],
                                                               scalar=st[:, 4, 0:1], in1=PR[m % 2][0][:],
                                                               op0=ALU.mult, op1=ALU.add).then_inc(q["mixed"], 1)
                            if t >= 1:
                                m = t - 1
                                dve.wait_ge(q["a_hi"], START + NT * h + m + 1)
                                w = slice(m % 2 * P, (m % 2 + 1) * P)
                                nc.vector.tensor_tensor(a_lo[:, :, w], pairs[2][:].rearrange("p a (b s) -> p (a b) s", s=P),
                                                        a_hi[:, :, w].bitcast(F32), ALU.subtract).then_inc(q["a_lo"], 1)
                            if t in (4, 6):
                                rotate(h + 1, t // 2 - 2)
                        dve.wait_ge(q["root"], START + h + 1)
                        nc.vector.scalar_tensor_tensor(out=O[:], in0=O[:], scalar=g_sub, in1=R[:], op0=ALU.mult,
                                                       op1=ALU.mult).then_inc(q["normed"], 1)

        def convolve(l):
            with Phase("conv", ["in0", "in1", "in2", "pad", "tap", "tanh", "silu", "squared", "total", "log", "root",
                                "normed", "put0", "put1", "put2"]
                       + Side.SEMS, Side.AHEAD) as (block, q):
                X = [sb(f"conv_x{n}", [P, S + 4]) for n in range(3)]
                Y = [sb(f"conv_y{n}", [P, S]) for n in range(3)]
                T = [sb(f"conv_t{n}", [P, S]) for n in range(3)]
                W = [sb(f"conv_w{n}", [P, 5]) for n in range(3)]
                R = [sb(f"conv_r{n}", [P, S]) for n in range(2)]
                side = Side(l, q, 4)
                side_unit = lambda h, k: h + U_CZ if k == 1 else h * 3 + (N_PLAIN + 4 + max(k - 1, 0))
                side_column = lambda h, k: side_unit(h, k) * P + (N_BA if k != 1 else 0)
                eps4 = sb("conv_eps4", [P, 1])
                flat = lambda pair: pair[:].rearrange("p a b -> p (a b)")

                @block.sync
                def _(sp):
                    sp.wait_ge(q["pad"], START + 3)

                    def load(h, n):
                        sp.dma_start(X[n][:, 2:S + 2], proj[U_C + 4 * n:U_C + 4 * n + 4][ds(h, 1)]
                                     .rearrange("o p s -> (o p) s")).then_inc(q[f"in{n}"], 16)
                        sp.dma_start(W[n][:], c_conv_w[ds(l, 1), :, 4 * n * P:4 * (n + 1) * P]
                                     .rearrange("o t (h p) -> h p (o t)", p=P)[ds(h, 1)].rearrange("o p t -> (o p) t"),
                                     allow_slow_non_contiguous=True).then_inc(q[f"in{n}"], 16)

                    def turn(h, more):
                        for k in range(2, 4):
                            side.load(sp, h, k, side_column(h, k))
                        for n in range(3):
                            if more:
                                sp.wait_ge(q["tap"], START + 15 * h + 5 * n + 5)
                                load(h + 1, n)
                                if n < 2:
                                    side.load(sp, h + 1, n, side_column(h + 1, n), ahead=True)
                        for n in range(3):
                            if n < 2:
                                sp.wait_ge(q["normed"], START + 2 * h + n + 1)
                            else:
                                sp.wait_ge(q["silu"], START + 3 * h + 3)
                            sp.dma_start(conv[4 * n:4 * n + 4][ds(h, 1)].rearrange("o p s -> (o p) s"), Y[n][:])\
                                .then_inc(q[f"put{n}"], 16)

                    for n in range(3):
                        load(0, n)
                    with sp.Fori(0, 3) as h:
                        turn(h, True)
                    turn(3, False)
                    for n in range(3):
                        sp.wait_ge(q[f"put{n}"], START + 64)

                @block.scalar
                def _(act):
                    with act.Fori(0, 4) as h:
                        def tanh(n):
                            act.wait_ge(q["tap"], START + 15 * h + 5 * n + 5)
                            nc.scalar.activation(T[n][:], Y[n][:], ACT.Tanh, scale=0.5).then_inc(q["tanh"], 1)

                        def side_out(n):
                            side.out(act, h, n // 2, n % 2, side_unit(h, n // 2), gate=n // 2 != 1)

                        def square(n):
                            act.wait_ge(q["silu"], START + 3 * h + n + 1)
                            nc.scalar.activation(T[n][:], Y[n][:], ACT.Square).then_inc(q["squared"], 1)

                        def to_root(n):
                            act.wait_ge(q["total"], START + 2 * h + n + 1)
                            root(act, R[n][:], flat(pairs[n]), 1, q["log"], 2 * h + n + 1, q["root"], bias=eps4[:])

                        side_out(0)
                        tanh(0)
                        side_out(1)
                        tanh(1)
                        square(0)
                        side_out(2)
                        to_root(0)
                        tanh(2)
                        side_out(3)
                        square(1)
                        side_out(4)
                        to_root(1)
                        for n in range(5, 8):
                            side_out(n)
                    side.finish(act, 4)

                @block.gpsimd
                def _(pool):
                    def splits(h, more):
                        for k in range(2, 4):
                            side.split(pool, h, k)
                        if more:
                            for k in range(2):
                                side.split(pool, h + 1, k, ahead=True)

                    with pool.Fori(0, 3) as h:
                        splits(h, True)
                    splits(3, False)

                @block.tensor
                def _(pe):
                    with pe.Fori(0, 4) as h:
                        for k in range(3):
                            side.half(pe, h, k // 2, k % 2)
                        for n in range(2):
                            if n == 1:
                                side.half(pe, h, 1, 1)
                                side.half(pe, h, 2, 0)
                            pe.wait_ge(q["squared"], START + 2 * h + n + 1)
                            for half in range(2):
                                last = nc.tensor.matmul(pairs[n][:, half, :], ones, T[n][:, half * HALF:(half + 1) * HALF],
                                                        start=True, stop=True)
                            last.then_inc(q["total"], 1)
                        for k in range(5, 8):
                            side.half(pe, h, k // 2, k % 2)

                @block.vector
                def _(dve):
                    nc.vector.memset(eps4[:], 4 * EPS)
                    for n in range(3):
                        nc.vector.memset(X[n][:], 0.0).then_inc(q["pad"], 1)
                    with dve.Fori(0, 4) as h:
                        def taps(n):
                            dve.wait_ge(q[f"in{n}"], START + 32 * h + 32)
                            dve.wait_ge(q[f"put{n}"], START + 16 * h)
                            for t in range(5):
                                x_t = X[n][:, t:t + S]
                                if t == 0:
                                    last = nc.vector.tensor_scalar(Y[n][:], x_t, W[n][:, 0:1], None, ALU.mult)
                                else:
                                    dve.wait_ge(q["tap"], START + 15 * h + 5 * n + t)
                                    last = nc.vector.scalar_tensor_tensor(out=Y[n][:], in0=x_t, scalar=W[n][:, t:t + 1],
                                                                          in1=Y[n][:], op0=ALU.mult, op1=ALU.add)
                                last.then_inc(q["tap"], 1)

                        def silu(n):
                            dve.wait_ge(q["tanh"], START + 3 * h + n + 1)
                            nc.vector.scalar_tensor_tensor(out=Y[n][:], in0=T[n][:], scalar=1.0, in1=Y[n][:],
                                                           op0=ALU.add, op1=ALU.mult).then_inc(q["silu"], 1)

                        def unit_length(n):
                            dve.wait_ge(q["root"], START + 2 * h + n + 1)
                            nc.vector.scalar_tensor_tensor(out=Y[n][:], in0=Y[n][:], scalar=(P ** -0.5, 1.0)[n],
                                                           in1=R[n][:], op0=ALU.mult, op1=ALU.mult).then_inc(q["normed"], 1)

                        taps(0)
                        taps(1)
                        silu(0)
                        taps(2)
                        silu(1)
                        unit_length(0)
                        silu(2)
                        unit_length(1)

        def delta_rule(l):
            pe_names = ["k_turned", "v_turned", "rows", "gram", "qk", "a_turned"]
            dve_names = ["col", "diff", "neg", "attn", "qm", "t_off", "t0"]
            for k in range(1, N_LEVELS):
                pe_names += [f"x{k}", f"tx{k}", f"ux{k}"] if k < N_LEVELS - 1 else [f"x{k}", f"ux{k}"]
                dve_names += [f"xm{k}", f"t{k}", f"u{k}"] if k < N_LEVELS - 1 else [f"xm{k}", f"u{k}"]
            pe_names += ["z", "v_new", "o", "s_add"]
            dve_names += ["r", "vw", "s"]
            act_names = ["k_tok", "v_tok", "rows_exp", "decay", "o_out"]
            pool_names = ["dtm", "bm", "u1", "u", "qd", "vt"]
            with Phase("delta", ["in0", "in1", "put0", "put1", "state", "pe0", "pe1", "dve0", "dve1", "act0", "act1",
                                 "pool0", "pool1", "xm_zero"] + Side.SEMS) as (block, q):
                pe_s, dve_s, act_s, pool_s = ([Steps(q[f"{e}{d}"], names) for d in range(2)] for e, names in
                                              (("pe", pe_names), ("dve", dve_names), ("act", act_names),
                                               ("pool", pool_names)))
                two = lambda name, shape: [sb(f"delta_{name}{d}", shape) for d in range(2)]
                IN = two("in", [P, 12, P])
                KT, VT, DT, EG, AT, BM, QM, T, U, QD, ST, OC = (
                    two(n, [P, 4, P]) for n in ("kt", "vt", "dt", "eg", "at", "bm", "qm", "t", "u", "qd", "st", "oc"))
                R, VW, VD = DT, BM, EG
                XM = [[None] + [sb(f"delta_xm{d}{k}", [P, 4, P]) for k in range(1, N_LEVELS)] for d in range(2)]
                side = Side(l, q, 1)
                side_unit = lambda c: c + (N_PLAIN + 16)
                COL = two("col", [P, 6, 4])
                G, BETA, GC, NEG, EL, ET = range(6)
                B = [[bank(3 * d + n).rearrange("p (h s) -> p h s", h=4) for n in range(3)] for d in range(2)]
                tile_of = lambda c, d: c if d == 0 else c * -1 + (NT - 1)
                col = lambda d, what: cols(COL[d][:, what, :], P)
                heads = lambda ap: bcast(ap, 4)

                def half_of(t, k, which):
                    return t.rearrange("p h (n w b) -> p h n w b", w=2, b=2 ** k)[:, :, :, which, :]

                @block.sync
                def _(sp):
                    def load(c, d):
                        t = tile_of(c, d)
                        src = conv[:, :, ds(t * P, P)] if not isinstance(t, int) else conv[:, :, t * P:(t + 1) * P]
                        sp.dma_start(IN[d][:], src.rearrange("u p s -> p u s")).then_inc(q[f"in{d}"], 16)

                    for d in range(2):
                        load(0, d)
                    side.load(sp, 0, 0, side_unit(0) * P + N_BA)
                    with sp.Fori(0, NT - 1) as c:
                        side.load(sp, c + 1, 0, side_unit(c + 1) * P + N_BA)
                        for d in range(2):
                            sp.wait_ge(pe_s[d].sem, pe_s[d].at(c, "z"))
                            sp.wait_ge(pool_s[d].sem, pool_s[d].at(c, "qd"))
                            load(c + 1, d)

                @block.tensor
                def _(pe):
                    with pe.Fori(0, NT) as c:
                        def four(d, out, lhs, rhs, name):
                            for h in range(4):
                                last = nc.tensor.matmul(out[:, h, :], lhs(h), rhs(h), start=True, stop=True)
                            pe_s[d].done(last, name)

                        parts = [0]

                        def side_part():
                            n = parts[0]
                            parts[0] += 1
                            side.part(pe, c, 0, n // KC, n % KC)

                        kT = lambda d: lambda h: IN[d][:, 4 + h, :]
                        qT = lambda d: lambda h: IN[d][:, h, :]
                        of = lambda t: lambda h: t[:, h, :]
                        for d in range(2):
                            a, b, e = B[d]
                            pe.wait_ge(q[f"in{d}"], START + 16 * c + 16)
                            pe.wait_ge(dve_s[d].sem, dve_s[d].at(c))
                            pe.wait_ge(act_s[d].sem, act_s[d].at(c))
                            for name, out_, first in (("k_turned", a, 4), ("v_turned", b, 8)):
                                for h in range(4):
                                    last = nc.tensor.transpose(out_[:, h, :], IN[d][:, first + h, :], ident)
                                pe_s[d].done(last, name)
                            pe.wait_ge(dve_s[d].sem, dve_s[d].at(c, "col"))
                            four(d, e, lambda h: COL[d][:, G, h:h + 1].to_broadcast([P, P]), lambda h: tri(d), "rows")
                        for d in range(2):
                            a, b, e = B[d]
                            pe.wait_ge(act_s[d].sem, act_s[d].at(c, "k_tok"))
                            four(d, a, kT(d), kT(d), "gram")
                            pe.wait_ge(act_s[d].sem, act_s[d].at(c, "v_tok"))
                            four(d, b, kT(d), qT(d), "qk")
                        for d in range(2):
                            a, b, e = B[d]
                            pe.wait_ge(dve_s[d].sem, dve_s[d].at(c, "qm"))
                            pe.wait_ge(act_s[d].sem, act_s[d].at(c, "rows_exp"))
                            for h in range(4):
                                last = nc.tensor.transpose(e[:, h, :], QM[d][:, h, :], ident)
                            pe_s[d].done(last, "a_turned")
                        for k in range(1, N_LEVELS):
                            for d in range(2):
                                a, b, e = B[d]
                                t_name = f"t{k - 1}"
                                pe.wait_ge(dve_s[d].sem, dve_s[d].at(c, t_name))
                                four(d, a, of(QM[d]), of(T[d]), f"x{k}")
                            side_part()
                            for d in range(2):
                                a, b, e = B[d]
                                if k == 1:
                                    pe.wait_ge(pool_s[d].sem, pool_s[d].at(c, "u"))
                                pe.wait_ge(dve_s[d].sem, dve_s[d].at(c, f"xm{k}"))
                                if k < N_LEVELS - 1:
                                    four(d, b, of(U[d]), of(XM[d][k]), f"tx{k}")
                                four(d, e, of(XM[d][k]), of(U[d]), f"ux{k}")
                            side_part()
                        for d in range(2):
                            a, b, e = B[d]
                            if d == 0:
                                pe.wait_ge(q["state"], START + 2)
                            four(d, a, kT(d), of(ST[d]), "z")
                        side_part()
                        side_part()
                        for d in range(2):
                            a, b, e = B[d]
                            pe.wait_ge(dve_s[d].sem, dve_s[d].at(c, "r"))
                            four(d, b, of(U[d]), of(R[d]), "v_new")
                        side_part()
                        side_part()
                        for d in range(2):
                            a, b, e = B[d]
                            pe.wait_ge(dve_s[d].sem, dve_s[d].at(c, "vw"))
                            pe.wait_ge(pool_s[d].sem, pool_s[d].at(c, "qd"))
                            for h in range(4):
                                nc.tensor.matmul(e[:, h, :], ST[d][:, h, :], QD[d][:, h, :], start=True, stop=False)
                                last = nc.tensor.matmul(e[:, h, :], VW[d][:, h, :], AT[d][:, h, :], start=False, stop=True)
                            pe_s[d].done(last, "o")
                            pe.wait_ge(pool_s[d].sem, pool_s[d].at(c, "vt"))
                            four(d, a, of(KT[d]), of(VD[d]), "s_add")

                @block.scalar
                def _(act):
                    with act.Fori(0, NT) as c:
                        for d in range(2):
                            a, b, e = B[d]
                            act.wait_ge(pe_s[d].sem, pe_s[d].at(c, "k_turned"))
                            act_s[d].done(nc.scalar.activation(KT[d][:], a, ACT.Copy), "k_tok")
                            act.wait_ge(pe_s[d].sem, pe_s[d].at(c, "v_turned"))
                            act_s[d].done(nc.scalar.activation(VT[d][:], b, ACT.Copy, scale=0.5), "v_tok")
                        for d in range(2):
                            a, b, e = B[d]
                            act.wait_ge(dve_s[d].sem, dve_s[d].at(c, "diff"))
                            act_s[d].done(nc.scalar.activation(EG[d][:], e, ACT.Exp), "rows_exp")
                            act.wait_ge(dve_s[d].sem, dve_s[d].at(c, "neg"))
                            act_s[d].done(nc.scalar.activation(DT[d][:], DT[d][:], ACT.Exp), "decay")
                        side.out(act, c, 0, 0, side_unit(c), gate=True)
                        side.out(act, c, 0, 1, side_unit(c), gate=True)
                        for d in range(2):
                            a, b, e = B[d]
                            act.wait_ge(pe_s[d].sem, pe_s[d].at(c, "o"))
                            act.wait_ge(q[f"put{d}"], START + 16 * c)
                            act_s[d].done(nc.scalar.activation(OC[d][:], e, ACT.Copy), "o_out")
                            act.wait_ge(act_s[d].sem, act_s[d].at(c, "o_out"))
                            act.dma_start(o_dir[d].rearrange("h p s -> p h s")[:, :, ds(tile_of(c, d) * P, P)], OC[d][:])\
                                .then_inc(q[f"put{d}"], 16)
                    for d in range(2):
                        act.wait_ge(q[f"put{d}"], START + 16 * NT)
                    side.finish(act, NT)

                @block.gpsimd
                def _(pool):
                    with pool.Fori(0, NT) as c:
                        side.split(pool, c, 0)
                        for d in range(2):
                            tt = nc.gpsimd.tensor_tensor
                            s = pool_s[d]
                            pool.wait_ge(act_s[d].sem, act_s[d].at(c, "decay"))
                            s.done(tt(DT[d][:], DT[d][:], heads(tri(d)), ALU.mult), "dtm")
                            pool.wait_ge(s.sem, s.at(c, "dtm"))
                            s.done(tt(BM[d][:], DT[d][:], col(d, BETA), ALU.mult), "bm")
                        for d in range(2):
                            s = pool_s[d]
                            pool.wait_ge(dve_s[d].sem, dve_s[d].at(c, "qm"))
                            s.done(tt(U[d][:], QM[d][:], heads(level(1 - d, 0)), ALU.mult), "u1")
                            pool.wait_ge(s.sem, s.at(c, "u1"))
                            s.done(tt(U[d][:], heads(ident), U[d][:], ALU.subtract), "u")
                        for d in range(2):
                            s = pool_s[d]
                            pool.wait_ge(q[f"in{d}"], START + 16 * c + 16)
                            pool.wait_ge(act_s[d].sem, act_s[d].at(c, "rows_exp"))
                            s.done(tt(QD[d][:], IN[d][:, 0:4, :], EG[d][:], ALU.mult), "qd")
                        for d in range(2):
                            s = pool_s[d]
                            pool.wait_ge(dve_s[d].sem, dve_s[d].at(c, "vw"))
                            pool.wait_ge(s.sem, s.at(c, "qd"))
                            s.done(tt(VD[d][:], VW[d][:], col(d, ET), ALU.mult), "vt")

                @block.vector
                def _(dve):
                    for d in range(2):
                        nc.vector.memset(ST[d][:], 0.0).then_inc(q["state"], 1)
                        for k in range(1, N_LEVELS):
                            nc.vector.memset(XM[d][k][:], 0.0).then_inc(q["xm_zero"], 1)
                    dve.wait_ge(q["xm_zero"], START + 2 * (N_LEVELS - 1))
                    tt = nc.vector.tensor_tensor
                    with dve.Fori(0, NT) as c:
                        for d in range(2):
                            a, b, e = B[d]
                            s = dve_s[d]
                            dve.wait_ge(s.sem, s.at(c))
                            s.done(nc.vector.tensor_scalar(
                                COL[d][:], decay[:, :, ds(tile_of(c, d), 1), 4 * d:4 * d + 4].rearrange("p w o n -> p w (o n)"),
                                1.0, None, ALU.mult), "col")
                            dve.wait_ge(s.sem, s.at(c, "col"))
                            dve.wait_ge(pe_s[d].sem, pe_s[d].at(c, "rows"))
                            s.done(tt(DT[d][:], e, col(d, GC), ALU.subtract), "diff")
                            dve.wait_ge(s.sem, s.at(c, "diff"))
                            s.done(nc.vector.tensor_scalar(DT[d][:], DT[d][:], 0.0, None, ALU.min), "neg")
                        for d in range(2):
                            a, b, e = B[d]
                            s = dve_s[d]
                            dve.wait_ge(pool_s[d].sem, pool_s[d].at(c, "dtm"))
                            dve.wait_ge(pe_s[d].sem, pe_s[d].at(c, "qk"))
                            s.done(tt(AT[d][:], b, DT[d][:], ALU.mult), "attn")
                            dve.wait_ge(pool_s[d].sem, pool_s[d].at(c, "bm"))
                            s.done(tt(QM[d][:], a, BM[d][:], ALU.mult), "qm")
                        for d in range(2):
                            a, b, e = B[d]
                            s = dve_s[d]
                            dve.wait_ge(pe_s[d].sem, pe_s[d].at(c, "a_turned"))
                            s.done(tt(T[d][:], e, heads(level(d, 0)), ALU.mult), "t_off")
                            dve.wait_ge(s.sem, s.at(c, "t_off"))
                            s.done(tt(T[d][:], heads(ident), T[d][:], ALU.subtract), "t0")
                        for k in range(1, N_LEVELS):
                            for d in range(2):
                                a, b, e = B[d]
                                dve.wait_ge(pe_s[d].sem, pe_s[d].at(c, f"x{k}"))
                                mask = half_of(heads(level(d, k)), k, d)
                                dve_s[d].done(tt(half_of(XM[d][k][:], k, d), half_of(a, k, d), mask, ALU.mult), f"xm{k}")
                            for d in range(2):
                                a, b, e = B[d]
                                if k < N_LEVELS - 1:
                                    dve.wait_ge(pe_s[d].sem, pe_s[d].at(c, f"tx{k}"))
                                    t_half = half_of(T[d][:], k, d)
                                    dve_s[d].done(tt(t_half, t_half, half_of(b, k, d), ALU.subtract), f"t{k}")
                                dve.wait_ge(pe_s[d].sem, pe_s[d].at(c, f"ux{k}"))
                                u_half = half_of(U[d][:], k, 1 - d)
                                dve_s[d].done(tt(u_half, u_half, half_of(e, k, 1 - d), ALU.subtract), f"u{k}")
                        for d in range(2):
                            a, b, e = B[d]
                            dve.wait_ge(pe_s[d].sem, pe_s[d].at(c, "z"))
                            dve.wait_ge(act_s[d].sem, act_s[d].at(c, "v_tok"))
                            for h in range(4):
                                last = nc.vector.scalar_tensor_tensor(out=R[d][:, h, :], in0=a[:, h, :],
                                                                      scalar=COL[d][:, NEG, h:h + 1], in1=VT[d][:, h, :],
                                                                      op0=ALU.mult, op1=ALU.add)
                            dve_s[d].done(last, "r")
                        for d in range(2):
                            a, b, e = B[d]
                            dve.wait_ge(pe_s[d].sem, pe_s[d].at(c, "v_new"))
                            dve_s[d].done(tt(VW[d][:], b, col(d, BETA), ALU.mult), "vw")
                        for d in range(2):
                            a, b, e = B[d]
                            dve.wait_ge(pe_s[d].sem, pe_s[d].at(c, "s_add"))
                            for h in range(4):
                                last = nc.vector.scalar_tensor_tensor(out=ST[d][:, h, :], in0=ST[d][:, h, :],
                                                                      scalar=COL[d][:, EL, h:h + 1], in1=a[:, h, :],
                                                                      op0=ALU.mult, op1=ALU.add)
                            dve_s[d].done(last, "s")

        def merge(l):
            with Phase("merge", ["in", "o_hi", "o_lo", "w_in0", "w_in1", "w_hi0", "w_hi1", "w_lo0", "w_lo1", "t_in0",
                                 "t_in1", "sum0", "sum1", "out0", "out1", "added0", "added1", "m_hi", "m_lo", "g_in",
                                 "g_half", "fwd_in", "bwd_in", "z_in", "summed", "squared", "total", "log", "root",
                                 "tanh", "z_gate", "normed", "gated"]) as (block, q):
                merged = sb("merged", [P, KC, S])
                branch = sb("branch", [P, 4, S])
                o_hi, o_lo = sb("branch_hi", [P, 4, S], F32R), sb("branch_lo", [P, 4, S], F32R)
                gate = [sb(f"gate{s}", [P, S]) for s in range(2)]
                over = [h_start]

                def sb_over(name, shape):
                    t = nc.alloc_sbuf_tensor_at(name, shape, F32, offset=over[0])
                    over[0] += 4 * shape[-1] * (shape[1] if len(shape) == 3 else 1)
                    return t

                OD, ZT = sb_over("delta_o", [P, 4, S]), sb_over("delta_zt", [P, 4, S])
                BWD, Z, SQ, R = (sb_over(f"delta_{n}", [P, S]) for n in ("bwd", "z", "sq", "r"))
                g_raw, g_half = small[:, 0:1], small[:, 1:2]
                w_bo = (w_bo_a, w_bo_b, w_bo_c)
                flat = lambda pair: pair[:].rearrange("p a b -> p (a b)")
                one = lambda ap: ap.rearrange("p o s -> p (o s)")
                unit = lambda t, h: one(t[:, ds(h, 1), :])

                @block.sync
                def _(sp):
                    sp.dma_start(g_raw, c_norm_g[ds(l, 1), :].rearrange("o p -> p o"), allow_slow_non_contiguous=True)\
                        .then_inc(q["g_in"], 16)

                    def loads(br, i):
                        w_l = w_bo[br].rearrange("l (k p) e -> l p k e", p=P)[ds(l, 1)].rearrange("o p k e -> (o p) k e")
                        for s in range(2):
                            j = 2 * i + (s - 8 * br)
                            sp.wait_ge(q[f"w_lo{s}"], START + i)
                            sp.dma_start(w_stage[s][:, 0:4, :], w_l[:, :, ds(j * P, P)]).then_inc(q[f"w_in{s}"], 16)
                            sp.wait_ge(q[f"out{s}"], START + i)
                            sp.dma_start(gate[s][:], proj[ds(2 * i + (N_PLAIN + s), 1)].rearrange("o p s -> (o p) s"))\
                                .then_inc(q[f"t_in{s}"], 16)

                    def load_branch(br):
                        sp.dma_start(branch[:], gated[4 * br:4 * br + 4].rearrange("u p s -> p u s")).then_inc(q["in"], 16)

                    def load_head(i):
                        sp.wait_ge(q["summed"], START + i)
                        sp.dma_start(BWD[:], o_dir[1, ds(i, 1)].rearrange("o p s -> (o p) s")).then_inc(q["bwd_in"], 16)
                        sp.wait_ge(q["z_gate"], START + i)
                        sp.dma_start(Z[:], proj[ds(i + U_CZ, 1)].rearrange("o p s -> (o p) s")).then_inc(q["z_in"], 16)

                    load_branch(0)
                    loads(0, 0)
                    sp.dma_start(OD[:], o_dir[0].rearrange("h p s -> p h s")).then_inc(q["fwd_in"], 16)
                    load_head(0)
                    with sp.Fori(1, 4) as i:
                        load_head(i)
                        loads(0, i)
                    sp.wait_ge(q["o_lo"], START + 4)
                    load_branch(1)
                    for br in (1, 2):
                        with sp.Fori(4 * br, 4 * br + 4) as i:
                            loads(br, i)
                    w_l = w_out.rearrange("l (k p) e -> l p k e", p=P)[ds(l, 1)].rearrange("o p k e -> (o p) k e")
                    for s in range(2):
                        sp.wait_ge(q[f"w_lo{s}"], START + 12)
                        sp.dma_start(w_stage[s][:], w_l[:, :, s * P:(s + 1) * P]).then_inc(q[f"w_in{s}"], 16)

                @block.gpsimd
                def _(pool):
                    def split(i, s, kc):
                        stage, hi, lo = (w[s][:, 0:kc, :] for w in (w_stage, w_hi, w_lo))
                        pool.wait_ge(q[f"w_in{s}"], START + 16 * i + 16)
                        pool.wait_ge(q[f"sum{s}"], START + i)
                        nc.gpsimd.tensor_tensor(hi, stage, bcast(ones, kc), ALU.mult).then_inc(q[f"w_hi{s}"], 1)
                        pool.wait_ge(q[f"w_hi{s}"], START + i + 1)
                        nc.gpsimd.tensor_tensor(lo, stage, hi.bitcast(F32), ALU.subtract).then_inc(q[f"w_lo{s}"], 1)

                    with pool.Fori(0, 12) as i:
                        for s in range(2):
                            split(i, s, 4)
                    for s in range(2):
                        split(12, s, KC)

                @block.tensor
                def _(pe):
                    for br in range(3):
                        with pe.Fori(4 * br, 4 * br + 4) as i:
                            for s in range(2):
                                pe.wait_ge(q[f"w_lo{s}"], START + i + 1)
                                pe.wait_ge(q[f"out{s}"], START + i)
                                product(pe, pairs[s], w_hi[s], w_lo[s], o_hi, o_lo, 4,
                                        ready=lambda k: pe.wait_ge(q["o_lo"], START + 4 * br + k + 1))\
                                    .then_inc(q[f"sum{s}"], 1)
                                if br == 0 and s == 0:
                                    pe.wait_ge(q["squared"], START + i + 1)
                                    for half in range(2):
                                        last = nc.tensor.matmul(pairs[2][:, half, :], ones,
                                                                SQ[:, half * HALF:(half + 1) * HALF], start=True, stop=True)
                                    last.then_inc(q["total"], 1)

                @block.scalar
                def _(act):
                    for br in range(3):
                        if br < 2:
                            act.wait_ge(q["in"], START + 16 * br + 16)
                        for s in range(2):
                            act.wait_ge(q[f"sum{s}"], START + 4 * br)
                        for k in range(4):
                            if br == 2:
                                act.wait_ge(q["gated"], START + k + 1)
                            nc.scalar.activation(o_hi[:, k, :], branch[:, k, :], ACT.Copy).then_inc(q["o_hi"], 1)
                        if br == 0:
                            for h in range(4):
                                act.wait_ge(q["z_in"], START + 16 * h + 16)
                                nc.scalar.activation(unit(ZT, h), Z[:], ACT.Tanh, scale=0.5).then_inc(q["tanh"], 1)
                                act.wait_ge(q["summed"], START + h + 1)
                                nc.scalar.activation(SQ[:], unit(OD, h), ACT.Square).then_inc(q["squared"], 1)
                                act.wait_ge(q["total"], START + h + 1)
                                act.wait_ge(q["normed"], START + h)
                                nc.scalar.activation(R[:], flat(pairs[2]), ACT.Ln, bias=eps, scale=1.0 / P)\
                                    .then_inc(q["log"], 1)
                                act.wait_ge(q["log"], START + h + 1)
                                nc.scalar.activation(R[:], R[:], ACT.Exp, scale=-0.5).then_inc(q["root"], 1)
                    for j in range(KC):
                        act.wait_ge(q[f"added{j % 2}"], START + 9 + j // 2)
                        nc.scalar.activation(h_hi[:, j, :], merged[:, j, :], ACT.Copy).then_inc(q["m_hi"], 1)

                @block.vector
                def _(dve):
                    dve.wait_ge(q["g_in"], START + 16)
                    nc.vector.tensor_scalar(g_half, g_raw, 0.5, None, ALU.mult).then_inc(q["g_half"], 1)
                    for br in range(3):
                        for k in range(4):
                            dve.wait_ge(q["o_hi"], START + 4 * br + k + 1)
                            nc.vector.tensor_tensor(o_lo[:, k, :], branch[:, k, :], o_hi[:, k, :].bitcast(F32), ALU.subtract)\
                                .then_inc(q["o_lo"], 1)
                        if br == 0:
                            dve.wait_ge(q["fwd_in"], START + 16)
                            dve.wait_ge(q["g_half"], START + 1)
                        if br == 1:
                            dve.wait_ge(q["o_lo"], START + 8)
                        with dve.Fori(4 * br, 4 * br + 4) as i:
                            h = i - 4 * br
                            if br == 0:
                                dve.wait_ge(q["bwd_in"], START + 16 * i + 16)
                                nc.vector.tensor_tensor(unit(OD, i), unit(OD, i), BWD[:], ALU.add).then_inc(q["summed"], 1)
                                dve.wait_ge(q["tanh"], START + i + 1)
                                nc.vector.scalar_tensor_tensor(out=unit(ZT, i), in0=unit(ZT, i), scalar=1.0, in1=Z[:],
                                                               op0=ALU.add, op1=ALU.mult).then_inc(q["z_gate"], 1)
                            for s in range(2):
                                j = 2 * i + (s - 8 * br)
                                dve.wait_ge(q[f"sum{s}"], START + i + 1)
                                dve.wait_ge(q[f"t_in{s}"], START + 16 * i + 16)
                                into = unit(merged, j)
                                if br == 0:
                                    nc.vector.scalar_tensor_tensor(out=into, in0=gate[s][:], scalar=1.0, in1=flat(pairs[s]),
                                                                   op0=ALU.add, op1=ALU.mult).then_inc(q[f"out{s}"], 1)
                                    dve.wait_ge(q[f"out{s}"], START + i + 1)
                                    dve.sem_inc(q[f"added{s}"], 1)
                                else:
                                    nc.vector.scalar_tensor_tensor(out=ev[s][:], in0=gate[s][:], scalar=1.0,
                                                                   in1=flat(pairs[s]), op0=ALU.add, op1=ALU.mult)\
                                        .then_inc(q[f"out{s}"], 1)
                                    dve.wait_ge(q[f"out{s}"], START + i + 1)
                                    dve.wait_ge(q[f"added{s}"], START + i)
                                    nc.vector.tensor_tensor(into, into, ev[s][:], ALU.add).then_inc(q[f"added{s}"], 1)
                                if br == 2:
                                    dve.wait_ge(q["m_hi"], START + j + 1)
                                    nc.vector.tensor_tensor(unit(h_lo, j), into, unit(h_hi, j).bitcast(F32), ALU.subtract)\
                                        .then_inc(q["m_lo"], 1)
                            if br == 0:
                                dve.wait_ge(q["root"], START + i + 1)
                                nc.vector.scalar_tensor_tensor(out=unit(OD, i), in0=unit(OD, i), scalar=g_half, in1=R[:],
                                                               op0=ALU.mult, op1=ALU.mult).then_inc(q["normed"], 1)
                            if br == 1:
                                dve.wait_ge(q["normed"], START + i - 3)
                                nc.vector.tensor_tensor(unit(branch, h), unit(OD, h), unit(ZT, h), ALU.mult)\
                                    .then_inc(q["gated"], 1)

        def add_output(l):
            with Phase("wout", ["w_in0", "w_in1", "w_hi0", "w_hi1", "w_lo0", "w_lo1", "x_in0", "x_in1", "sum0", "sum1",
                                "out0", "out1", "put0", "put1", "squared", "x_sq"]) as (block, q):
                top[0] = after_x
                sq = [sb(f"wout_sq{s}", [P, S]) for s in range(2)]
                flat = lambda pair: pair[:].rearrange("p a b -> p (a b)")
                unit = lambda t, j: t[:, ds(j, 1), :].rearrange("p o s -> p (o s)")
                w_l = w_out.rearrange("l (k p) e -> l p k e", p=P)[ds(l, 1)].rearrange("o p k e -> (o p) k e")

                @block.sync
                def _(sp):
                    def load_x_unit(i, s):
                        sp.wait_ge(q[f"out{s}"], START + i)
                        sp.dma_start(ev[s][:], resid[ds(2 * i + s, 1)].rearrange("o p s -> (o p) s"))\
                            .then_inc(q[f"x_in{s}"], 16)

                    for s in range(2):
                        load_x_unit(0, s)
                    with sp.Fori(1, KC // 2) as i:
                        for s in range(2):
                            sp.wait_ge(q[f"w_lo{s}"], START + i)
                            sp.dma_start(w_stage[s][:], w_l[:, :, ds((2 * i + s) * P, P)]).then_inc(q[f"w_in{s}"], 16)
                            load_x_unit(i, s)

                @block.gpsimd
                def _(pool):
                    with pool.Fori(1, KC // 2) as i:
                        for s in range(2):
                            pool.wait_ge(q[f"w_in{s}"], START + 16 * i)
                            pool.wait_ge(q[f"sum{s}"], START + i)
                            nc.gpsimd.tensor_tensor(w_hi[s][:], w_stage[s][:], bcast(ones, KC), ALU.mult)\
                                .then_inc(q[f"w_hi{s}"], 1)
                            pool.wait_ge(q[f"w_hi{s}"], START + i)
                            nc.gpsimd.tensor_tensor(w_lo[s][:], w_stage[s][:], w_hi[s][:].bitcast(F32), ALU.subtract)\
                                .then_inc(q[f"w_lo{s}"], 1)

                @block.tensor
                def _(pe):
                    with pe.Fori(0, KC // 2) as i:
                        for s in range(2):
                            pe.wait_ge(q[f"w_lo{s}"], START + i + 1)
                            pe.wait_ge(q[f"out{s}"], START + i)
                            product(pe, pairs[s], w_hi[s], w_lo[s], h_hi, h_lo, KC).then_inc(q[f"sum{s}"], 1)

                @block.vector
                def _(dve):
                    for s in range(2):
                        dve.sem_inc(q[f"w_lo{s}"], 1)
                    nc.vector.memset(x_sq[:], 0.0).then_inc(q["x_sq"], 1)
                    with dve.Fori(0, KC // 2) as i:
                        for s in range(2):
                            dve.wait_ge(q[f"sum{s}"], START + i + 1)
                            dve.wait_ge(q[f"x_in{s}"], START + 16 * i + 16)
                            nc.vector.scalar_tensor_tensor(out=unit(xT, 2 * i + s), in0=flat(pairs[s]), scalar=0.5,
                                                           in1=ev[s][:], op0=ALU.mult, op1=ALU.add).then_inc(q[f"out{s}"], 1)
                            dve.wait_ge(q["squared"], START + 2 * i + (s + 1))
                            dve.wait_ge(q["x_sq"], START + 2 * i + (s + 1))
                            nc.vector.tensor_tensor(x_sq[:], x_sq[:], sq[s][:], ALU.add).then_inc(q["x_sq"], 1)

                @block.scalar
                def _(act):
                    for j in range(KC):
                        i, s = j // 2, j % 2
                        act.wait_ge(q[f"out{s}"], START + i + 1)
                        act.dma_start(resid[j], xT[:, j, :]).then_inc(q[f"put{s}"], 16)
                        if j >= 2:
                            act.wait_ge(q["x_sq"], START + j)
                        nc.scalar.activation(sq[s][:], xT[:, j, :], ACT.Square).then_inc(q["squared"], 1)
                    for s in range(2):
                        act.wait_ge(q[f"put{s}"], START + 16 * (KC // 2))

        load_x()
        layers = nc.Fori(0, DEPTH)
        with layers as l:
            if "G" in phases:
                project(l)
            if "A" in phases:
                attend_window(l)
            if "B" in phases:
                attend_full(l)
            if "C" in phases:
                convolve(l)
            if "c" in phases:
                delta_rule(l)
            if "M" in phases:
                merge(l)
            if "O" in phases:
                add_output(l)
        if "O" in phases:
            final_norm()


_INS = ["x", "norm_g", "w_in", "a_sink", "b_lambda", "b_subln_g", "c_conv_w", "c_a_log", "c_dt_bias", "c_norm_g",
        "w_bo_a", "w_bo_b", "w_bo_c", "w_out", "final_g"]


def constants():
    import numpy as np
    inv = (1.0 / (np.float32(10000.0) ** (np.arange(0, HD, 2, dtype=np.float32) / np.float32(HD)))).astype(np.float32)
    ang = (np.arange(S, dtype=np.float32)[None, :] * inv[:, None]).astype(np.float32)
    cos, sin = np.cos(ang), np.sin(ang)
    cos_t = np.tile(cos, (4, 1)).astype(np.float32)
    sin_t = np.concatenate([-sin, sin, -sin, sin], 0).astype(np.float32)
    r = np.arange(P)
    m = np.zeros((P, 2 * N_LEVELS + 4, P), np.float32)
    for k in range(N_LEVELS):
        b = 1 << k
        low = (r[:, None] // (2 * b) == r[None, :] // (2 * b)) & (r[:, None] // b % 2 == 1) & (r[None, :] // b % 2 == 0)
        m[:, k] = low
        m[:, N_LEVELS + k] = low.T
    m[:, 2 * N_LEVELS] = r[:, None] <= r[None, :]
    m[:, 2 * N_LEVELS + 1] = r[:, None] >= r[None, :]
    m[:, 2 * N_LEVELS + 2] = np.eye(P)
    m[:, 2 * N_LEVELS + 3] = 1.0
    kpos = np.arange(3 * P)[None, :] - P
    band = np.where(np.abs(kpos - r[:, None]) <= P, 0.0, -1e30).astype(np.float32)
    lam = np.zeros((P, DEPTH, 2), np.float32)
    for l in range(DEPTH):
        lam[:, l, 0] = 0.8 - 0.6 * math.exp(-0.3 * l)
        lam[:, l, 1] = 0.5 * (1.0 - lam[0, l, 0])
    return {"cos_t": cos_t, "sin_t": sin_t, "masks_t": m, "band_t": band, "lam_t": lam}


def kernel(**inputs):
    import numpy as _np
    import concourse.bacc as _bacc
    from concourse.bass_utils import run_bass_kernel_spmd as _run

    nc = _bacc.Bacc("TRN2", target_bir_lowering=False, num_devices=1)
    arrays, args = {}, []
    for name, a in {**{n: inputs[n] for n in _INS}, **constants()}.items():
        a = _np.ascontiguousarray(a)
        arrays[f"in_{name}"] = a
        args.append(nc.dram_tensor(f"in_{name}", a.shape, mybir.dt.from_np(a.dtype), kind="ExternalInput").ap())
    args.append(nc.dram_tensor("out_x", (1, S, D), F32, kind="ExternalOutput").ap())
    build_program(nc, *args)
    r = _run(nc, [arrays], core_ids=[0])
    return r.results[0]["out_x"]
```
